# Optimizing a Trainium2 kernel written in Bass

```python
import jax, jax.numpy as jnp
from jax import lax
import numpy as np

D_MODEL = 1024
BATCH = 1
SEQ = 512
DEPTH = 2

CTX_LEN = 256
GRID_W = 64
N_MIXERS = 2
N_CONV_LAYERS = (DEPTH + 1) // 2
N_RET_LAYERS = DEPTH // 2
CONV_WIDTH = 31
RET_HEADS = 4
RET_DK = D_MODEL // RET_HEADS
RET_DV = D_MODEL // RET_HEADS
RET_QK = RET_HEADS * RET_DK
RET_V = RET_HEADS * RET_DV
RET_IN = 2 * RET_QK + 3 * RET_V
RET_CHUNK = 128
FFN_DIM = ((8 * D_MODEL // 3 + 127) // 128) * 128
FFN_CONV_WIDTH = 3
ROPE_BASE = 10000.0
NORM_EPS = 1e-6
GN_EPS = 1e-5

kernel_name = "hybrid_conformer_retention_dit"

def rmsnorm(x, g):
    x32 = x.astype(jnp.float32)
    y = x32 * lax.rsqrt(jnp.mean(x32 * x32, axis=-1, keepdims=True) + NORM_EPS)
    return (y * g.astype(jnp.float32)).astype(x.dtype)

def layernorm(x, g, b):
    x32 = x.astype(jnp.float32)
    mu = jnp.mean(x32, axis=-1, keepdims=True)
    var = jnp.mean(jnp.square(x32 - mu), axis=-1, keepdims=True)
    y = (x32 - mu) * lax.rsqrt(var + NORM_EPS) * g.astype(jnp.float32) + b.astype(jnp.float32)
    return y.astype(x.dtype)

def modulate(h, shift, scale):
    return h * (1 + scale) + shift

def dwconv(x, w, b):
    k = w.shape[0]
    y = lax.conv_general_dilated(x, w[:, None, :], window_strides=(1,), padding=[(k // 2, k // 2)],
                                 dimension_numbers=("NWC", "WIO", "NWC"),
                                 feature_group_count=x.shape[-1])
    return y + b

def conv_module(h, pw1_w, pw1_b, dw_w, dw_b, ln_g, ln_b, pw2_w, pw2_b):
    z = h @ pw1_w + pw1_b
    a, g = jnp.split(z, 2, axis=-1)
    u = a * jax.nn.sigmoid(g)
    u = dwconv(u, dw_w, dw_b)
    u = jax.nn.silu(layernorm(u, ln_g, ln_b))
    return u @ pw2_w + pw2_b

def conv_ffn(h, w_in, dw_w, dw_b, w_out):
    z = h @ w_in
    u, g = z[..., :FFN_DIM], z[..., FFN_DIM:]
    g = dwconv(g, dw_w, dw_b)
    return (u * jax.nn.silu(g)) @ w_out

def rope_1d(t, pos):
    half = t.shape[-1] // 2
    freqs = ROPE_BASE ** (-jnp.arange(half, dtype=jnp.float32) / half)
    ang = pos[:, None] * freqs[None, :]
    cos = jnp.cos(ang)[None, :, None, :]
    sin = jnp.sin(ang)[None, :, None, :]
    t1, t2 = t[..., :half], t[..., half:]
    return jnp.concatenate([t1 * cos - t2 * sin, t1 * sin + t2 * cos], axis=-1)

def rope_2d(t, row_pos, col_pos):
    half = t.shape[-1] // 2
    t32 = t.astype(jnp.float32)
    out = jnp.concatenate([rope_1d(t32[..., :half], row_pos), rope_1d(t32[..., half:], col_pos)], axis=-1)
    return out.astype(t.dtype)

def chunk_retention(q, k, v, log_gamma, s0):
    b, l, h, _ = q.shape
    n_chunks = l // RET_CHUNK

    def to_chunks(t):
        return t.astype(jnp.float32).reshape(b, n_chunks, RET_CHUNK, h, -1).transpose(1, 0, 3, 2, 4)

    idx = jnp.arange(RET_CHUNK, dtype=jnp.float32)
    diff = idx[:, None] - idx[None, :]
    dmask = jnp.where(diff[None] >= 0, jnp.exp(jnp.maximum(diff, 0.0)[None] * log_gamma[:, None, None]), 0.0)
    xi = jnp.exp((idx + 1.0)[None, :] * log_gamma[:, None])[:, :, None]
    zeta = jnp.exp((RET_CHUNK - 1.0 - idx)[None, :] * log_gamma[:, None])[:, :, None]
    g_chunk = jnp.exp(RET_CHUNK * log_gamma)[:, None, None]

    def step(s, qkv):
        qc, kc, vc = qkv
        scores = jnp.einsum("bhid,bhjd->bhij", qc, kc) * dmask
        o = jnp.einsum("bhij,bhjv->bhiv", scores, vc) + jnp.einsum("bhid,bhdv->bhiv", qc, s) * xi
        s = g_chunk * s + jnp.einsum("bhjd,bhjv->bhdv", kc * zeta, vc)
        return s, o

    s_final, o = lax.scan(step, s0, (to_chunks(q), to_chunks(k), to_chunks(v)))
    o = o.transpose(1, 0, 3, 2, 4).reshape(b, l, h, -1)
    return o, s_final

def retention_project(h, w_in):
    b, l, _ = h.shape
    z = h @ w_in
    q = z[..., :RET_QK].reshape(b, l, RET_HEADS, RET_DK)
    k = z[..., RET_QK:2 * RET_QK].reshape(b, l, RET_HEADS, RET_DK) * (RET_DK ** -0.5)
    v = z[..., 2 * RET_QK:2 * RET_QK + RET_V].reshape(b, l, RET_HEADS, RET_DV)
    g_f = z[..., 2 * RET_QK + RET_V:2 * RET_QK + 2 * RET_V]
    g_b = z[..., 2 * RET_QK + 2 * RET_V:]
    return q, k, v, g_f, g_b

def head_groupnorm(o, g):
    b, l, _, _ = o.shape
    mu = jnp.mean(o, axis=-1, keepdims=True)
    var = jnp.mean(jnp.square(o - mu), axis=-1, keepdims=True)
    y = (o - mu) * lax.rsqrt(var + GN_EPS)
    return y.reshape(b, l, RET_V) * g.astype(jnp.float32)

def retention_output(o_f, o_b, g_f, g_b, gn_f, gn_b, w_out):
    y = (jax.nn.silu(g_f.astype(jnp.float32)) * head_groupnorm(o_f, gn_f)
         + jax.nn.silu(g_b.astype(jnp.float32)) * head_groupnorm(o_b, gn_b))
    return y.astype(w_out.dtype) @ w_out

def retention_mixer(h, hc, w_in, w_out, a_f, a_b, gn_f, gn_b, row_pos, col_pos, with_ctx_out):
    lg_f = -jnp.exp(a_f.astype(jnp.float32))
    lg_b = -jnp.exp(a_b.astype(jnp.float32))
    qc, kc, vc, gcf, gcb = retention_project(hc, w_in)
    s0 = jnp.zeros((hc.shape[0], RET_HEADS, RET_DK, RET_DV), jnp.float32)
    oc_f, sc_f = chunk_retention(qc, kc, vc, lg_f, s0)
    oc_b, sc_b = chunk_retention(qc[:, ::-1], kc[:, ::-1], vc[:, ::-1], lg_b, s0)
    q, k, v, gf, gb = retention_project(h, w_in)
    q = rope_2d(q, row_pos, col_pos)
    k = rope_2d(k, row_pos, col_pos)
    o_f, _ = chunk_retention(q, k, v, lg_f, sc_f)
    o_b, _ = chunk_retention(q[:, ::-1], k[:, ::-1], v[:, ::-1], lg_b, sc_b)
    y = retention_output(o_f, o_b[:, ::-1], gf, gb, gn_f, gn_b, w_out)
    yc = retention_output(oc_f, oc_b[:, ::-1], gcf, gcb, gn_f, gn_b, w_out) if with_ctx_out else None
    return y, yc

def setup_inputs(seed: int = 0) -> dict:
    key = jax.random.key(seed)
    ks = jax.random.split(key, 32)
    f32 = jnp.float32
    d, f = D_MODEL, FFN_DIM
    na, nb = N_CONV_LAYERS, N_RET_LAYERS

    def nrm(k, shape, scale):
        return jax.random.normal(k, shape, f32) * scale

    base_decay = jnp.asarray(np.log(-np.log(1.0 - 2.0 ** (-5.0 - np.arange(RET_HEADS)))), dtype=f32)
    return {
        "x": nrm(ks[0], (BATCH, SEQ, d), 1.0),
        "c": nrm(ks[1], (BATCH, d), 1.0),
        "ctx": nrm(ks[2], (BATCH, CTX_LEN, d), 1.0),
        "c_ctx": nrm(ks[3], (d,), 1.0),
        "ada_w": nrm(ks[4], (DEPTH, d, 6 * d), 0.5 * d ** -0.5),
        "ada_b": nrm(ks[5], (DEPTH, 6 * d), 0.01),
        "norm1_g": 1.0 + nrm(ks[6], (DEPTH, d), 0.02),
        "norm2_g": 1.0 + nrm(ks[7], (DEPTH, d), 0.02),
        "conv_pw1_w": nrm(ks[8], (na, d, 2 * d), d ** -0.5),
        "conv_pw1_b": nrm(ks[9], (na, 2 * d), 0.01),
        "conv_dw_w": nrm(ks[10], (na, CONV_WIDTH, d), CONV_WIDTH ** -0.5),
        "conv_dw_b": nrm(ks[11], (na, d), 0.01),
        "conv_ln_g": 1.0 + nrm(ks[12], (na, d), 0.02),
        "conv_ln_b": nrm(ks[13], (na, d), 0.01),
        "conv_pw2_w": nrm(ks[14], (na, d, d), d ** -0.5),
        "conv_pw2_b": nrm(ks[15], (na, d), 0.01),
        "ret_w_in": nrm(ks[16], (nb, d, RET_IN), d ** -0.5),
        "ret_w_out": nrm(ks[17], (nb, RET_V, d), RET_V ** -0.5),
        "ret_decay_f": base_decay[None, :] + nrm(ks[18], (nb, RET_HEADS), 0.01),
        "ret_decay_b": base_decay[None, :] + nrm(ks[19], (nb, RET_HEADS), 0.01),
        "ret_gn_f": 1.0 + nrm(ks[20], (nb, RET_V), 0.02),
        "ret_gn_b": 1.0 + nrm(ks[21], (nb, RET_V), 0.02),
        "ffn_w_in": nrm(ks[22], (DEPTH, d, 2 * f), d ** -0.5),
        "ffn_dw_w": nrm(ks[23], (DEPTH, FFN_CONV_WIDTH, f), FFN_CONV_WIDTH ** -0.5),
        "ffn_dw_b": nrm(ks[24], (DEPTH, f), 0.01),
        "ffn_w_out": nrm(ks[25], (DEPTH, f, d), f ** -0.5),
        "final_g": 1.0 + nrm(ks[26], (d,), 0.02),
    }

def reference(x, c, ctx, c_ctx, ada_w, ada_b, norm1_g, norm2_g,
              conv_pw1_w, conv_pw1_b, conv_dw_w, conv_dw_b, conv_ln_g, conv_ln_b, conv_pw2_w, conv_pw2_b,
              ret_w_in, ret_w_out, ret_decay_f, ret_decay_b, ret_gn_f, ret_gn_b,
              ffn_w_in, ffn_dw_w, ffn_dw_b, ffn_w_out, final_g):
    seq_len = x.shape[1]
    rows = seq_len // GRID_W
    row_pos = jnp.repeat(jnp.arange(rows, dtype=jnp.float32), GRID_W)
    col_pos = jnp.tile(jnp.arange(GRID_W, dtype=jnp.float32), rows)
    silu_c = jax.nn.silu(c)
    silu_cc = jax.nn.silu(c_ctx)
    hctx = ctx
    for i in range(DEPTH):
        last = i == DEPTH - 1
        j = i // N_MIXERS
        mod_x = (silu_c @ ada_w[i] + ada_b[i])[:, None, :]
        mod_c = (silu_cc @ ada_w[i] + ada_b[i])[None, None, :]
        sx1, cx1, gx1, sx2, cx2, gx2 = jnp.split(mod_x, 6, axis=-1)
        sc1, cc1, gc1, sc2, cc2, gc2 = jnp.split(mod_c, 6, axis=-1)
        hx = modulate(rmsnorm(x, norm1_g[i]), sx1, cx1)
        hc = modulate(rmsnorm(hctx, norm1_g[i]), sc1, cc1)
        if i % N_MIXERS == 0:
            conv_args = (conv_pw1_w[j], conv_pw1_b[j], conv_dw_w[j], conv_dw_b[j],
                         conv_ln_g[j], conv_ln_b[j], conv_pw2_w[j], conv_pw2_b[j])
            yx = conv_module(hx, *conv_args)
            yc = None if last else conv_module(hc, *conv_args)
        else:
            yx, yc = retention_mixer(hx, hc, ret_w_in[j], ret_w_out[j], ret_decay_f[j], ret_decay_b[j],
                                     ret_gn_f[j], ret_gn_b[j], row_pos, col_pos, not last)
        x = x + gx1 * yx
        hx = modulate(rmsnorm(x, norm2_g[i]), sx2, cx2)
        x = x + gx2 * conv_ffn(hx, ffn_w_in[i], ffn_dw_w[i], ffn_dw_b[i], ffn_w_out[i])
        if not last:
            hctx = hctx + gc1 * yc
            hc = modulate(rmsnorm(hctx, norm2_g[i]), sc2, cc2)
            hctx = hctx + gc2 * conv_ffn(hc, ffn_w_in[i], ffn_dw_w[i], ffn_dw_b[i], ffn_w_out[i])
    return rmsnorm(x, final_g)


_drawn_inputs = setup_inputs


def setup_inputs(seed=0):
    import zlib

    import numpy as np

    out = dict(_drawn_inputs(seed))
    spreads = {}
    factors = {'ada_b': 2.978,
     'norm1_g': 5.068,
     'norm2_g': 6.264,
     'conv_pw1_b': 8.0,
     'conv_dw_b': 8.0,
     'conv_ln_g': 8.0,
     'conv_ln_b': 8.0,
     'conv_pw2_b': 8.0,
     'ret_gn_f': 8.0,
     'ret_gn_b': 8.0,
     'ffn_dw_b': 8.0,
     'final_g': 2.792}
    for name, (base, spread) in spreads.items():
        noise = np.random.default_rng([zlib.crc32(name.encode()), seed]).standard_normal(out[name].shape)
        drawn = base * np.exp(spread * noise) if base else spread * noise
        out[name] = __import__('jax').numpy.asarray(drawn.astype(out[name].dtype))
    for name, factor in factors.items():
        out[name] = (out[name] * factor).astype(out[name].dtype)
    return out
```

```python
from contextlib import ExitStack

import concourse.bass as bass
from concourse import mybir

F32 = mybir.dt.float32
F32R = mybir.dt.float32r
ALU = mybir.AluOpType
ACT = mybir.ActivationFunctionType
ds = bass.ds

P = 128
D = 1024
KT = D // P
LAT, CTX = 512, 256
TOK = LAT + CTX
LT, CT = LAT // P, CTX // P
DEPTH = 2
F = ((8 * D // 3 + 127) // 128) * 128
FT = F // P
TAPS = 31
PAD = TAPS // 2
CTX_PAD = PAD + LAT + PAD
PADW = CTX_PAD + CTX + PAD
CTX_OUT = LAT + PAD
OUTW = CTX_OUT + CTX
HEADS, DH = 4, 256
GRID_W = 64
ROWS = LAT // GRID_W
NORM_EPS, GN_EPS = 1e-6, 1e-5
CHUNKS = [8, 8, FT - 16]
RING = 4

PW1, PW2 = 0, KT
FFN0 = PW2 + KT // 2
FFN_BLOCKS = FT + 4 * len(CHUNKS)
RET = FFN0 + FFN_BLOCKS
RET_OUT = RET + 5 * HEADS
FFN1 = RET_OUT + KT // 2
BLOCKS = FFN1 + FFN_BLOCKS
UNITS = 2 * BLOCKS

S_XT = 0
S_PW1 = S_XT + KT
S_LN = S_PW1 + KT
S_PW2 = S_LN + 2
S_FFN0 = S_PW2 + KT
S_FFN = FT + KT * len(CHUNKS)
S_RET = S_FFN0 + S_FFN
HEAD_USES = 8
S_RET_OUT = S_RET + HEAD_USES * HEADS
S_FFN1 = S_RET_OUT + KT
S_OUT = S_FFN1 + S_FFN

ADA_B = 0
NORM1, NORM2 = 96, 112
PW1_B, DW_B, LN_G, LN_B, PW2_B, FFN_DW_B, FINAL_G, C_COL = 128, 144, 152, 160, 168, 176, 220, 228
DW_W = 256
FFN_DW_W = 512
ADA_RING = 4


def backbone(nc, x, c, ctx_tok, c_ctx, ada_w, ada_b, norm1_g, norm2_g, pw1_w, pw1_b, dw_w, dw_b, ln_g, ln_b,
             pw2_w, pw2_b, ret_w_in, ret_w_out, decay_f, decay_b, gn_f, gn_b, ffn_w_in, ffn_dw_w, ffn_dw_b,
             ffn_w_out, final_g, eye, ages, tri_low, tri_up, rope_row, rope_col, token_cols, out):
    with ExitStack() as stack:
        def sb(name, shape, dt=F32, where=stack):
            return where.enter_context(nc.sbuf_tensor(name, shape, dt))

        def sem(name):
            return stack.enter_context(nc.semaphore(name))

        X = sb("X", [P, KT, TOK])
        H_hi = sb("H_hi", [P, KT, TOK], F32R)
        H_lo = sb("H_lo", [P, KT, TOK], F32R)
        w_raw = sb("w_raw", [P, RING, KT * P])
        w_hi = sb("w_hi", [P, RING, KT * P], F32R)
        w_lo = sb("w_lo", [P, RING, KT * P], F32R)
        rstd = sb("rstd", [P, TOK])
        sq = sb("sq", [P, 2, TOK])
        tmp = sb("tmp", [P, 2, TOK])
        par = sb("par", [P, 768])
        ident = sb("ident", [P, P])
        mean_of = sb("mean_of", [P, P])
        eps = sb("eps", [P, 2])
        silu_c = sb("silu_c", [P, KT, 2])
        mod = sb("mod", [P, DEPTH, 48, 2])
        gain = sb("gain", [P, DEPTH, 2, KT, 2])
        pw2_gb = sb("pw2_gb", [P, KT, 2])
        decay_log = sb("decay_log", [P, 2 * HEADS])
        lgam = sb("lgam", [P, 2 * HEADS])
        ngam = sb("ngam", [P, 2 * HEADS])
        lgam512 = sb("lgam512", [P, 2 * HEADS])
        rrow = sb("rrow", [P, 2, ROWS])
        rcol = sb("rcol", [P, 2, GRID_W])
        tcol = sb("tcol", [P, 6])
        zeta = sb("zeta", [P, HEADS, 2, CT])
        iota = sb("iota", [P, LAT])
        tlow = sb("tlow", [P, P])
        tup = sb("tup", [P, P])
        with ExitStack() as ph:
            conv = sb("conv", [P, KT, OUTW + 1], F32, ph)
            ada = sb("ada", [P, ADA_RING, KT, 2 * P], F32, ph)
            upad = sb("upad", [P, 2, PADW], F32, ph)
        with ExitStack() as ph:
            mid_hi = sb("mid_hi", [P, 8, TOK], F32R, ph)
            mid_lo = sb("mid_lo", [P, 8, TOK], F32R, ph)
            m32 = sb("m32", [P, 2, TOK], F32, ph)
        with ExitStack() as ph:
            y_hi = sb("y_hi", [P, KT, LAT], F32R, ph)
            y_lo = sb("y_lo", [P, KT, LAT], F32R, ph)
            qT = sb("qT", [P, 2, LAT], F32, ph)
            kT = sb("kT", [P, 2, LAT], F32, ph)
            V = sb("V", [P, LT, DH], F32, ph)
            scores = sb("scores", [P, 2, 10 * P], F32, ph)
            state = sb("state", [P, 2, 2, DH], F32, ph)
            decay = sb("decay", [P, 2, LAT], F32, ph)
            gn_st = sb("gn_st", [P, LT, 6], F32, ph)
            gn_mv = sb("gn_mv", [P, LT, 2], F32, ph)
        y_tok = qT[:].rearrange("p f t -> p (f t)").rearrange("p (t v) -> p t v", t=LT)
        q_dec = tmp[:, 0:2, :].rearrange("p a b -> p (a b)")[:, 0:2 * LAT].rearrange("p (a b) -> p a b", a=2)
        rot = tmp[:, 0:2, :].rearrange("p a b -> p (a b)")[:, 2 * LAT:3 * LAT]
        cosd = rstd[:, 0:LAT]
        gate = sq[:, 0:2, :].rearrange("p a b -> p (a b)")[:, 0:LT * DH].rearrange("p (a b) -> p a b", a=LT)
        gn_row = sq[:, 0:2, :].rearrange("p a b -> p (a b)")[:, LT * DH:LT * DH + 2 * DH].rearrange(
            "p (a b) -> p a b", a=2)
        kctx = scores[:, 0, 0:4 * DH].rearrange("p (d t v) -> p d t v", d=2, t=CT)
        vctx = scores[:, 1, 0:2 * DH].rearrange("p (t v) -> p t v", t=CT)
        xin = conv[:, :, :].rearrange("p a b -> p (a b)")[:, 0:6 * D].rearrange("p (t d) -> p t d", t=6)
        sil = ada[:].rearrange("p r k n -> p (r k n)")[:, 0:2 * TOK].rearrange("p (a b) -> p a b", a=2)
        prow = tmp[:, :, :].rearrange("p a b -> p (a b)")[:, 0:768].rearrange("p (a b) -> p a b", b=P)
        otok = conv[:, :, :].rearrange("p a b -> p (a b)")[:, 0:LT * D].rearrange("p (t d) -> p t d", t=LT)

        ps = stack.enter_context(nc.psum_tensor("ps", [P, 8, 512], F32))

        raw_ready = [sem(f"raw_ready{r}") for r in range(RING)]
        hi_ready = sem("hi_ready")
        lo_ready = sem("lo_ready")
        unit_done = sem("unit_done")
        slot_read = [sem("slot_read0"), sem("slot_read1")]
        par_rows = sem("par_rows")
        consts_in = sem("consts_in")
        eye_in = sem("eye_in")
        tokens_in = sem("tokens_in")
        filled = sem("filled")
        par_T = sem("par_T")
        par_ready = sem("par_ready")
        silu_c_ready = sem("silu_c_ready")
        ada_in = [sem(f"ada_in{r}") for r in range(ADA_RING)]
        ada_done = sem("ada_done")
        mod_ready = sem("mod_ready")
        xT_done = sem("xT_done")
        sq_ready = sem("sq_ready")
        sq_summed = sem("sq_summed")
        std_ready = sem("std_ready")
        rstd_ready = sem("rstd_ready")
        scaled = sem("scaled")
        h_hi_ready = sem("h_hi_ready")
        h_lo_ready = sem("h_lo_ready")
        sig_ready = sem("sig_ready")
        tap_done = sem("tap_done")
        mu_summed = sem("mu_summed")
        centered = sem("centered")
        lsq_ready = sem("lsq_ready")
        lsq_summed = sem("lsq_summed")
        ln_scaled = sem("ln_scaled")
        ln_silu = sem("ln_silu")
        x_updated = sem("x_updated")
        g_first = sem("g_first")
        g_taps = sem("g_taps")
        g_silu = sem("g_silu")
        mid_hi_ready = sem("mid_hi_ready")
        mid_lo_ready = sem("mid_lo_ready")
        lg_step = sem("lg_step")
        zeta_ready = sem("zeta_ready")
        gn_in = sem("gn_in")
        rot_step = sem("rot_step")
        age_ready = sem("age_ready")
        decay_exp = sem("decay_exp")
        decay_ready = sem("decay_ready")
        score_done = sem("score_done")
        score_read = sem("score_read")
        qdec_ready = sem("qdec_ready")
        gn_stats = sem("gn_stats")
        gn_var = sem("gn_var")
        gn_std = sem("gn_std")
        gn_rstd = sem("gn_rstd")
        gate_ready = sem("gate_ready")
        y_step = sem("y_step")
        yT_done = sem("yT_done")
        y_hi_ready = sem("y_hi_ready")
        y_lo_ready = sem("y_lo_ready")
        fin_ready = sem("fin_ready")
        out_ready = sem("out_ready")
        stored = sem("stored")

        LATS, CTXS = slice(0, LAT), slice(LAT, TOK)

        def groups(both):
            return [(0, LATS), (1, CTXS)] if both else [(0, LATS)]

        def flat(ap):
            return ap.rearrange("p a b -> p (a b)")

        def taps_at(layer):
            return 4 * FT * layer

        block = stack.enter_context(nc.Block())

        @block.sync
        def _(sp):
            for n, (lo, rows, src) in enumerate([
                    (0, 96, ada_b.rearrange("l (t p) -> (l t) p", p=P)),
                    (NORM1, 16, norm1_g.rearrange("l (t p) -> (l t) p", p=P)),
                    (NORM2, 16, norm2_g.rearrange("l (t p) -> (l t) p", p=P)),
                    (PW1_B, 16, pw1_b.rearrange("l (t p) -> (l t) p", p=P)),
                    (DW_B, 8, dw_b.rearrange("l (t p) -> (l t) p", p=P)),
                    (LN_G, 8, ln_g.rearrange("l (t p) -> (l t) p", p=P)),
                    (LN_B, 8, ln_b.rearrange("l (t p) -> (l t) p", p=P)),
                    (PW2_B, 8, pw2_b.rearrange("l (t p) -> (l t) p", p=P)),
                    (FFN_DW_B, 44, ffn_dw_b.rearrange("l (t p) -> (l t) p", p=P)),
                    (FINAL_G, 8, final_g.rearrange("(t p) -> t p", p=P)),
                    (C_COL, 8, c.rearrange("b (t p) -> (b t) p", p=P)),
                    (C_COL + 8, 8, c_ctx.rearrange("(t p) -> t p", p=P)),
                    (DW_W, 128, dw_w[0].rearrange("k (t p) -> (k t) p", p=P)[0:128]),
                    (DW_W + 128, 120, dw_w[0].rearrange("k (t p) -> (k t) p", p=P)[128:248]),
                    (FFN_DW_W, 66, ffn_dw_w[0].rearrange("k (t p) -> (k t) p", p=P)),
                    (FFN_DW_W + 128, 66, ffn_dw_w[1].rearrange("k (t p) -> (k t) p", p=P))]):
                r0 = lo % P
                sp.dma_start(prow[r0:r0 + rows, lo // P, :], src).then_inc(par_rows, 16)
                if n == 0:
                    sp.dma_start(ident[:], eye).then_inc(eye_in, 16)
            for t in range(LT):
                sp.dma_start(xin[:, t, :], x[0, t * P:(t + 1) * P, :]).then_inc(tokens_in, 16)
            for t in range(CT):
                sp.dma_start(xin[:, LT + t, :], ctx_tok[0, t * P:(t + 1) * P, :]).then_inc(tokens_in, 16)
            for dst, src in ((iota[:], ages), (tlow[:], tri_low), (tup[:], tri_up),
                             (rrow[:], rope_row), (rcol[:], rope_col), (tcol[:], token_cols),
                             (decay_log[:, 0:HEADS], decay_f.to_broadcast([P, HEADS])),
                             (decay_log[:, HEADS:], decay_b.to_broadcast([P, HEADS]))):
                sp.dma_start(dst, src).then_inc(consts_in, 16)

            def load(unit, r, src):
                if not (isinstance(unit, int) and unit < RING):
                    sp.wait_ge(lo_ready, unit - (RING - 1))
                k = src.shape[0] // P
                sp.dma_start(w_raw[:, r, 0:k * P].rearrange("p (k n) -> p k n", n=P),
                             src.rearrange("(k p) n -> p k n", p=P)).then_inc(raw_ready[r], 16)

            def load_pairs(first, w, half, n):
                def body(i):
                    for q in range(2):
                        for h in range(2):
                            load(2 * first + 4 * i + 2 * q + h, 2 * q + h,
                                 w[:, ds(i * (2 * P) + (q * P + h * half), P)])
                if first == PW1:
                    body(0)
                with sp.Fori(1 if first == PW1 else 0, n // 2) as i:
                    body(i)

            def load_cols(first, w, n):
                with sp.Fori(0, n // 2) as i:
                    for u in range(4):
                        load(2 * first + 4 * i + u, u, w[:, ds(i * (4 * P) + u * P, P)])

            def load_ffn(first, layer):
                w_in, w_out = ffn_w_in[layer], ffn_w_out[layer]
                f = 0
                for n in CHUNKS:
                    load_pairs(first, w_in[:, f * P:], F, n)
                    load_cols(first + n, w_out[f * P:(f + n) * P, :], 4)
                    first += n + 4
                    f += n

            load_pairs(PW1, pw1_w[0], D, KT)
            load_cols(PW2, pw2_w[0], KT // 2)
            load_ffn(FFN0, 0)
            for h in range(HEADS):
                for part in range(5):
                    for u in range(2):
                        unit = 2 * (RET + 5 * h + part) + u
                        load(unit, unit % RING, ret_w_in[0][:, part * D + h * DH + u * P:part * D + h * DH + (u + 1) * P])
            load_cols(RET_OUT, ret_w_out[0], KT // 2)
            load_ffn(FFN1, 1)
            for t in range(LT):
                sp.wait_ge(out_ready, 1)
                sp.dma_start(out[0, t * P:(t + 1) * P, :], otok[:, t, :]).then_inc(stored, 16)
            sp.wait_ge(stored, 16 * LT)

        @block.gpsimd
        def _(pool):
            nc.gpsimd.memset(mean_of[:], 1.0 / D).then_inc(filled, 1)
            nc.gpsimd.memset(eps[:, 0:1], NORM_EPS).then_inc(filled, 1)
            nc.gpsimd.memset(eps[:, 1:2], GN_EPS).then_inc(filled, 1)
            nc.gpsimd.memset(upad[:], 0.0).then_inc(filled, 1)
            for n in range(ADA_RING):
                pool.dma_start(ada[:, n], ada_w[0][:, n * 2 * P:(n + 1) * 2 * P].rearrange("(k p) n -> p k n", p=P)) \
                    .then_inc(ada_in[n], 16)
            for layer in range(DEPTH):
                with pool.Fori(1 - layer, 6) as i:
                    for r in range(ADA_RING):
                        pool.wait_ge(ada_done, 24 * layer + ADA_RING * i + (r + 1 - ADA_RING))
                        pool.dma_start(ada[:, r], ada_w[layer][:, ds(i * (8 * P) + r * 2 * P, 2 * P)]
                                       .rearrange("(k p) n -> p k n", p=P)).then_inc(ada_in[r], 16)
            for h in range(HEADS):
                if h == 0:
                    pool.wait_ge(sq_summed, 3 * KT)
                else:
                    pool.wait_ge(y_step, 3 * h)
                for n, g in enumerate((gn_f, gn_b)):
                    pool.dma_start(gn_row[:, n, :], g[:, h * DH:(h + 1) * DH].to_broadcast([P, DH])) \
                        .then_inc(gn_in, 16)

        @block.tensor
        def _(pe):
            def mm(o, a, b, first, last):
                return nc.tensor.matmul(o, a, b, start=first, stop=last, skip_group_check=True)

            def slot_free(s, half):
                p = s % 2
                if half is None:
                    half = s // 2
                if not (isinstance(half, int) and half < 1):
                    pe.wait_ge(slot_read[p], half)

            def unit_product(unit, r, kt, src, streams, ready=None):
                s_hi, s_lo = src
                pe.wait_ge(lo_ready, unit + 1)
                for k in range(kt):
                    if ready is not None:
                        pe.wait_ge(ready[0], ready[1] + (k + 1))
                    a_hi, a_lo = w_hi[:, r, k * P:(k + 1) * P], w_lo[:, r, k * P:(k + 1) * P]
                    for a, b in ((a_hi, s_hi), (a_hi, s_lo), (a_lo, s_hi)):
                        for o, toks in streams:
                            m = mm(o, a, b[:, k, toks], k == 0 and a is a_hi and b is s_hi, k == kt - 1 and a is a_lo)
                m.then_inc(unit_done, 1)

            def slot(p, bank):
                return ps[:, 3 * p + bank, :]

            def pair_block(blk, q, s, half, src, both, ready):
                slot_free(s, half)
                for h in range(2):
                    streams = [(slot(s % 2, h), LATS)]
                    if both:
                        streams.append((slot(s % 2, 2)[:, h * CTX:(h + 1) * CTX], CTXS))
                    unit_product(2 * blk + h, 2 * q + h, KT, src, streams, ready)

            def sum_squares(n, both):
                pe.wait_ge(sq_ready, n + 1)
                first, last = n % KT == 0, n % KT == KT - 1
                b = sq[:, n % 2]
                m = mm(ps[:, 6, :], mean_of[:], b[:, LATS], first, last)
                if both:
                    m = mm(ps[:, 7, 0:CTX], mean_of[:], b[:, CTXS], first, last)
                m.then_inc(sq_summed, 1)

            def out_phase(blk, s, kt, src, both, ready, norm=None):
                if norm is None:
                    loop = pe.Fori(0, 2)
                    with loop as i:
                        for u in range(4):
                            slot_free(s + u, s // 2 + 2 * i + u // 2)
                            streams = [(slot((s + u) % 2, 0), LATS)] + \
                                ([(slot((s + u) % 2, 2)[:, 0:CTX], CTXS)] if both else [])
                            unit_product(2 * blk + 4 * i + u, u, kt, src, streams, ready)
                    return
                for u in range(KT):
                    slot_free(s + u, None)
                    streams = [(slot((s + u) % 2, 0), LATS)] + \
                        ([(slot((s + u) % 2, 2)[:, 0:CTX], CTXS)] if both else [])
                    unit_product(2 * blk + u, u % RING, kt, src, streams, ready)
                    if u >= 1:
                        sum_squares(norm * KT + u - 1, both)
                sum_squares(norm * KT + KT - 1, both)

            def ada_block(n, r, bank, col):
                pe.wait_ge(ada_in[r], 16 * n)
                for t in range(2):
                    for k in range(KT):
                        m = mm(ps[:, bank, ds(col + 2 * t, 2)], ada[:, r, k, t * P:(t + 1) * P], silu_c[:, k, :],
                               k == 0, k == KT - 1)
                m.then_inc(ada_done, 1)

            pe.wait_ge(eye_in, 16)
            pe.wait_ge(par_rows, 16 * 16)
            for j, rows in enumerate((128, 116, 128, 120, 66, 66)):
                m = nc.tensor.transpose(ps[:, 6 + j // 4, (j % 4) * P:(j % 4) * P + rows], prow[0:rows, j, :],
                                        ident[0:rows, 0:rows])
            m.then_inc(par_T, 1)
            pe.wait_ge(silu_c_ready, 2)
            for n in range(8):
                ada_block(n // ADA_RING + 1, n % ADA_RING, 6, 4 * n)
            pe.wait_ge(tokens_in, 16 * (LT + CT))
            pe.wait_ge(filled, 4)
            pe.wait_ge(mod_ready, 1)
            for j in range(KT):
                s = S_XT + j
                slot_free(s, None)
                for t in range(LT + CT):
                    o = slot(s % 2, 0)[:, t * P:(t + 1) * P] if t < LT else slot(s % 2, 2)[:, (t - LT) * P:(t - LT + 1) * P]
                    m = nc.tensor.transpose(o, xin[:, t, j * P:(j + 1) * P], ident[:])
                m.then_inc(xT_done, 1)
                if j >= 1:
                    sum_squares(j - 1, True)
            sum_squares(KT - 1, True)
            pe.wait_ge(std_ready, 1)

            def pw1_body(i):
                for q in range(2):
                    pair_block(PW1 + 2 * i + q, q, S_PW1 + q, S_PW1 // 2 + i, (H_hi, H_lo), True, (h_lo_ready, 0))
                    for n in range(2):
                        ada_block(3 + i, 2 * q + n, 7, 32 + 16 * i + 8 * q + 4 * n)
            with pe.Fori(0, KT // 2) as i:
                pw1_body(i)
            with pe.Fori(0, 6) as i:
                for r in range(ADA_RING):
                    ada_block(7 + i, r, 6, 16 * i + 4 * r)
            slot_free(S_LN, None)
            for j in range(KT):
                pe.wait_ge(tap_done, TAPS * (j + 1))
                mm(slot(0, 0), mean_of[:], conv[:, j, 0:LAT], j == 0, j == KT - 1)
                m = mm(slot(0, 2)[:, 0:CTX], mean_of[:], conv[:, j, CTX_OUT:OUTW], j == 0, j == KT - 1)
            m.then_inc(mu_summed, 1)
            slot_free(S_LN + 1, None)
            for j in range(KT):
                pe.wait_ge(lsq_ready, j + 1)
                mm(slot(1, 0), mean_of[:], sq[:, j % 2, LATS], j == 0, j == KT - 1)
                mm(slot(1, 2)[:, 0:CTX], mean_of[:], sq[:, j % 2, CTXS], j == 0, j == KT - 1).then_inc(lsq_summed, 1)
            out_phase(PW2, S_PW2, KT, (H_hi, H_lo), True, (h_lo_ready, KT), norm=1)

            def ffn(blk, s, layer, both):
                h_at = 2 * KT + 2 * KT * layer
                mid_at = layer * FT
                pe.wait_ge(std_ready, 2 + 2 * layer)
                for c_no, n in enumerate(CHUNKS):
                    with pe.Fori(0, n // 2) as i:
                        for q in range(2):
                            pair_block(blk + 2 * i + q, q, s + q, s // 2 + i, (H_hi, H_lo), both, (h_lo_ready, h_at))
                    blk, s = blk + n, s + n
                    last = c_no == len(CHUNKS) - 1
                    out_phase(blk, s, n, (mid_hi, mid_lo), both, (mid_lo_ready, mid_at),
                              norm=2 + 2 * layer if last else None)
                    mid_at += n
                    blk, s = blk + 4, s + KT

            ffn(FFN0, S_FFN0, 0, True)

            H2 = (H_hi, H_lo)
            pe.wait_ge(std_ready, 3)

            def token_major(blk, streams):
                u0 = 2 * blk % RING
                pe.wait_ge(lo_ready, 2 * blk + 2)
                for o, t0 in streams:
                    for k in range(KT):
                        b_hi, b_lo = (w[:, u0:u0 + 2, k * P:(k + 1) * P] for w in (w_hi, w_lo))
                        a_hi, a_lo = (a[:, k, t0:t0 + P] for a in H2)
                        mm(o, a_hi, b_hi, k == 0, False)
                        mm(o, a_hi, b_lo, False, False)
                        m = mm(o, a_lo, b_hi, False, k == KT - 1)
                return m

            def toks4(p):
                return [(ps[:, 3 * p + t // 2, (t % 2) * DH:(t % 2 + 1) * DH], t * P) for t in range(LT)]

            def toks2(p):
                return [(ps[:, 3 * p + 2, t * DH:(t + 1) * DH], LAT + t * P) for t in range(CT)]

            h_at = 3 * KT
            for h in range(HEADS):
                blk, s = RET + 5 * h, S_RET + HEAD_USES * h
                slot_free(s, None)
                for u in range(2):
                    unit_product(2 * blk + u, (2 * blk + u) % RING, KT, H2, [(slot(0, u), LATS)], (h_lo_ready, h_at))
                blk += 1
                slot_free(s + 1, None)
                pe.wait_ge(lo_ready, 2 * blk + 2)
                token_major(blk, toks2(1))
                for u in range(2):
                    unit_product(2 * blk + u, (2 * blk + u) % RING, KT, H2, [(slot(1, u), LATS)])
                blk += 1
                slot_free(s + 2, None)
                token_major(blk, toks4(0) + toks2(0)).then_inc(unit_done, 2)
                slot_free(s + 3, None)
                pe.wait_ge(slot_read[0], (s + 2) // 2 + 1)
                for d in range(2):
                    for f in range(2):
                        for t in range(CT):
                            m = mm(ps[:, 3 + d, f * DH:(f + 1) * DH], kctx[:, d, t, f * P:(f + 1) * P], vctx[:, t, :],
                                   t == 0, t == CT - 1)
                m.then_inc(score_done, 1)
                pe.wait_ge(rot_step, 15 * h + 15)
                for j in range(LT):
                    n = h * LT + j
                    if n >= 2:
                        pe.wait_ge(score_read, n - 1)
                    if j < 2 and h >= 1:
                        pe.wait_ge(y_lo_ready, 2 * h)
                    for f in range(2):
                        m = mm(ps[:, 6 + j % 2, :], kT[:, f, j * P:(j + 1) * P], qT[:, f, :], f == 0, f == 1)
                    m.then_inc(score_done, 1)
                for d in range(2):
                    blk += 1
                    slot_free(s + 4 + 2 * d, None)
                    token_major(blk, toks4(0)).then_inc(unit_done, 2)
                    slot_free(s + 5 + 2 * d, None)
                    pe.wait_ge(score_read, (h + 1) * LT)
                    pe.wait_ge(qdec_ready, 2 * h + d + 1)
                    for i in range(LT):
                        o = ps[:, 3 + i // 2, (i % 2) * DH:(i % 2 + 1) * DH]
                        js = range(0, i + 1) if d == 0 else range(i, LT)
                        for n, j in enumerate(js):
                            at = sum((LT - a) if d == 0 else (a + 1) for a in range(j)) + (i - j if d == 0 else i)
                            mm(o, scores[:, d, at * P:(at + 1) * P], V[:, j, :], n == 0, False)
                        for f in range(2):
                            m = mm(o, (q_dec if d == 0 else kT)[:, f, i * P:(i + 1) * P], state[:, d, f, :], False, f == 1)
                    m.then_inc(score_done, 1)
                pe.wait_ge(y_step, 3 * (h + 1))
                for f in range(2):
                    for t in range(LT):
                        m = nc.tensor.transpose(ps[:, 6 + f, t * P:(t + 1) * P], y_tok[:, t, f * P:(f + 1) * P], ident[:])
                m.then_inc(yT_done, 1)
            pe.wait_ge(y_lo_ready, 2 * HEADS)
            out_phase(RET_OUT, S_RET_OUT, KT, (y_hi, y_lo), False, None, norm=3)
            ffn(FFN1, S_FFN1, 1, False)
            for j in range(KT):
                s = S_OUT + j
                slot_free(s, None)
                pe.wait_ge(fin_ready, j + 1)
                for t in range(LT):
                    m = nc.tensor.transpose(slot(s % 2, 0)[:, t * P:(t + 1) * P], tmp[:, j % 2, t * P:(t + 1) * P],
                                            ident[:])
                m.then_inc(xT_done, 1)

        @block.scalar
        def _(act):
            A = nc.scalar.activation

            def split_hi(unit, r):
                if isinstance(unit, int):
                    if unit >= UNITS:
                        return
                    act.wait_ge(raw_ready[r], 16 * (unit // RING + 1))
                    if unit >= RING:
                        act.wait_ge(unit_done, unit - (RING - 1))
                A(w_hi[:, r, :], w_raw[:, r, :], ACT.Copy).then_inc(hi_ready, 1)

            def split_hi_at(base, i, off):
                unit = base + off
                if isinstance(i, int):
                    return split_hi(unit + 4 * i, unit % RING)
                act.wait_ge(raw_ready[unit % RING], 16 * i + 16 * (unit // RING + 1))
                act.wait_ge(unit_done, 4 * i + (unit - (RING - 1)))
                A(w_hi[:, unit % RING, :], w_raw[:, unit % RING, :], ACT.Copy).then_inc(hi_ready, 1)

            def bank(p, b):
                return ps[:, 3 * p + b, :]

            def square(n, both, wait, val):
                act.wait_ge(wait, val)
                if n >= 2:
                    act.wait_ge(sq_summed, n - 1)
                w = TOK if both else LAT
                A(sq[:, n % 2, 0:w], X[:, n % KT, 0:w], ACT.Square).then_inc(sq_ready, 1)

            def root(norm, both):
                act.wait_ge(sq_summed, KT * (norm + 1))
                a = A(rstd[:, LATS], ps[:, 6, :], ACT.Sqrt, bias=eps[:, 0:1])
                if both:
                    a = A(rstd[:, CTXS], ps[:, 7, 0:CTX], ACT.Sqrt, bias=eps[:, 0:1])
                a.then_inc(std_ready, 1)

            def shifted_hi(at, n_scaled, layer, sub, both):
                for j in range(KT):
                    act.wait_ge(scaled, n_scaled + j + 1)
                    for m, toks in groups(both):
                        a = A(H_hi[:, j, toks], tmp[:, j % 2, toks], ACT.Identity,
                              bias=mod[:, layer, 24 * sub + j, m:m + 1])
                    a.then_inc(h_hi_ready, 1)

            act.wait_ge(par_ready, 1)
            for v in range(2):
                A(silu_c[:, :, v], par[:, C_COL + 8 * v:C_COL + 8 * v + 8], ACT.Silu).then_inc(silu_c_ready, 1)
            for u in range(3):
                split_hi(u, u)
            for j in range(KT):
                p = j % 2
                act.wait_ge(xT_done, j + 1)
                A(X[:, j, LATS], bank(p, 0), ACT.Copy)
                A(X[:, j, CTXS], bank(p, 2)[:, 0:CTX], ACT.Copy).then_inc(slot_read[p], 1)
                square(j, True, slot_read[p], j // 2 + 1)
            root(0, True)
            shifted_hi(0, 0, 0, 0, True)

            def pw1_body(i):
                for q in range(2):
                    split_hi_at(2 * PW1, i, 2 * q + 3)
                    split_hi_at(2 * PW1, i, 2 * q + 4)
                    act.wait_ge(unit_done, 4 * i + (2 * q + 2))
                    b = par[:, ds(2 * i + (PW1_B + KT + q), 1)]
                    A(tmp[:, q, LATS], bank(q, 1), ACT.Sigmoid, bias=b)
                    A(tmp[:, q, CTXS], bank(q, 2)[:, CTX:], ACT.Sigmoid, bias=b).then_inc(sig_ready, 1)
            pw1_body(0)
            with act.Fori(1, KT // 2) as i:
                pw1_body(i)
            for j in range(KT):
                act.wait_ge(centered, 2 * j + 2 if j < KT - 1 else 2 * j + 1)
                if j == KT - 1:
                    act.wait_ge(slot_read[0], S_LN // 2 + 1)
                if j >= 2:
                    act.wait_ge(lsq_summed, j - 1)
                A(sq[:, j % 2, LATS], conv[:, j, 0:LAT], ACT.Square)
                A(sq[:, j % 2, CTXS], conv[:, j, CTX_OUT:OUTW], ACT.Square).then_inc(lsq_ready, 1)
            act.wait_ge(lsq_summed, KT)
            A(rstd[:, LATS], bank(1, 0), ACT.Sqrt, bias=eps[:, 0:1])
            A(rstd[:, CTXS], bank(1, 2)[:, 0:CTX], ACT.Sqrt, bias=eps[:, 0:1]).then_inc(slot_read[1], 1)
            for j in range(KT):
                act.wait_ge(ln_scaled, j + 1)
                if j >= 2:
                    act.wait_ge(h_lo_ready, KT + j - 1)
                A(sil[:, j % 2, :], tmp[:, j % 2, :], ACT.Silu, bias=par[:, LN_B + j:LN_B + j + 1]).then_inc(ln_silu, 1)
                act.wait_ge(ln_silu, j + 1)
                A(H_hi[:, j, :], sil[:, j % 2, :], ACT.Copy).then_inc(h_hi_ready, 1)

            def gated(p, both, gates, bias=None):
                for m, toks in groups(both):
                    a = A(tmp[:, p, toks], bank(p, 0) if m == 0 else bank(p, 2)[:, 0:CTX], ACT.Identity,
                          scale=gates[m], bias=0.0 if bias is None else bias[m])
                a.then_inc(slot_read[p], 1)

            def out_phase(blk, s, x_at, both, layer, gate_at):
                with act.Fori(0, 2) as i:
                    for u in range(4):
                        p = u % 2
                        split_hi_at(2 * blk, i, u + 3)
                        act.wait_ge(unit_done, 4 * i + (2 * blk + u + 1))
                        act.wait_ge(x_updated, 4 * i + (x_at + u - 1))
                        g = [mod[:, layer, ds(4 * i + (gate_at + u), 1), m] for m in range(2)]
                        gated(p, both, g)

            def out_phase_norm(blk, s, x_at, both, layer, gate_at, norm, bias=False):
                for u in range(KT):
                    p = u % 2
                    split_hi(2 * blk + u + 3, (u + 3) % RING)
                    act.wait_ge(unit_done, 2 * blk + u + 1)
                    if x_at + u - 1 > 0:
                        act.wait_ge(x_updated, x_at + u - 1)
                    g = [mod[:, layer, gate_at + u, m:m + 1] for m in range(2)]
                    gated(p, both, g, [pw2_gb[:, u, m:m + 1] for m in range(2)] if bias else None)
                    square(norm * KT + u, both, x_updated, x_at + u + 1)
                root(norm, both)

            act.wait_ge(mod_ready, 6)
            out_phase_norm(PW2, S_PW2, 0, True, 0, 16, 1, bias=True)

            def ffn(blk, s, layer, both, x_at):
                f = 0
                for c_no, n in enumerate(CHUNKS):
                    act.wait_ge(x_updated, x_at)
                    with act.Fori(0, n // 2) as i:
                        for q in range(2):
                            g_at = layer * FT + f + q
                            split_hi_at(2 * blk, i, 2 * q + 3)
                            split_hi_at(2 * blk, i, 2 * q + 4)
                            act.wait_ge(unit_done, 4 * i + (2 * blk + 2 * q + 2))
                            w1 = par[:, ds(2 * i + (FFN_DW_W + layer * P + FT + f + q), 1)]
                            b = par[:, ds(2 * i + (FFN_DW_B + g_at), 1)]
                            a = A(tmp[:, q, LATS], bank(q, 1), ACT.Identity, scale=w1, bias=b)
                            if both:
                                a = A(tmp[:, q, CTXS], bank(q, 2)[:, CTX:], ACT.Identity, scale=w1, bias=b)
                            a.then_inc(g_first, 1)
                            w = TOK if both else LAT
                            act.wait_ge(g_taps, (8 if both else 4) * i + (taps_at(layer) + (4 if both else 2) * (f + q + 1)))
                            A(tmp[:, q, 0:w], tmp[:, q, 0:w], ACT.Silu).then_inc(g_silu, 1)
                            act.wait_ge(slot_read[q], i + (s // 2 + 1))
                            A(mid_hi[:, ds(2 * i + q, 1), 0:w], m32[:, q:q + 1, 0:w], ACT.Copy).then_inc(mid_hi_ready, 1)
                    f += n
                    blk, s = blk + n, s + n
                    if c_no < len(CHUNKS) - 1:
                        out_phase(blk, s, x_at, both, layer, 40)
                    else:
                        out_phase_norm(blk, s, x_at, both, layer, 40, 2 + 2 * layer)
                    blk, s, x_at = blk + 4, s + KT, x_at + KT

            shifted_hi(2 * KT, KT, 0, 1, True)
            ffn(FFN0, S_FFN0, 0, True, KT)
            shifted_hi(3 * KT, 2 * KT, 1, 0, True)

            act.wait_ge(consts_in, 16 * 8)
            A(ngam[:], decay_log[:], ACT.Exp).then_inc(lg_step, 1)
            act.wait_ge(lg_step, 2)
            for h in range(HEADS):
                for d in range(2):
                    A(zeta[:, h, d, :], tcol[:, 2 + 2 * d:4 + 2 * d], ACT.Exp,
                      scale=lgam[:, HEADS * d + h:HEADS * d + h + 1]).then_inc(zeta_ready, 1)
            for h in range(HEADS):
                blk, s = RET + 5 * h, S_RET + HEAD_USES * h
                ab = slice(h, h + 1), slice(HEADS + h, HEADS + h + 1)
                u = 2 * blk
                split_hi(u + 3, (u + 3) % RING)
                act.wait_ge(age_ready, 2 * h + 2)
                A(decay[:, 0, :], decay[:, 0, :], ACT.Exp, scale=lgam[:, ab[0]])
                A(decay[:, 1, :], decay[:, 1, :], ACT.Exp, scale=ngam[:, ab[1]]).then_inc(decay_exp, 1)
                split_hi(u + 4, (u + 4) % RING)
                split_hi(u + 5, (u + 5) % RING)
                split_hi(u + 6, (u + 6) % RING)
                act.wait_ge(unit_done, 2 * (blk + 2) + 2)
                A(V[:].rearrange("p a b -> p (a b)"), ps[:, 0:2, :].rearrange("p a b -> p (a b)"), ACT.Copy)
                A(vctx.rearrange("p a b -> p (a b)"), ps[:, 2, :], ACT.Copy).then_inc(slot_read[0], 1)
                split_hi(u + 7, (u + 7) % RING)
                split_hi(u + 8, (u + 8) % RING)
                act.wait_ge(score_done, 7 * h + 1)
                A(state[:].rearrange("p d f v -> p (d f v)"), ps[:, 3:5, :].rearrange("p a b -> p (a b)"),
                  ACT.Copy).then_inc(slot_read[1], 1)
                act.wait_ge(score_read, LT * (h + 1))
                A(decay[:, 0, :], iota[:], ACT.Exp, scale=lgam[:, ab[0]], bias=lgam[:, ab[0]])
                A(decay[:, 1, :], iota[:], ACT.Exp, scale=ngam[:, ab[1]], bias=lgam512[:, ab[1]]).then_inc(decay_exp, 1)
                for d in range(2):
                    act.wait_ge(unit_done, 2 * (blk + 3 + d) + 2)
                    if 2 * h + d >= 1:
                        act.wait_ge(y_step, 3 * h + d)
                    A(gate.rearrange("p a b -> p (a b)"), ps[:, 0:2, :].rearrange("p a b -> p (a b)"), ACT.Silu) \
                        .then_inc(slot_read[0], 1)
                    if d == 0:
                        split_hi(u + 9, (u + 9) % RING)
                        split_hi(u + 10, (u + 10) % RING)
                    else:
                        split_hi(u + 11, (u + 11) % RING)
                        split_hi(u + 12, (u + 12) % RING)
                    act.wait_ge(gn_stats, 2 * (2 * h + d) + 2)
                    A(gn_mv[:, :, 1], gn_mv[:, :, 1], ACT.Sqrt, bias=eps[:, 1:2]).then_inc(gn_std, 1)
                act.wait_ge(yT_done, h + 1)
                for f in range(2):
                    a = A(y_hi[:, 2 * h + f, :], ps[:, 6 + f, :], ACT.Copy)
                    a.then_inc(y_hi_ready, 1)
            out_phase_norm(RET_OUT, S_RET_OUT, KT * 4, False, 1, 16, 3)
            shifted_hi(4 * KT, 3 * KT, 1, 1, False)
            ffn(FFN1, S_FFN1, 1, False, KT * 5)
            for j in range(KT):
                p = j % 2
                act.wait_ge(xT_done, KT + j + 1)
                a = A(otok[:, :, j * P:(j + 1) * P], bank(p, 0).rearrange("p (t n) -> p t n", t=LT), ACT.Copy)
                a.then_inc(slot_read[p], 1) if j < KT - 1 else a.then_inc(out_ready, 1)

        @block.vector
        def _(dve):
            v = nc.vector

            def bank(p, b):
                return ps[:, 3 * p + b, :]

            def split_lo(unit, r):
                if isinstance(unit, int) and unit >= UNITS:
                    return
                dve.wait_ge(hi_ready, unit + 1)
                v.tensor_tensor(w_lo[:, r, :], w_raw[:, r, :], w_hi[:, r, :].bitcast(F32), ALU.subtract) \
                    .then_inc(lo_ready, 1)

            def recip(norm, std_at, both):
                dve.wait_ge(std_ready, std_at)
                w = TOK if both else LAT
                v.reciprocal(rstd[:, 0:w], rstd[:, 0:w]).then_inc(rstd_ready, 1)

            def normed(at, rstd_at, scaled_at, layer, sub, both):
                def scale(j):
                    if j == 0:
                        dve.wait_ge(rstd_ready, rstd_at)
                    if j >= 2:
                        dve.wait_ge(h_lo_ready, at + j - 1)
                    for m, toks in groups(both):
                        o = v.scalar_tensor_tensor(tmp[:, j % 2, toks], X[:, j, toks], gain[:, layer, sub, j, m:m + 1],
                                                   rstd[:, toks], ALU.mult, ALU.mult)
                    o.then_inc(scaled, 1)
                scale(0)
                for j in range(KT):
                    if j + 1 < KT:
                        scale(j + 1)
                    dve.wait_ge(h_hi_ready, at + j + 1)
                    for m, toks in groups(both):
                        o = v.scalar_tensor_tensor(H_lo[:, j, toks], tmp[:, j % 2, toks],
                                                   mod[:, layer, 24 * sub + j, m:m + 1],
                                                   H_hi[:, j, toks].bitcast(F32), ALU.add, ALU.subtract)
                    o.then_inc(h_lo_ready, 1)

            def two(ap):
                return ap.unsqueeze(2).to_broadcast([P, ap.shape[1], 2])

            def modulation(src_bank, layer, t0, t1, at):
                v.tensor_tensor(mod[:, layer, t0:t1, :], ps[:, src_bank, 2 * t0:2 * t1].rearrange("p (t m) -> p t m", m=2),
                                two(par[:, ADA_B + 48 * layer + t0:ADA_B + 48 * layer + t1]), ALU.add) \
                    .then_inc(mod_ready, 1)
                at += 1
                dve.wait_ge(mod_ready, at)
                for sub, (col, g) in enumerate(((8, NORM1), (32, NORM2))):
                    if t0 <= col < t1:
                        v.scalar_tensor_tensor(gain[:, layer, sub], mod[:, layer, col:col + KT, :], 1.0,
                                               two(par[:, g + KT * layer:g + KT * (layer + 1)]), ALU.add, ALU.mult) \
                            .then_inc(mod_ready, 1)

            dve.wait_ge(par_T, 1)
            v.tensor_copy(par[:, 0:244], ps[:, 6, 0:244])
            v.tensor_copy(par[:, 256:504], ps[:, 6, 256:504])
            for layer in range(DEPTH):
                o = v.tensor_copy(par[:, FFN_DW_W + P * layer:FFN_DW_W + P * layer + 66],
                                  ps[:, 7, P * layer:P * layer + 66])
            o.then_inc(par_ready, 1)
            for u in range(3):
                split_lo(u, u)
            dve.wait_ge(par_ready, 1)
            dve.wait_ge(ada_done, 8)
            modulation(6, 0, 0, 16, 0)
            recip(0, 1, True)
            dve.wait_ge(mod_ready, 2)
            normed(0, 1, 0, 0, 0, True)

            def pw1_body(i):
                for q in range(2):
                    split_lo(4 * i + (2 * q + 3), (2 * q + 3) % RING)
                    split_lo(4 * i + (2 * q + 4), (2 * q + 4) % RING)
                    dve.wait_ge(sig_ready, 2 * i + (q + 1))
                    if not (isinstance(i, int)):
                        dve.wait_ge(tap_done, 2 * TAPS * i + TAPS * (q - 1))
                    else:
                        dve.wait_ge(filled, 4)
                    b = par[:, ds(2 * i + (PW1_B + q), 1)]
                    v.scalar_tensor_tensor(upad[:, q, PAD:PAD + LAT], bank(q, 0), b, tmp[:, q, LATS], ALU.add, ALU.mult)
                    v.scalar_tensor_tensor(upad[:, q, CTX_PAD:CTX_PAD + CTX], bank(q, 2)[:, 0:CTX], b, tmp[:, q, CTXS],
                                           ALU.add, ALU.mult).then_inc(slot_read[q], 1)
                    dve.wait_ge(slot_read[q], i + (S_PW1 // 2 + 1))
                    row = conv[:, ds(2 * i + q, 1), 0:OUTW].rearrange("p a b -> p (a b)")
                    for k in range(TAPS):
                        w = par[:, ds(2 * i + (DW_W + KT * k + q), 1)]
                        if k == 0:
                            o = v.tensor_scalar(row, upad[:, q, 0:OUTW], w, par[:, ds(2 * i + (DW_B + q), 1)],
                                                ALU.mult, ALU.add)
                        else:
                            dve.wait_ge(tap_done, 2 * TAPS * i + (TAPS * q + k))
                            o = v.scalar_tensor_tensor(row, upad[:, q, k:k + OUTW], w, row, ALU.mult, ALU.add)
                        o.then_inc(tap_done, 1)
            pw1_body(0)
            with dve.Fori(1, KT // 2) as i:
                pw1_body(i)
            dve.wait_ge(ada_done, 24)
            modulation(7, 0, 16, 48, 2)
            v.tensor_tensor(pw2_gb[:], mod[:, 0, 16:24, :], two(par[:, PW2_B:PW2_B + KT]), ALU.mult)
            dve.wait_ge(ada_done, 48)
            modulation(6, 1, 0, 48, 4)
            dve.wait_ge(mu_summed, 1)
            for j in range(KT):
                v.tensor_tensor(conv[:, j, 0:LAT], conv[:, j, 0:LAT], bank(0, 0), ALU.subtract).then_inc(centered, 1)
                v.tensor_tensor(conv[:, j, CTX_OUT:OUTW], conv[:, j, CTX_OUT:OUTW], bank(0, 2)[:, 0:CTX], ALU.subtract) \
                    .then_inc(centered if j < KT - 1 else slot_read[0], 1)
            dve.wait_ge(slot_read[1], S_LN // 2 + 1)
            v.reciprocal(rstd[:], rstd[:]).then_inc(rstd_ready, 1)
            dve.wait_ge(rstd_ready, 2)

            def ln_scale(j):
                if j >= 2:
                    dve.wait_ge(ln_silu, j - 1)
                g = par[:, LN_G + j:LN_G + j + 1]
                v.scalar_tensor_tensor(tmp[:, j % 2, LATS], conv[:, j, 0:LAT], g, rstd[:, LATS], ALU.mult, ALU.mult)
                v.scalar_tensor_tensor(tmp[:, j % 2, CTXS], conv[:, j, CTX_OUT:OUTW], g, rstd[:, CTXS],
                                       ALU.mult, ALU.mult).then_inc(ln_scaled, 1)
            dve.wait_ge(slot_read[0], S_LN // 2 + 1)
            ln_scale(0)
            for j in range(KT):
                if j + 1 < KT:
                    ln_scale(j + 1)
                dve.wait_ge(h_hi_ready, KT + j + 1)
                v.tensor_tensor(H_lo[:, j, :], sil[:, j % 2, :], H_hi[:, j, :].bitcast(F32), ALU.subtract) \
                    .then_inc(h_lo_ready, 1)

            def residual(s, x_at, i, u, both, col):
                w = TOK if both else LAT
                p = (s + u) % 2
                if isinstance(i, int) and i == 0:
                    dve.wait_ge(slot_read[p], (s + u) // 2 + 1)
                else:
                    dve.wait_ge(slot_read[p], 2 * i + ((s + u) // 2 + 1))
                row = X[:, col, 0:w]
                if not isinstance(col, int):
                    row = row.rearrange("p a b -> p (a b)")
                v.tensor_tensor(row, row, tmp[:, p, 0:w], ALU.add).then_inc(x_updated, 1)

            def out_phase(blk, s, x_at, both, norm=None):
                if norm is None:
                    with dve.Fori(0, 2) as i:
                        for u in range(4):
                            split_lo(4 * i + (2 * blk + u + 3), (u + 3) % RING)
                            dve.wait_ge(x_updated, x_at - KT + 4 * i + (u + 1))
                            residual(s, x_at, i, u, both, ds(4 * i + u, 1))
                else:
                    for u in range(KT):
                        split_lo(2 * blk + u + 3, (u + 3) % RING)
                        if x_at:
                            dve.wait_ge(x_updated, x_at - KT + u + 1)
                        residual(s, x_at, 0, u, both, u)

            out_phase(PW2, S_PW2, 0, True, norm=1)

            def ffn(blk, s, layer, both, x_at):
                f = 0
                w = TOK if both else LAT
                steps = 4 if both else 2
                for c_no, n in enumerate(CHUNKS):
                    with dve.Fori(0, n // 2) as i:
                        for q in range(2):
                            split_lo(4 * i + (2 * blk + 2 * q + 3), (2 * q + 3) % RING)
                            split_lo(4 * i + (2 * blk + 2 * q + 4), (2 * q + 4) % RING)
                            t_at = taps_at(layer) + steps * (f + q)
                            wt = [par[:, ds(2 * i + (FFN_DW_W + layer * P + FT * k + f + q), 1)] for k in (0, 2)]
                            t = tmp[:, q]
                            dve.wait_ge(g_first, 2 * i + (layer * FT + f + q + 1))
                            streams = [(bank(q, 1), 0, LAT)] + ([(bank(q, 2)[:, CTX:], LAT, CTX)] if both else [])
                            for b, t0, m in streams:
                                v.scalar_tensor_tensor(t[:, t0 + 1:t0 + m], b[:, 0:m - 1], wt[0], t[:, t0 + 1:t0 + m],
                                                       ALU.mult, ALU.add).then_inc(g_taps, 1)
                            for n_s, (b, t0, m) in enumerate(streams):
                                dve.wait_ge(g_taps, 2 * steps * i + (t_at + n_s + 1))
                                v.scalar_tensor_tensor(t[:, t0:t0 + m - 1], b[:, 1:m], wt[1], t[:, t0:t0 + m - 1],
                                                       ALU.mult, ALU.add).then_inc(g_taps, 1)
                            dve.wait_ge(g_silu, 2 * i + (layer * FT + f + q + 1))
                            o = v.tensor_tensor(m32[:, q, LATS], bank(q, 0), tmp[:, q, LATS], ALU.mult)
                            if both:
                                o = v.tensor_tensor(m32[:, q, CTXS], bank(q, 2)[:, 0:CTX], tmp[:, q, CTXS], ALU.mult)
                            o.then_inc(slot_read[q], 1)
                            dve.wait_ge(mid_hi_ready, 2 * i + (layer * FT + f + q + 1))
                            v.tensor_tensor(mid_lo[:, ds(2 * i + q, 1), 0:w], m32[:, q:q + 1, 0:w],
                                            mid_hi[:, ds(2 * i + q, 1), 0:w].bitcast(F32), ALU.subtract) \
                                .then_inc(mid_lo_ready, 1)
                    f += n
                    blk, s = blk + n, s + n
                    out_phase(blk, s, x_at, both, norm=2 if c_no == len(CHUNKS) - 1 else None)
                    blk, s, x_at = blk + 4, s + KT, x_at + KT

            recip(1, 2, True)
            normed(2 * KT, 3, KT, 0, 1, True)
            ffn(FFN0, S_FFN0, 0, True, KT)
            recip(2, 3, True)
            normed(3 * KT, 4, 2 * KT, 1, 0, True)

            dve.wait_ge(lg_step, 1)
            v.tensor_scalar(lgam512[:], ngam[:], -float(LAT), None, ALU.mult)
            v.tensor_scalar(lgam[:], ngam[:], -1.0, None, ALU.mult).then_inc(lg_step, 1)

            def grid(ap, parts=slice(0, P)):
                return ap[parts].rearrange("p (r c) -> p r c", c=GRID_W)

            def rotate(p, dst, scale, n, frees=None):
                for f in range(2):
                    n_at = n + 4 * f
                    if f == 0:
                        cs = [rrow[:, a, :].unsqueeze(2).to_broadcast([P, ROWS, GRID_W]) for a in range(2)]
                    else:
                        cs = [rcol[:, a, :].unsqueeze(1).to_broadcast([P, ROWS, GRID_W]) for a in range(2)]
                    if n_at:
                        dve.wait_ge(rot_step, n_at)
                    src = bank(p, f)
                    v.scalar_tensor_tensor(grid(cosd), grid(src), scale, cs[0], ALU.mult, ALU.mult).then_inc(rot_step, 1)
                    for a in range(2):
                        to, frm = slice(64 * a, 64 * a + 64), slice(64 - 64 * a, 128 - 64 * a)
                        o = v.scalar_tensor_tensor(grid(rot, to), grid(src, frm), scale, cs[1][to], ALU.mult, ALU.mult)
                        if f == 1 and a == 1 and frees is not None:
                            o.then_inc(slot_read[p], 1)
                            dve.wait_ge(slot_read[p], frees)
                        else:
                            o.then_inc(rot_step, 1)
                            dve.wait_ge(rot_step, n_at + 2 + a)
                    v.tensor_tensor(dst[:, f, :], cosd, rot, ALU.add).then_inc(rot_step, 1)

            for h in range(HEADS):
                blk, s = RET + 5 * h, S_RET + HEAD_USES * h
                u = 2 * blk
                split_lo(u + 3, (u + 3) % RING)
                if h:
                    dve.wait_ge(qdec_ready, 2 * h)
                v.tensor_scalar(decay[:, 0, :], iota[:], tcol[:, 0:1], 0.0, ALU.subtract, ALU.max).then_inc(age_ready, 1)
                v.tensor_scalar(decay[:, 1, :], iota[:], tcol[:, 1:2], 0.0, ALU.subtract, ALU.min).then_inc(age_ready, 1)
                split_lo(u + 4, (u + 4) % RING)
                dve.wait_ge(unit_done, 2 * blk + 2)
                if h:
                    dve.wait_ge(y_step, 3 * h)
                rotate(0, qT, DH ** -0.5, 15 * h, s // 2 + 1)
                split_lo(u + 5, (u + 5) % RING)
                split_lo(u + 6, (u + 6) % RING)
                dve.wait_ge(decay_exp, 2 * h + 1)
                v.tensor_tensor(decay[:, 0, 0:P], decay[:, 0, 0:P], tup[:], ALU.mult)
                v.tensor_tensor(decay[:, 1, LAT - P:LAT], decay[:, 1, LAT - P:LAT], tlow[:], ALU.mult) \
                    .then_inc(decay_ready, 1)
                dve.wait_ge(unit_done, 2 * (blk + 1) + 2)
                if h == 0:
                    dve.wait_ge(zeta_ready, 2 * HEADS)
                rotate(1, kT, 1.0, 15 * h + 7)
                for t in range(CT):
                    for d in range(2):
                        o = v.tensor_scalar(kctx[:, d, t, :], bank(1, 2)[:, t * DH:(t + 1) * DH], zeta[:, h, d, t:t + 1],
                                            None, ALU.mult)
                o.then_inc(slot_read[1], 1)
                split_lo(u + 7, (u + 7) % RING)
                split_lo(u + 8, (u + 8) % RING)
                for j in range(LT):
                    dve.wait_ge(score_done, 7 * h + 2 + j)
                    if j == 0:
                        dve.wait_ge(decay_ready, h + 1)
                    at0 = sum(LT - a for a in range(j)) * P
                    at1 = sum(a + 1 for a in range(j)) * P
                    b = ps[:, 6 + j % 2, :]
                    v.tensor_tensor(scores[:, 0, at0:at0 + LAT - j * P], b[:, j * P:], decay[:, 0, 0:LAT - j * P], ALU.mult)
                    v.tensor_tensor(scores[:, 1, at1:at1 + (j + 1) * P], b[:, 0:(j + 1) * P],
                                    decay[:, 1, LAT - (j + 1) * P:], ALU.mult).then_inc(score_read, 1)
                dve.wait_ge(decay_exp, 2 * h + 2)
                dve.wait_ge(rot_step, 15 * h + 15)
                for d, dst in enumerate((q_dec, kT[:])):
                    v.tensor_tensor(dst, qT[:], decay[:, d, :].unsqueeze(1).to_broadcast([P, 2, LAT]), ALU.mult) \
                        .then_inc(qdec_ready, 1)
                for d in range(2):
                    n = 2 * h + d
                    if d == 0:
                        split_lo(u + 9, (u + 9) % RING)
                        split_lo(u + 10, (u + 10) % RING)
                    else:
                        split_lo(u + 11, (u + 11) % RING)
                        split_lo(u + 12, (u + 12) % RING)
                    dve.wait_ge(slot_read[0], (s + 4 + 2 * d) // 2 + 1)
                    dve.wait_ge(gn_in, 32 * (h + 1))
                    v.tensor_tensor(gate, gate, gn_row[:, d, :].unsqueeze(1).to_broadcast([P, LT, DH]), ALU.mult) \
                        .then_inc(gate_ready, 1)
                    dve.wait_ge(score_done, 7 * h + 6 + d)
                    if n:
                        dve.wait_ge(y_step, 3 * h + d)
                    for i in range(LT):
                        o_i = ps[:, 3 + i // 2, (i % 2) * DH:(i % 2 + 1) * DH]
                        o = v.bn_stats(gn_st[:, i, :], o_i)
                    o.then_inc(gn_stats, 1)
                    dve.wait_ge(gn_stats, 2 * n + 1)
                    for i in range(LT):
                        o = v.bn_aggr(gn_mv[:, i, :], gn_st[:, i, :])
                    o.then_inc(gn_stats, 1)
                    dve.wait_ge(gn_std, n + 1)
                    v.reciprocal(gn_mv[:, :, 1], gn_mv[:, :, 1]).then_inc(gn_rstd, 1)
                    dve.wait_ge(gn_rstd, n + 1)
                    dst = y_tok if d == 0 else q_dec.rearrange("p a b -> p (a b)").rearrange("p (t v) -> p t v", t=LT)
                    for i in range(LT):
                        o_i = ps[:, 3 + i // 2, (i % 2) * DH:(i % 2 + 1) * DH]
                        o = v.tensor_scalar(dst[:, i, :], o_i, gn_mv[:, i, 0:1], gn_mv[:, i, 1:2], ALU.subtract, ALU.mult)
                    o.then_inc(slot_read[1], 1)
                    dve.wait_ge(slot_read[1], (s + 5 + 2 * d) // 2 + 1)
                    dve.wait_ge(gate_ready, n + 1)
                    if d == 0:
                        v.tensor_tensor(y_tok, y_tok, gate, ALU.mult).then_inc(y_step, 1)
                    else:
                        v.tensor_tensor(dst, dst, gate, ALU.mult).then_inc(y_step, 1)
                        dve.wait_ge(y_step, 3 * h + 2)
                        v.tensor_tensor(y_tok, y_tok, dst, ALU.add).then_inc(y_step, 1)
                dve.wait_ge(y_hi_ready, 2 * h + 2)
                for f in range(2):
                    v.tensor_tensor(y_lo[:, 2 * h + f, :], ps[:, 6 + f, :], y_hi[:, 2 * h + f, :].bitcast(F32),
                                    ALU.subtract).then_inc(y_lo_ready, 1)

            out_phase(RET_OUT, S_RET_OUT, KT * 4, False, norm=3)
            recip(3, 4, False)
            normed(4 * KT, 5, 3 * KT, 1, 1, False)
            ffn(FFN1, S_FFN1, 1, False, KT * 5)
            recip(4, 5, False)
            dve.wait_ge(rstd_ready, 6)
            for j in range(KT):
                if j >= 2:
                    dve.wait_ge(xT_done, KT + j - 1)
                v.scalar_tensor_tensor(tmp[:, j % 2, LATS], X[:, j, LATS], par[:, FINAL_G + j:FINAL_G + j + 1],
                                       rstd[:, LATS], ALU.mult, ALU.mult).then_inc(fin_ready, 1)


_INS = ["x", "c", "ctx", "c_ctx", "ada_w", "ada_b", "norm1_g", "norm2_g", "conv_pw1_w", "conv_pw1_b", "conv_dw_w",
        "conv_dw_b", "conv_ln_g", "conv_ln_b", "conv_pw2_w", "conv_pw2_b", "ret_w_in", "ret_w_out", "ret_decay_f",
        "ret_decay_b", "ret_gn_f", "ret_gn_b", "ffn_w_in", "ffn_dw_w", "ffn_dw_b", "ffn_w_out", "final_g"]


def shape_constants():
    import numpy as np
    f = np.float32
    p = np.arange(P)
    half = DH // 4
    freqs = (10000.0 ** (-np.arange(half, dtype=f) / f(half))).astype(f)
    sign = np.where(p < half, -1.0, 1.0)[:, None]

    def table(pos):
        ang = (pos[None, :].astype(f) * freqs[p % half][:, None]).astype(f).astype(np.float64)
        return np.stack([np.cos(ang), sign * np.sin(ang)], axis=1).astype(f)

    col = np.stack([p, p + LAT - P, CTX - 1 - p, CTX - 1 - P - p, p, p + P], axis=1).astype(f)
    return {
        "eye": np.eye(P, dtype=f),
        "ages": np.broadcast_to(np.arange(LAT, dtype=f), (P, LAT)).copy(),
        "tri_low": (p[None, :] <= p[:, None]).astype(f),
        "tri_up": (p[None, :] >= p[:, None]).astype(f),
        "rope_row": table(np.arange(ROWS)),
        "rope_col": table(np.arange(GRID_W)),
        "token_cols": col,
    }


def kernel(**inputs):
    import numpy as _np
    import concourse.bacc as _bacc
    from concourse import mybir as _mybir
    from concourse.bass_utils import run_bass_kernel_spmd as _run

    nc = _bacc.Bacc("TRN2", target_bir_lowering=False, num_devices=1)
    arrays, args = {}, []
    for name, a in [(n, _np.ascontiguousarray(inputs[n])) for n in _INS] + list(shape_constants().items()):
        arrays[f"in_{name}"] = a
        args.append(nc.dram_tensor(f"in_{name}", a.shape, _mybir.dt.from_np(a.dtype), kind="ExternalInput").ap())
    args.append(nc.dram_tensor("out", (1, LAT, D), _mybir.dt.float32, kind="ExternalOutput").ap())
    backbone(nc, *args)
    r = _run(nc, [arrays], core_ids=[0])
    return r.results[0]["out"]
```

```python
from contextlib import ExitStack

import concourse.bass as bass
from concourse import mybir

F32 = mybir.dt.float32
F32R = mybir.dt.float32r
ALU = mybir.AluOpType
ACT = mybir.ActivationFunctionType
ds = bass.ds

P = 128
D = 1024
KT = D // P
LAT, CTX = 512, 256
TOK = LAT + CTX
LT, CT = LAT // P, CTX // P
DEPTH = 2
F = ((8 * D // 3 + 127) // 128) * 128
FT = F // P
TAPS = 31
PAD = TAPS // 2
CTX_PAD = PAD + LAT + PAD
PADW = CTX_PAD + CTX + PAD
CTX_OUT = LAT + PAD
OUTW = CTX_OUT + CTX
HEADS, DH = 4, 256
GRID_W = 64
ROWS = LAT // GRID_W
NORM_EPS, GN_EPS = 1e-6, 1e-5
CHUNKS = [8, 8, FT - 16]
RING = 4

PW1, PW2 = 0, KT
FFN0 = PW2 + KT // 2
FFN_BLOCKS = FT + 4 * len(CHUNKS)
RET = FFN0 + FFN_BLOCKS
RET_OUT = RET + 5 * HEADS
FFN1 = RET_OUT + KT // 2
BLOCKS = FFN1 + FFN_BLOCKS
UNITS = 2 * BLOCKS

S_XT = 0
S_PW1 = S_XT + KT
S_LN = S_PW1 + 2 * KT
S_PW2 = S_LN + 2
S_FFN0 = S_PW2 + KT
S_FFN = FT + KT * len(CHUNKS)
S_RET = S_FFN0 + S_FFN
HEAD_USES = 8
S_RET_OUT = S_RET + HEAD_USES * HEADS
S_FFN1 = S_RET_OUT + KT
S_OUT = S_FFN1 + S_FFN

ADA_B = 0
NORM1, NORM2 = 96, 112
PW1_B, DW_B, LN_G, LN_B, PW2_B, FFN_DW_B, FINAL_G, C_COL = 128, 144, 152, 160, 168, 176, 220, 228
DW_W = 256
FFN_DW_W = 512
GROUP = 4
PE_TAPS = 9
DVE_TAPS = TAPS - PE_TAPS


def backbone(nc, x, c, ctx_tok, c_ctx, ada_w, ada_b, norm1_g, norm2_g, pw1_w, pw1_b, dw_w, dw_b, ln_g, ln_b,
             pw2_w, pw2_b, ret_w_in, ret_w_out, decay_f, decay_b, gn_f, gn_b, ffn_w_in, ffn_dw_w, ffn_dw_b,
             ffn_w_out, final_g, eye, ages, tri_low, tri_up, rope_row, rope_col, token_cols, out):
    with ExitStack() as stack:
        def sb(name, shape, dt=F32, where=stack):
            return where.enter_context(nc.sbuf_tensor(name, shape, dt))

        def sem(name):
            return stack.enter_context(nc.semaphore(name))

        X = sb("X", [P, KT, TOK])
        H_hi = sb("H_hi", [P, KT, TOK], F32R)
        H_lo = sb("H_lo", [P, KT, TOK], F32R)
        w_raw = sb("w_raw", [P, RING, KT * P])
        w_hi = sb("w_hi", [P, RING, KT * P], F32R)
        w_lo = sb("w_lo", [P, RING, KT * P], F32R)
        rstd = sb("rstd", [P, TOK])
        sq = sb("sq", [P, 2, TOK])
        tmp = sb("tmp", [P, 2, TOK])
        par = sb("par", [P, 768])
        ident = sb("ident", [P, P])
        mean_of = sb("mean_of", [P, P])
        eps = sb("eps", [P, 2])
        silu_c = sb("silu_c", [P, KT, 32])
        mod = sb("mod", [P, DEPTH, 48, 2])
        gain = sb("gain", [P, DEPTH, 2, KT, 2])
        pw2_gb = sb("pw2_gb", [P, KT, 2])
        decay_log = sb("decay_log", [P, 2 * HEADS])
        lgam = sb("lgam", [P, 2 * HEADS])
        ngam = sb("ngam", [P, 2 * HEADS])
        lgam512 = sb("lgam512", [P, 2 * HEADS])
        rrow = sb("rrow", [P, 2, ROWS])
        rcol = sb("rcol", [P, 2, GRID_W])
        tcol = sb("tcol", [P, 6])
        zeta = sb("zeta", [P, HEADS, 2, CT])
        with ExitStack() as ph:
            conv = sb("conv", [P, KT, OUTW + 1], F32, ph)
            ada = sb("ada", [P, 2, KT // 2, GROUP * P], F32, ph)
            diag_hi = sb("diag_hi", [P, 2, PE_TAPS, P], F32R, ph)
            diag_lo = sb("diag_lo", [P, 2, PE_TAPS, P], F32R, ph)
            tap_hi = sb("tap_hi", [P, PE_TAPS * KT], F32R, ph)
            tap_lo = sb("tap_lo", [P, PE_TAPS * KT], F32, ph)
            u_hi = sb("u_hi", [P, PADW], F32R, ph)
            u_lo = sb("u_lo", [P, PADW], F32R, ph)
        with ExitStack() as ph:
            mid_hi = sb("mid_hi", [P, 8, TOK], F32R, ph)
            mid_lo = sb("mid_lo", [P, 8, TOK], F32R, ph)
            m32 = sb("m32", [P, 2, TOK], F32, ph)
        with ExitStack() as ph:
            y_hi = sb("y_hi", [P, KT, LAT], F32R, ph)
            y_lo = sb("y_lo", [P, KT, LAT], F32R, ph)
            qT = sb("qT", [P, 2, LAT], F32, ph)
            kT = sb("kT", [P, 2, LAT], F32, ph)
            V = sb("V", [P, LT, DH], F32, ph)
            scores = sb("scores", [P, 2, 10 * P], F32, ph)
            state = sb("state", [P, 2, 2, DH], F32, ph)
            decay = sb("decay", [P, 2, LAT], F32, ph)
            iota = sb("iota", [P, LAT], F32, ph)
            tlow = sb("tlow", [P, P], F32, ph)
            tup = sb("tup", [P, P], F32, ph)
            gn_st = sb("gn_st", [P, LT, 6], F32, ph)
            gn_mv = sb("gn_mv", [P, LT, 2], F32, ph)
        y_tok = qT[:].rearrange("p f t -> p (f t)").rearrange("p (t v) -> p t v", t=LT)
        flat_tmp, flat_sq = (a[:].rearrange("p a b -> p (a b)") for a in (tmp, sq))
        upad = [flat_tmp[:, 0:PADW], flat_sq[:, 0:PADW]]
        ada_row = flat_tmp[:, 2 * TOK - GROUP * P:]
        norm_buf = [tmp[:, 0], tmp[:, 1], sq[:, 0], sq[:, 1]]
        q_dec = tmp[:, 0:2, :].rearrange("p a b -> p (a b)")[:, 0:2 * LAT].rearrange("p (a b) -> p a b", a=2)
        rot = tmp[:, 0:2, :].rearrange("p a b -> p (a b)")[:, 2 * LAT:3 * LAT]
        cosd = rstd[:, 0:LAT]
        gate = sq[:, 0:2, :].rearrange("p a b -> p (a b)")[:, 0:LT * DH].rearrange("p (a b) -> p a b", a=LT)
        gn_row = sq[:, 0:2, :].rearrange("p a b -> p (a b)")[:, LT * DH:LT * DH + 2 * DH].rearrange(
            "p (a b) -> p a b", a=2)
        kctx = scores[:, 0, 0:4 * DH].rearrange("p (d t v) -> p d t v", d=2, t=CT)
        vctx = scores[:, 1, 0:2 * DH].rearrange("p (t v) -> p t v", t=CT)
        xin = conv[:, :, :].rearrange("p a b -> p (a b)")[:, 0:6 * D].rearrange("p (t d) -> p t d", t=6)
        prow = tmp[:, :, :].rearrange("p a b -> p (a b)")[:, 0:768].rearrange("p (a b) -> p a b", b=P)
        otok = conv[:, :, :].rearrange("p a b -> p (a b)")[:, 0:LT * D].rearrange("p (t d) -> p t d", t=LT)

        ps = stack.enter_context(nc.psum_tensor("ps", [P, 8, 512], F32))

        raw_ready = [sem(f"raw_ready{r}") for r in range(RING)]
        hi_ready = sem("hi_ready")
        lo_ready = sem("lo_ready")
        unit_done = sem("unit_done")
        slot_read = [sem("slot_read0"), sem("slot_read1")]
        par_rows = sem("par_rows")
        consts_in = sem("consts_in")
        eye_in = sem("eye_in")
        ages_in = sem("ages_in")
        tokens_in = sem("tokens_in")
        filled = sem("filled")
        par_T = sem("par_T")
        par_ready = sem("par_ready")
        silu_c_ready = sem("silu_c_ready")
        ada_in = [sem("ada_in0"), sem("ada_in1")]
        ada_done = sem("ada_done")
        ada_row_ready = sem("ada_row_ready")
        ada_T = sem("ada_T")
        mod_sum = sem("mod_sum")
        mod_ready = sem("mod_ready")
        xT_done = sem("xT_done")
        sq_ready = sem("sq_ready")
        ssq_ready = sem("ssq_ready")
        sq_summed = sem("sq_summed")
        modulated = sem("modulated")
        taps_split = sem("taps_split")
        padded = sem("padded")
        diag_ready = sem("diag_ready")
        u_hi_ready = sem("u_hi_ready")
        u_lo_ready = sem("u_lo_ready")
        conv_done = sem("conv_done")
        std_ready = sem("std_ready")
        rstd_ready = sem("rstd_ready")
        scaled = sem("scaled")
        h_hi_ready = sem("h_hi_ready")
        h_lo_ready = sem("h_lo_ready")
        sig_ready = sem("sig_ready")
        tap_done = sem("tap_done")
        mu_summed = sem("mu_summed")
        centered = sem("centered")
        ln_scaled = sem("ln_scaled")
        ln_silu = sem("ln_silu")
        x_updated = sem("x_updated")
        g_first = sem("g_first")
        g_taps = sem("g_taps")
        g_silu = sem("g_silu")
        mid_hi_ready = sem("mid_hi_ready")
        mid_lo_ready = sem("mid_lo_ready")
        lg_step = sem("lg_step")
        zeta_ready = sem("zeta_ready")
        gn_in = sem("gn_in")
        rot_step = sem("rot_step")
        age_ready = sem("age_ready")
        decay_exp = sem("decay_exp")
        decay_ready = sem("decay_ready")
        score_done = sem("score_done")
        score_read = sem("score_read")
        qdec_ready = sem("qdec_ready")
        gn_stats = sem("gn_stats")
        gn_var = sem("gn_var")
        gn_std = sem("gn_std")
        gn_rstd = sem("gn_rstd")
        gate_ready = sem("gate_ready")
        y_step = sem("y_step")
        yT_done = sem("yT_done")
        y_hi_ready = sem("y_hi_ready")
        y_lo_ready = sem("y_lo_ready")
        fin_ready = sem("fin_ready")
        stored = sem("stored")

        LATS, CTXS = slice(0, LAT), slice(LAT, TOK)

        def groups(both):
            return [(0, LATS), (1, CTXS)] if both else [(0, LATS)]

        def flat(ap):
            return ap.rearrange("p a b -> p (a b)")

        def taps_at(layer):
            return 4 * FT * layer

        block = stack.enter_context(nc.Block())

        @block.sync
        def _(sp):
            for n, (lo, rows, src) in enumerate([
                    (0, 96, ada_b.rearrange("l (t p) -> (l t) p", p=P)),
                    (NORM1, 16, norm1_g.rearrange("l (t p) -> (l t) p", p=P)),
                    (NORM2, 16, norm2_g.rearrange("l (t p) -> (l t) p", p=P)),
                    (PW1_B, 16, pw1_b.rearrange("l (t p) -> (l t) p", p=P)),
                    (DW_B, 8, dw_b.rearrange("l (t p) -> (l t) p", p=P)),
                    (LN_G, 8, ln_g.rearrange("l (t p) -> (l t) p", p=P)),
                    (LN_B, 8, ln_b.rearrange("l (t p) -> (l t) p", p=P)),
                    (PW2_B, 8, pw2_b.rearrange("l (t p) -> (l t) p", p=P)),
                    (FFN_DW_B, 44, ffn_dw_b.rearrange("l (t p) -> (l t) p", p=P)),
                    (FINAL_G, 8, final_g.rearrange("(t p) -> t p", p=P)),
                    (C_COL, 8, c.rearrange("b (t p) -> (b t) p", p=P)),
                    (C_COL + 8, 8, c_ctx.rearrange("(t p) -> t p", p=P)),
                    (DW_W, 128, dw_w[0].rearrange("k (t p) -> (k t) p", p=P)[0:128]),
                    (DW_W + 128, 120, dw_w[0].rearrange("k (t p) -> (k t) p", p=P)[128:248]),
                    (FFN_DW_W, 66, ffn_dw_w[0].rearrange("k (t p) -> (k t) p", p=P)),
                    (FFN_DW_W + 128, 66, ffn_dw_w[1].rearrange("k (t p) -> (k t) p", p=P))]):
                r0 = lo % P
                sp.dma_start(prow[r0:r0 + rows, lo // P, :], src).then_inc(par_rows, 16)
                if n == 0:
                    sp.dma_start(ident[:], eye).then_inc(eye_in, 16)
            for dst, src in ((rrow[:], rope_row), (rcol[:], rope_col), (tcol[:], token_cols),
                             (decay_log[:, 0:HEADS], decay_f.to_broadcast([P, HEADS])),
                             (decay_log[:, HEADS:], decay_b.to_broadcast([P, HEADS]))):
                sp.dma_start(dst, src).then_inc(consts_in, 16)

            def load(unit, r, src):
                if not (isinstance(unit, int) and unit < RING):
                    sp.wait_ge(lo_ready, unit - (RING - 1))
                k = src.shape[0] // P
                sp.dma_start(w_raw[:, r, 0:k * P].rearrange("p (k n) -> p k n", n=P),
                             src.rearrange("(k p) n -> p k n", p=P)).then_inc(raw_ready[r], 16)

            def load_pairs(first, w, half, n):
                def body(i):
                    for q in range(2):
                        for h in range(2):
                            load(2 * first + 4 * i + 2 * q + h, 2 * q + h,
                                 w[:, ds(i * (2 * P) + (q * P + h * half), P)])
                if first == PW1:
                    body(0)
                with sp.Fori(1 if first == PW1 else 0, n // 2) as i:
                    body(i)

            def load_cols(first, w, n):
                with sp.Fori(0, n // 2) as i:
                    for u in range(4):
                        load(2 * first + 4 * i + u, u, w[:, ds(i * (4 * P) + u * P, P)])

            def load_ffn(first, layer):
                w_in, w_out = ffn_w_in[layer], ffn_w_out[layer]
                f = 0
                for n in CHUNKS:
                    load_pairs(first, w_in[:, f * P:], F, n)
                    load_cols(first + n, w_out[f * P:(f + n) * P, :], 4)
                    first += n + 4
                    f += n

            load_pairs(PW1, pw1_w[0], D, KT)
            load_cols(PW2, pw2_w[0], KT // 2)
            load_ffn(FFN0, 0)
            for h in range(HEADS):
                for part in range(5):
                    for u in range(2):
                        unit = 2 * (RET + 5 * h + part) + u
                        load(unit, unit % RING, ret_w_in[0][:, part * D + h * DH + u * P:part * D + h * DH + (u + 1) * P])
            load_cols(RET_OUT, ret_w_out[0], KT // 2)
            load_ffn(FFN1, 1)
            for n in range(KT // 2):
                sp.wait_ge(slot_read[1], S_OUT // 2 + n + 1)
                cols = slice(2 * n * P, 2 * (n + 1) * P)
                sp.dma_start(out[0].rearrange("(t p) d -> p t d", p=P)[:, :, cols], otok[:, :, cols]) \
                    .then_inc(stored, 16)
            sp.wait_ge(stored, 16 * (KT // 2))

        @block.gpsimd
        def _(pool):
            nc.gpsimd.memset(mean_of[:], 1.0 / D).then_inc(filled, 1)
            nc.gpsimd.memset(eps[:, 0:1], NORM_EPS).then_inc(filled, 1)
            nc.gpsimd.memset(eps[:, 1:2], GN_EPS).then_inc(filled, 1)
            nc.gpsimd.memset(silu_c[:], 0.0).then_inc(filled, 1)

            def load_group(layer, col, done):
                for half in range(2):
                    if done is not None:
                        pool.wait_ge(ada_done, done + half)
                    rows = slice(half * D // 2, (half + 1) * D // 2)
                    pool.dma_start(ada[:, half], ada_w[layer][rows, ds(col, GROUP * P)]
                                   .rearrange("(k p) n -> p k n", p=P)).then_inc(ada_in[half], 16)
            load_group(0, 0, None)
            with pool.Fori(1, 4) as i:
                load_group(0, i * (GROUP * P), 2 * i - 1)
            with pool.Fori(0, KT) as i:
                load_group(0, i * (GROUP * P) + 4 * GROUP * P, 4 * i + 7)
                load_group(1, i * (GROUP * P), 4 * i + 9)
            with pool.Fori(0, 4) as i:
                load_group(1, i * (GROUP * P) + KT * GROUP * P, 2 * i + 39)
            for h in range(HEADS):
                if h == 0:
                    pool.wait_ge(h_lo_ready, 4 * KT)
                    for dst, src in ((iota, ages), (tlow, tri_low), (tup, tri_up)):
                        pool.dma_start(dst[:], src).then_inc(ages_in, 16)
                else:
                    pool.wait_ge(y_step, 3 * h)
                for n, g in enumerate((gn_f, gn_b)):
                    pool.dma_start(gn_row[:, n, :], g[:, h * DH:(h + 1) * DH].to_broadcast([P, DH])) \
                        .then_inc(gn_in, 16)

        @block.tensor
        def _(pe):
            def mm(o, a, b, first, last):
                return nc.tensor.matmul(o, a, b, start=first, stop=last, skip_group_check=True)

            def slot_free(s, half):
                p = s % 2
                if half is None:
                    half = s // 2
                if not (isinstance(half, int) and half < 1):
                    pe.wait_ge(slot_read[p], half)

            def unit_product(unit, r, kt, src, streams, ready=None):
                s_hi, s_lo = src
                pe.wait_ge(lo_ready, unit + 1)
                for k in range(kt):
                    if ready is not None:
                        pe.wait_ge(ready[0], ready[1] + (k + 1))
                    a_hi, a_lo = w_hi[:, r, k * P:(k + 1) * P], w_lo[:, r, k * P:(k + 1) * P]
                    for a, b in ((a_hi, s_hi), (a_hi, s_lo), (a_lo, s_hi)):
                        for o, toks in streams:
                            m = mm(o, a, b[:, k, toks], k == 0 and a is a_hi and b is s_hi, k == kt - 1 and a is a_lo)
                m.then_inc(unit_done, 1)

            def slot(p, bank):
                return ps[:, 3 * p + bank, :]

            def pair_block(blk, q, s, half, src, both, ready):
                slot_free(s, half)
                for h in range(2):
                    streams = [(slot(s % 2, h), LATS)]
                    if both:
                        streams.append((slot(s % 2, 2)[:, h * CTX:(h + 1) * CTX], CTXS))
                    unit_product(2 * blk + h, 2 * q + h, KT, src, streams, ready)

            def sum_squares(st, both):
                pe.wait_ge(ssq_ready, 7 * (st + 1))
                if st:
                    pe.wait_ge(std_ready, st)
                m = mm(ps[:, 6, :], mean_of[:], rstd[:, LATS], True, True)
                if both:
                    m = mm(ps[:, 7, 0:CTX], mean_of[:], rstd[:, CTXS], True, True)
                m.then_inc(sq_summed, 1)

            def out_phase(blk, s, kt, src, both, ready, norm=None):
                if norm is None:
                    loop = pe.Fori(0, 2)
                    with loop as i:
                        for u in range(4):
                            slot_free(s + u, s // 2 + 2 * i + u // 2)
                            streams = [(slot((s + u) % 2, 0), LATS)] + \
                                ([(slot((s + u) % 2, 2)[:, 0:CTX], CTXS)] if both else [])
                            unit_product(2 * blk + 4 * i + u, u, kt, src, streams, ready)
                    return
                for u in range(KT):
                    slot_free(s + u, None)
                    streams = [(slot((s + u) % 2, 0), LATS)] + \
                        ([(slot((s + u) % 2, 2)[:, 0:CTX], CTXS)] if both else [])
                    unit_product(2 * blk + u, u % RING, kt, src, streams, ready)
                sum_squares(norm, both)

            def ada_products(m):
                if not isinstance(m, int) or m:
                    pe.wait_ge(ada_row_ready, m)
                for half in range(2):
                    pe.wait_ge(ada_in[half], 16 * m + 16)
                    for k in range(KT // 2):
                        o = mm(ps[32 * k:32 * k + 32, 6, :], silu_c[:, half * (KT // 2) + k, :], ada[:, half, k, :],
                               half == 0, half == 1)
                    o.then_inc(ada_done, 1)

            def ada_transposes(m):
                pe.wait_ge(ada_row_ready, m + 1)
                if not isinstance(m, int) or m:
                    pe.wait_ge(mod_sum, m)
                for t in range(GROUP):
                    o = nc.tensor.transpose(ps[:, 7, t * P:(t + 1) * P], ada_row[:, t * P:(t + 1) * P], ident[:])
                o.then_inc(ada_T, 1)

            pe.wait_ge(eye_in, 16)
            pe.wait_ge(par_rows, 16 * 16)
            for j, rows in enumerate((128, 116, 128, 120, 66, 66)):
                m = nc.tensor.transpose(ps[:, 6 + j // 4, (j % 4) * P:(j % 4) * P + rows], prow[0:rows, j, :],
                                        ident[0:rows, 0:rows])
            m.then_inc(par_T, 1)
            pe.wait_ge(tokens_in, 16 * (LT + CT))
            pe.wait_ge(filled, 4)
            pe.wait_ge(silu_c_ready, 2)
            for j in range(KT):
                s = S_XT + j
                slot_free(s, None)
                for t in range(LT + CT):
                    o = slot(s % 2, 0)[:, t * P:(t + 1) * P] if t < LT else slot(s % 2, 2)[:, (t - LT) * P:(t - LT + 1) * P]
                    m = nc.tensor.transpose(o, xin[:, t, j * P:(j + 1) * P], ident[:])
                m.then_inc(xT_done, 1)
                if j % 2 and j < 7:
                    if j >= 3:
                        ada_transposes(j // 2 - 1)
                    ada_products(j // 2)
            ada_transposes(2)
            pe.wait_ge(mod_sum, 3)
            sum_squares(0, True)
            pe.wait_ge(std_ready, 1)
            ada_products(3)
            ada_transposes(3)

            def conv_taps(b, p):
                n = b + S_PW1 // 2
                pe.wait_ge(slot_read[1], n)
                pe.wait_ge(diag_ready, b + 1)
                pe.wait_ge(u_lo_ready, b + 1)
                for k in range(PE_TAPS):
                    for a, u in ((diag_hi, u_hi), (diag_hi, u_lo), (diag_lo, u_hi)):
                        first, last = k == 0 and a is diag_hi and u is u_hi, k == PE_TAPS - 1 and a is diag_lo
                        mm(slot(1, 0), a[:, p, k, :], u[:, k:k + LAT], first, last)
                        m = mm(slot(1, 2)[:, 0:CTX], a[:, p, k, :], u[:, CTX_OUT + k:OUTW + k], first, last)
                m.then_inc(conv_done, 1)

            def pw1_body(i):
                for q in range(2):
                    b = 2 * i + q
                    pe.wait_ge(slot_read[0], b + S_PW1 // 2)
                    for h in range(2):
                        unit_product(4 * i + (2 * q + h), 2 * q + h, KT, (H_hi, H_lo),
                                     [(slot(0, h), LATS), (slot(0, 2)[:, h * CTX:(h + 1) * CTX], CTXS)], (h_lo_ready, 0))
                        if h == 0:
                            ada_products(4 * i + (2 * q + 4))
                    ada_transposes(4 * i + (2 * q + 4))
                    ada_products(4 * i + (2 * q + 5))
                    if not (isinstance(i, int) and b == 0):
                        conv_taps(2 * i + (q - 1), 1 - q)
                    ada_transposes(4 * i + (2 * q + 5))
            pw1_body(0)
            with pe.Fori(1, KT // 2) as i:
                pw1_body(i)
            for m in range(20, 24):
                ada_products(m)
                if m == 21:
                    conv_taps(KT - 1, 1)
                ada_transposes(m)
            slot_free(S_LN, None)
            for j in range(KT):
                pe.wait_ge(slot_read[1], S_PW1 // 2 + j + 1)
                mm(slot(0, 0), mean_of[:], conv[:, j, 0:LAT], j == 0, j == KT - 1)
                m = mm(slot(1, 0)[:, 0:CTX], mean_of[:], conv[:, j, CTX_OUT:OUTW], j == 0, j == KT - 1)
            m.then_inc(mu_summed, 1)
            pe.wait_ge(mod_sum, 24)
            sum_squares(1, True)
            out_phase(PW2, S_PW2, KT, (H_hi, H_lo), True, (h_lo_ready, KT), norm=2)

            def ffn(blk, s, layer, both):
                h_at = 2 * KT + 2 * KT * layer
                mid_at = layer * FT
                for c_no, n in enumerate(CHUNKS):
                    with pe.Fori(0, n // 2) as i:
                        for q in range(2):
                            pair_block(blk + 2 * i + q, q, s + q, s // 2 + i, (H_hi, H_lo), both, (h_lo_ready, h_at))
                    blk, s = blk + n, s + n
                    last = c_no == len(CHUNKS) - 1
                    out_phase(blk, s, n, (mid_hi, mid_lo), both, (mid_lo_ready, mid_at),
                              norm=3 + 2 * layer if last else None)
                    mid_at += n
                    blk, s = blk + 4, s + KT

            ffn(FFN0, S_FFN0, 0, True)

            H2 = (H_hi, H_lo)
            pe.wait_ge(std_ready, 4)

            def token_major(blk, streams):
                u0 = 2 * blk % RING
                pe.wait_ge(lo_ready, 2 * blk + 2)
                for o, t0 in streams:
                    for k in range(KT):
                        b_hi, b_lo = (w[:, u0:u0 + 2, k * P:(k + 1) * P] for w in (w_hi, w_lo))
                        a_hi, a_lo = (a[:, k, t0:t0 + P] for a in H2)
                        mm(o, a_hi, b_hi, k == 0, False)
                        mm(o, a_hi, b_lo, False, False)
                        m = mm(o, a_lo, b_hi, False, k == KT - 1)
                return m

            def toks4(p):
                return [(ps[:, 3 * p + t // 2, (t % 2) * DH:(t % 2 + 1) * DH], t * P) for t in range(LT)]

            def toks2(p):
                return [(ps[:, 3 * p + 2, t * DH:(t + 1) * DH], LAT + t * P) for t in range(CT)]

            def transposes(h):
                pe.wait_ge(y_step, 3 * (h + 1))
                for f in range(2):
                    for t in range(LT):
                        m = nc.tensor.transpose(ps[:, 6 + f, t * P:(t + 1) * P], y_tok[:, t, f * P:(f + 1) * P], ident[:])
                m.then_inc(yT_done, 1)

            h_at = 3 * KT
            for h in range(HEADS):
                blk, s = RET + 5 * h, S_RET + HEAD_USES * h
                slot_free(s, None)
                for u in range(2):
                    unit_product(2 * blk + u, (2 * blk + u) % RING, KT, H2, [(slot(0, u), LATS)], (h_lo_ready, h_at))
                if h:
                    transposes(h - 1)
                blk += 1
                slot_free(s + 1, None)
                pe.wait_ge(lo_ready, 2 * blk + 2)
                token_major(blk, toks2(1))
                for u in range(2):
                    unit_product(2 * blk + u, (2 * blk + u) % RING, KT, H2, [(slot(1, u), LATS)])
                blk += 1
                slot_free(s + 2, None)
                token_major(blk, toks4(0) + toks2(0)).then_inc(unit_done, 2)
                slot_free(s + 3, None)
                pe.wait_ge(slot_read[0], (s + 2) // 2 + 1)
                for d in range(2):
                    for f in range(2):
                        for t in range(CT):
                            m = mm(ps[:, 3 + d, f * DH:(f + 1) * DH], kctx[:, d, t, f * P:(f + 1) * P], vctx[:, t, :],
                                   t == 0, t == CT - 1)
                m.then_inc(score_done, 1)
                pe.wait_ge(rot_step, 15 * h + 15)
                for j in range(LT):
                    n = h * LT + j
                    if n >= 2:
                        pe.wait_ge(score_read, n - 1)
                    if j < 2 and h >= 1:
                        pe.wait_ge(y_lo_ready, 2 * h)
                    for f in range(2):
                        m = mm(ps[:, 6 + j % 2, :], kT[:, f, j * P:(j + 1) * P], qT[:, f, :], f == 0, f == 1)
                    m.then_inc(score_done, 1)
                for d in range(2):
                    blk += 1
                    slot_free(s + 4 + 2 * d, None)
                    token_major(blk, toks4(0)).then_inc(unit_done, 2)
                    slot_free(s + 5 + 2 * d, None)
                    pe.wait_ge(score_read, (h + 1) * LT)
                    pe.wait_ge(qdec_ready, 2 * h + d + 1)
                    for i in range(LT):
                        o = ps[:, 3 + i // 2, (i % 2) * DH:(i % 2 + 1) * DH]
                        js = range(0, i + 1) if d == 0 else range(i, LT)
                        for n, j in enumerate(js):
                            at = sum((LT - a) if d == 0 else (a + 1) for a in range(j)) + (i - j if d == 0 else i)
                            mm(o, scores[:, d, at * P:(at + 1) * P], V[:, j, :], n == 0, False)
                        for f in range(2):
                            m = mm(o, (q_dec if d == 0 else kT)[:, f, i * P:(i + 1) * P], state[:, d, f, :], False, f == 1)
                    m.then_inc(score_done, 1)
            transposes(HEADS - 1)
            pe.wait_ge(y_lo_ready, 2 * HEADS)
            out_phase(RET_OUT, S_RET_OUT, KT, (y_hi, y_lo), False, None, norm=4)
            ffn(FFN1, S_FFN1, 1, False)
            for j in range(KT):
                s = S_OUT + j
                slot_free(s, None)
                pe.wait_ge(fin_ready, j + 1)
                for t in range(LT):
                    m = nc.tensor.transpose(slot(s % 2, 0)[:, t * P:(t + 1) * P], tmp[:, j % 2, t * P:(t + 1) * P],
                                            ident[:])
                m.then_inc(xT_done, 1)

        @block.scalar
        def _(act):
            A = nc.scalar.activation

            def split_hi(unit, r):
                if isinstance(unit, int):
                    if unit >= UNITS:
                        return
                    act.wait_ge(raw_ready[r], 16 * (unit // RING + 1))
                    if unit >= RING:
                        act.wait_ge(unit_done, unit - (RING - 1))
                A(w_hi[:, r, :], w_raw[:, r, :], ACT.Copy).then_inc(hi_ready, 1)

            def split_hi_at(base, i, off):
                unit = base + off
                if isinstance(i, int):
                    return split_hi(unit + 4 * i, unit % RING)
                act.wait_ge(raw_ready[unit % RING], 16 * i + 16 * (unit // RING + 1))
                act.wait_ge(unit_done, 4 * i + (unit - (RING - 1)))
                A(w_hi[:, unit % RING, :], w_raw[:, unit % RING, :], ACT.Copy).then_inc(hi_ready, 1)

            def bank(p, b):
                return ps[:, 3 * p + b, :]

            def square(st, j, both, wait, val, src=None):
                act.wait_ge(wait, val)
                if j >= 3:
                    act.wait_ge(ssq_ready, 7 * st + j - 2)
                dst = rstd if j == 0 else sq[:, j % 2]
                if src is None:
                    w = TOK if both else LAT
                    a = A(dst[:, 0:w], X[:, j, 0:w], ACT.Square)
                else:
                    A(dst[:, LATS], src[0], ACT.Square)
                    a = A(dst[:, CTXS], src[1], ACT.Square)
                a.then_inc(sq_ready, 1)

            def root(st, both):
                act.wait_ge(sq_summed, st + 1)
                a = A(rstd[:, LATS], ps[:, 6, :], ACT.Sqrt, bias=eps[:, 0:1])
                if both:
                    a = A(rstd[:, CTXS], ps[:, 7, 0:CTX], ACT.Sqrt, bias=eps[:, 0:1])
                a.then_inc(std_ready, 1)

            def affine_hi(n_at, one, w=TOK):
                def first(j):
                    act.wait_ge(scaled, n_at + j + 1)
                    one(j, norm_buf[j % 4]).then_inc(modulated, 1)
                first(0)
                for j in range(KT):
                    if j + 1 < KT:
                        first(j + 1)
                    act.wait_ge(modulated, n_at + j + 1)
                    A(H_hi[:, j, 0:w], norm_buf[j % 4][:, 0:w], ACT.Copy).then_inc(h_hi_ready, 1)

            def modulate(layer, sub, both):
                def one(j, b):
                    for m, toks in groups(both):
                        a = A(b[:, toks], b[:, toks], ACT.Identity, scale=gain[:, layer, sub, j, m:m + 1],
                              bias=mod[:, layer, 24 * sub + j, m:m + 1])
                    return a
                return one

            def ada_copy(m):
                act.wait_ge(ada_done, 2 * m + 2)
                if not isinstance(m, int) or m:
                    act.wait_ge(ada_T, m)
                A(ada_row, ps[:, 6, :], ACT.Copy).then_inc(ada_row_ready, 1)

            for t in range(LT):
                act.dma_start(xin[:, t, :], x[0, t * P:(t + 1) * P, :]).then_inc(tokens_in, 16)
            for t in range(CT):
                act.dma_start(xin[:, LT + t, :], ctx_tok[0, t * P:(t + 1) * P, :]).then_inc(tokens_in, 16)
            act.wait_ge(filled, 4)
            act.wait_ge(par_ready, 1)
            for v in range(2):
                A(silu_c[:, :, v], par[:, C_COL + 8 * v:C_COL + 8 * v + 8], ACT.Silu).then_inc(silu_c_ready, 1)
            for u in range(3):
                split_hi(u, u)
            for j in range(KT):
                square(0, j, True, slot_read[j % 2], j // 2 + 1)
                if j % 2 and j < 7:
                    ada_copy(j // 2)
            root(0, True)
            ada_copy(3)
            A(tap_hi[:], par[:, DW_W:DW_W + PE_TAPS * KT], ACT.Copy).then_inc(taps_split, 1)
            affine_hi(0, modulate(0, 0, True))
            act.wait_ge(taps_split, 2)
            act.wait_ge(h_lo_ready, KT)

            def pw1_body(i):
                for q in range(2):
                    split_hi_at(2 * PW1, i, 2 * q + 3)
                    ada_copy(4 * i + (2 * q + 4))
                    split_hi_at(2 * PW1, i, 2 * q + 4)
                    act.wait_ge(unit_done, 4 * i + (2 * q + 2))
                    b = par[:, ds(2 * i + (PW1_B + KT + q), 1)]
                    A(rstd[:, LATS], bank(0, 1), ACT.Sigmoid, bias=b)
                    A(rstd[:, CTXS], bank(0, 2)[:, CTX:], ACT.Sigmoid, bias=b).then_inc(sig_ready, 1)
                    ada_copy(4 * i + (2 * q + 5))
                    for k in range(PE_TAPS):
                        A(diag_hi[:, q, k, :], ident[:], ACT.Copy, scale=tap_hi[:, ds(2 * i + (KT * k + q), 1)].bitcast(F32))
                        a = A(diag_lo[:, q, k, :], ident[:], ACT.Copy, scale=tap_lo[:, ds(2 * i + (KT * k + q), 1)])
                    a.then_inc(diag_ready, 1)
                    act.wait_ge(slot_read[0], 2 * i + (S_PW1 // 2 + q + 1))
                    if not (isinstance(i, int) and q == 0):
                        act.wait_ge(conv_done, 2 * i + q)
                    A(u_hi[:], upad[q], ACT.Copy).then_inc(u_hi_ready, 1)
            pw1_body(0)
            with act.Fori(1, KT // 2) as i:
                pw1_body(i)
            for m in range(20, 24):
                ada_copy(m)
            for j in range(KT):
                if j == KT - 1:
                    act.wait_ge(slot_read[0], S_LN // 2 + 1)
                square(1, j, True, centered if j < KT - 1 else slot_read[1], 2 * j + 2 if j < KT - 1 else S_LN // 2 + 1,
                       (conv[:, j, 0:LAT], conv[:, j, CTX_OUT:OUTW]))
            root(1, True)
            affine_hi(KT, lambda j, b: A(b, b, ACT.Silu, scale=par[:, LN_G + j:LN_G + j + 1],
                                         bias=par[:, LN_B + j:LN_B + j + 1]))

            def gated(p, both, gates, bias=None):
                for m, toks in groups(both):
                    a = A(tmp[:, p, toks], bank(p, 0) if m == 0 else bank(p, 2)[:, 0:CTX], ACT.Identity,
                          scale=gates[m], bias=0.0 if bias is None else bias[m])
                a.then_inc(slot_read[p], 1)

            def out_phase(blk, s, x_at, both, layer, gate_at):
                with act.Fori(0, 2) as i:
                    for u in range(4):
                        p = u % 2
                        split_hi_at(2 * blk, i, u + 3)
                        act.wait_ge(unit_done, 4 * i + (2 * blk + u + 1))
                        act.wait_ge(x_updated, 4 * i + (x_at + u - 1))
                        g = [mod[:, layer, ds(4 * i + (gate_at + u), 1), m] for m in range(2)]
                        gated(p, both, g)

            def out_phase_norm(blk, s, x_at, both, layer, gate_at, norm, bias=False):
                for u in range(KT):
                    p = u % 2
                    split_hi(2 * blk + u + 3, (u + 3) % RING)
                    act.wait_ge(unit_done, 2 * blk + u + 1)
                    if x_at + u - 1 > 0:
                        act.wait_ge(x_updated, x_at + u - 1)
                    g = [mod[:, layer, gate_at + u, m:m + 1] for m in range(2)]
                    gated(p, both, g, [pw2_gb[:, u, m:m + 1] for m in range(2)] if bias else None)
                    square(norm, u, both, x_updated, x_at + u + 1)
                root(norm, both)

            act.wait_ge(mod_ready, 6)
            out_phase_norm(PW2, S_PW2, 0, True, 0, 16, 2, bias=True)

            def ffn(blk, s, layer, both, x_at):
                f = 0
                for c_no, n in enumerate(CHUNKS):
                    act.wait_ge(x_updated, x_at)
                    with act.Fori(0, n // 2) as i:
                        for q in range(2):
                            g_at = layer * FT + f + q
                            split_hi_at(2 * blk, i, 2 * q + 3)
                            split_hi_at(2 * blk, i, 2 * q + 4)
                            act.wait_ge(unit_done, 4 * i + (2 * blk + 2 * q + 2))
                            w1 = par[:, ds(2 * i + (FFN_DW_W + layer * P + FT + f + q), 1)]
                            b = par[:, ds(2 * i + (FFN_DW_B + g_at), 1)]
                            a = A(tmp[:, q, LATS], bank(q, 1), ACT.Identity, scale=w1, bias=b)
                            if both:
                                a = A(tmp[:, q, CTXS], bank(q, 2)[:, CTX:], ACT.Identity, scale=w1, bias=b)
                            a.then_inc(g_first, 1)
                            w = TOK if both else LAT
                            act.wait_ge(g_taps, (8 if both else 4) * i + (taps_at(layer) + (4 if both else 2) * (f + q + 1)))
                            A(tmp[:, q, 0:w], tmp[:, q, 0:w], ACT.Silu).then_inc(g_silu, 1)
                            act.wait_ge(slot_read[q], i + (s // 2 + 1))
                            A(mid_hi[:, ds(2 * i + q, 1), 0:w], m32[:, q:q + 1, 0:w], ACT.Copy).then_inc(mid_hi_ready, 1)
                    f += n
                    blk, s = blk + n, s + n
                    if c_no < len(CHUNKS) - 1:
                        out_phase(blk, s, x_at, both, layer, 40)
                    else:
                        out_phase_norm(blk, s, x_at, both, layer, 40, 3 + 2 * layer)
                    blk, s, x_at = blk + 4, s + KT, x_at + KT

            affine_hi(2 * KT, modulate(0, 1, True))
            ffn(FFN0, S_FFN0, 0, True, KT)
            affine_hi(3 * KT, modulate(1, 0, True))

            act.wait_ge(consts_in, 16 * 5)
            A(ngam[:], decay_log[:], ACT.Exp).then_inc(lg_step, 1)
            act.wait_ge(lg_step, 2)
            for h in range(HEADS):
                for d in range(2):
                    A(zeta[:, h, d, :], tcol[:, 2 + 2 * d:4 + 2 * d], ACT.Exp,
                      scale=lgam[:, HEADS * d + h:HEADS * d + h + 1]).then_inc(zeta_ready, 1)
            def y_parts(h):
                act.wait_ge(yT_done, h + 1)
                for f in range(2):
                    A(y_hi[:, 2 * h + f, :], ps[:, 6 + f, :], ACT.Copy).then_inc(y_hi_ready, 1)

            for h in range(HEADS):
                blk, s = RET + 5 * h, S_RET + HEAD_USES * h
                ab = slice(h, h + 1), slice(HEADS + h, HEADS + h + 1)
                u = 2 * blk
                split_hi(u + 3, (u + 3) % RING)
                act.wait_ge(age_ready, 2 * h + 2)
                A(decay[:, 0, :], decay[:, 0, :], ACT.Exp, scale=lgam[:, ab[0]])
                A(decay[:, 1, :], decay[:, 1, :], ACT.Exp, scale=ngam[:, ab[1]]).then_inc(decay_exp, 1)
                split_hi(u + 4, (u + 4) % RING)
                split_hi(u + 5, (u + 5) % RING)
                if h:
                    y_parts(h - 1)
                split_hi(u + 6, (u + 6) % RING)
                act.wait_ge(unit_done, 2 * (blk + 2) + 2)
                A(V[:].rearrange("p a b -> p (a b)"), ps[:, 0:2, :].rearrange("p a b -> p (a b)"), ACT.Copy)
                A(vctx.rearrange("p a b -> p (a b)"), ps[:, 2, :], ACT.Copy).then_inc(slot_read[0], 1)
                split_hi(u + 7, (u + 7) % RING)
                split_hi(u + 8, (u + 8) % RING)
                act.wait_ge(score_done, 7 * h + 1)
                A(state[:].rearrange("p d f v -> p (d f v)"), ps[:, 3:5, :].rearrange("p a b -> p (a b)"),
                  ACT.Copy).then_inc(slot_read[1], 1)
                act.wait_ge(score_read, LT * (h + 1))
                A(decay[:, 0, :], iota[:], ACT.Exp, scale=lgam[:, ab[0]], bias=lgam[:, ab[0]])
                A(decay[:, 1, :], iota[:], ACT.Exp, scale=ngam[:, ab[1]], bias=lgam512[:, ab[1]]).then_inc(decay_exp, 1)
                for d in range(2):
                    act.wait_ge(unit_done, 2 * (blk + 3 + d) + 2)
                    if 2 * h + d >= 1:
                        act.wait_ge(y_step, 3 * h + d)
                    A(gate.rearrange("p a b -> p (a b)"), ps[:, 0:2, :].rearrange("p a b -> p (a b)"), ACT.Silu) \
                        .then_inc(slot_read[0], 1)
                    if d == 0:
                        split_hi(u + 9, (u + 9) % RING)
                        split_hi(u + 10, (u + 10) % RING)
                    else:
                        split_hi(u + 11, (u + 11) % RING)
                        split_hi(u + 12, (u + 12) % RING)
                    act.wait_ge(gn_stats, 2 * (2 * h + d) + 2)
                    A(gn_mv[:, :, 1], gn_mv[:, :, 1], ACT.Sqrt, bias=eps[:, 1:2]).then_inc(gn_std, 1)
            y_parts(HEADS - 1)
            out_phase_norm(RET_OUT, S_RET_OUT, KT * 4, False, 1, 16, 4)
            affine_hi(4 * KT, modulate(1, 1, False), LAT)
            ffn(FFN1, S_FFN1, 1, False, KT * 5)
            for j in range(KT):
                p = j % 2
                act.wait_ge(xT_done, KT + j + 1)
                a = A(otok[:, :, j * P:(j + 1) * P], bank(p, 0).rearrange("p (t n) -> p t n", t=LT), ACT.Copy)
                a.then_inc(slot_read[p], 1)

        @block.vector
        def _(dve):
            v = nc.vector

            def bank(p, b):
                return ps[:, 3 * p + b, :]

            def split_lo(unit, r):
                if isinstance(unit, int) and unit >= UNITS:
                    return
                dve.wait_ge(hi_ready, unit + 1)
                v.tensor_tensor(w_lo[:, r, :], w_raw[:, r, :], w_hi[:, r, :].bitcast(F32), ALU.subtract) \
                    .then_inc(lo_ready, 1)

            def recip(st, both):
                dve.wait_ge(std_ready, st + 1)
                w = TOK if both else LAT
                v.reciprocal(rstd[:, 0:w], rstd[:, 0:w]).then_inc(rstd_ready, 1)
                dve.wait_ge(rstd_ready, st + 1)

            def add_squares(st, j, both):
                dve.wait_ge(sq_ready, KT * st + j + 1)
                if j >= 2:
                    dve.wait_ge(ssq_ready, 7 * st + j - 1)
                w = TOK if both else LAT
                v.tensor_tensor(rstd[:, 0:w], rstd[:, 0:w], sq[:, j % 2, 0:w], ALU.add).then_inc(ssq_ready, 1)

            def normed(n_at, at, both, conv_rows=False):
                w = TOK if both else LAT

                def scale(j):
                    b = norm_buf[j % 4]
                    if j >= 4:
                        dve.wait_ge(h_lo_ready, at + j - 3)
                    if conv_rows:
                        v.tensor_tensor(b[:, LATS], conv[:, j, 0:LAT], rstd[:, LATS], ALU.mult)
                        o = v.tensor_tensor(b[:, CTXS], conv[:, j, CTX_OUT:OUTW], rstd[:, CTXS], ALU.mult)
                    else:
                        o = v.tensor_tensor(b[:, 0:w], X[:, j, 0:w], rstd[:, 0:w], ALU.mult)
                    o.then_inc(scaled, 1)
                for j in range(3):
                    scale(j)
                for j in range(KT):
                    if j + 3 < KT:
                        scale(j + 3)
                    dve.wait_ge(h_hi_ready, at + j + 1)
                    v.tensor_tensor(H_lo[:, j, 0:w], norm_buf[j % 4][:, 0:w], H_hi[:, j, 0:w].bitcast(F32),
                                    ALU.subtract).then_inc(h_lo_ready, 1)

            def two(ap):
                return ap.unsqueeze(2).to_broadcast([P, ap.shape[1], 2])

            def ada_sum(m, layer, g):
                dve.wait_ge(ada_T, m + 1)
                v.tensor_reduce(mod[:, layer, GROUP * g:GROUP * (g + 1), :],
                                ps[:, 7, :].rearrange("p (t j c) -> p t c j", j=4, c=32)[:, :, 0:2, :],
                                mybir.AxisListType.X, ALU.add).then_inc(mod_sum, 1)

            def modulation(m, layer, t0, t1, at):
                dve.wait_ge(mod_sum, m + 1)
                v.tensor_tensor(mod[:, layer, t0:t1, :], mod[:, layer, t0:t1, :],
                                two(par[:, ADA_B + 48 * layer + t0:ADA_B + 48 * layer + t1]), ALU.add) \
                    .then_inc(mod_ready, 1)
                at += 1
                dve.wait_ge(mod_ready, at)
                for sub, (col, g) in enumerate(((8, NORM1), (32, NORM2))):
                    if t0 <= col < t1:
                        v.scalar_tensor_tensor(gain[:, layer, sub], mod[:, layer, col:col + KT, :], 1.0,
                                               two(par[:, g + KT * layer:g + KT * (layer + 1)]), ALU.add, ALU.mult) \
                            .then_inc(mod_ready, 1)

            dve.wait_ge(par_T, 1)
            v.tensor_copy(par[:, 0:244], ps[:, 6, 0:244])
            v.tensor_copy(par[:, 256:504], ps[:, 6, 256:504])
            for layer in range(DEPTH):
                o = v.tensor_copy(par[:, FFN_DW_W + P * layer:FFN_DW_W + P * layer + 66],
                                  ps[:, 7, P * layer:P * layer + 66])
            o.then_inc(par_ready, 1)
            for u in range(3):
                split_lo(u, u)
            for j in range(KT):
                p = j % 2
                dve.wait_ge(xT_done, j + 1)
                v.tensor_copy(X[:, j, LATS], bank(p, 0))
                v.tensor_copy(X[:, j, CTXS], bank(p, 2)[:, 0:CTX]).then_inc(slot_read[p], 1)
                dve.wait_ge(slot_read[p], j // 2 + 1)
                if j >= 2:
                    add_squares(0, j - 1, True)
                if j == 3 or j == 5:
                    ada_sum(j // 2 - 1, 0, j // 2 - 1)
            add_squares(0, KT - 1, True)
            ada_sum(2, 0, 2)
            recip(0, True)
            dve.wait_ge(par_ready, 1)
            ada_sum(3, 0, 3)
            modulation(3, 0, 0, 16, 0)
            dve.wait_ge(taps_split, 1)
            v.tensor_tensor(tap_lo[:], par[:, DW_W:DW_W + PE_TAPS * KT], tap_hi[:].bitcast(F32), ALU.subtract) \
                .then_inc(taps_split, 1)
            normed(0, 0, True)
            dve.wait_ge(h_lo_ready, KT)
            for b in upad:
                for lo, hi in ((0, PAD), (PAD + LAT, CTX_PAD), (CTX_PAD + CTX, PADW)):
                    o = v.memset(b[:, lo:hi], 0.0)
            o.then_inc(padded, 1)

            def taps(b, ks):
                row = conv[:, b, 0:OUTW]
                for k in ks:
                    n = b * DVE_TAPS + k - PE_TAPS
                    w = par[:, DW_W + KT * k + b:DW_W + KT * k + b + 1]
                    if k == PE_TAPS:
                        o = v.tensor_scalar(row, upad[b % 2][:, k:k + OUTW], w, None, ALU.mult)
                    else:
                        dve.wait_ge(tap_done, n)
                        o = v.scalar_tensor_tensor(row, upad[b % 2][:, k:k + OUTW], w, row, ALU.mult, ALU.add)
                    o.then_inc(tap_done, 1)

            def merge(b):
                dve.wait_ge(conv_done, b + 1)
                dve.wait_ge(tap_done, DVE_TAPS * (b + 1))
                bias = par[:, DW_B + b:DW_B + b + 1]
                v.scalar_tensor_tensor(conv[:, b, 0:LAT], bank(1, 0), bias, conv[:, b, 0:LAT], ALU.add, ALU.add)
                v.scalar_tensor_tensor(conv[:, b, CTX_OUT:OUTW], bank(1, 2)[:, 0:CTX], bias, conv[:, b, CTX_OUT:OUTW],
                                       ALU.add, ALU.add).then_inc(slot_read[1], 1)

            for b in range(KT):
                split_lo(2 * b + 3, (2 * b + 3) % RING)
                split_lo(2 * b + 4, (2 * b + 4) % RING)
                dve.wait_ge(sig_ready, b + 1)
                if b == 0:
                    dve.wait_ge(padded, 1)
                if b >= 2:
                    dve.wait_ge(u_lo_ready, b - 1)
                bias = par[:, PW1_B + b:PW1_B + b + 1]
                v.scalar_tensor_tensor(upad[b % 2][:, PAD:PAD + LAT], bank(0, 0), bias, rstd[:, LATS], ALU.add, ALU.mult)
                v.scalar_tensor_tensor(upad[b % 2][:, CTX_PAD:CTX_PAD + CTX], bank(0, 2)[:, 0:CTX], bias, rstd[:, CTXS],
                                       ALU.add, ALU.mult).then_inc(slot_read[0], 1)
                dve.wait_ge(slot_read[0], S_PW1 // 2 + b + 1)
                ada_sum(4 + 2 * b, 0, 4 + b)
                taps(b, range(PE_TAPS, PE_TAPS + 11))
                if b:
                    merge(b - 1)
                dve.wait_ge(u_hi_ready, b + 1)
                v.tensor_tensor(u_lo[:], upad[b % 2], u_hi[:].bitcast(F32), ALU.subtract).then_inc(u_lo_ready, 1)
                ada_sum(5 + 2 * b, 1, b)
                if b == KT - 1:
                    ada_sum(20, 1, 8)
                taps(b, range(PE_TAPS + 11, TAPS))
            merge(KT - 1)
            for m in range(21, 24):
                ada_sum(m, 1, m - 12)
            modulation(23, 0, 16, 48, 2)
            v.tensor_tensor(pw2_gb[:], mod[:, 0, 16:24, :], two(par[:, PW2_B:PW2_B + KT]), ALU.mult)
            modulation(23, 1, 0, 48, 4)
            dve.wait_ge(mu_summed, 1)
            for j in range(KT):
                last = j == KT - 1
                v.tensor_tensor(conv[:, j, 0:LAT], conv[:, j, 0:LAT], bank(0, 0), ALU.subtract) \
                    .then_inc(slot_read[0] if last else centered, 1)
                v.tensor_tensor(conv[:, j, CTX_OUT:OUTW], conv[:, j, CTX_OUT:OUTW], bank(1, 0)[:, 0:CTX], ALU.subtract) \
                    .then_inc(slot_read[1] if last else centered, 1)
                if j >= 2:
                    add_squares(1, j - 1, True)
            add_squares(1, KT - 1, True)
            recip(1, True)
            normed(KT, KT, True, conv_rows=True)

            def residual(s, x_at, i, u, both, col):
                w = TOK if both else LAT
                p = (s + u) % 2
                if isinstance(i, int) and i == 0:
                    dve.wait_ge(slot_read[p], (s + u) // 2 + 1)
                else:
                    dve.wait_ge(slot_read[p], 2 * i + ((s + u) // 2 + 1))
                row = X[:, col, 0:w]
                if not isinstance(col, int):
                    row = row.rearrange("p a b -> p (a b)")
                v.tensor_tensor(row, row, tmp[:, p, 0:w], ALU.add).then_inc(x_updated, 1)

            def out_phase(blk, s, x_at, both, norm=None):
                if norm is None:
                    with dve.Fori(0, 2) as i:
                        for u in range(4):
                            split_lo(4 * i + (2 * blk + u + 3), (u + 3) % RING)
                            dve.wait_ge(x_updated, x_at - KT + 4 * i + (u + 1))
                            residual(s, x_at, i, u, both, ds(4 * i + u, 1))
                else:
                    for u in range(KT):
                        split_lo(2 * blk + u + 3, (u + 3) % RING)
                        if x_at:
                            dve.wait_ge(x_updated, x_at - KT + u + 1)
                        residual(s, x_at, 0, u, both, u)
                        if u >= 2:
                            add_squares(norm, u - 1, both)
                    add_squares(norm, KT - 1, both)

            out_phase(PW2, S_PW2, 0, True, norm=2)

            def ffn(blk, s, layer, both, x_at):
                f = 0
                w = TOK if both else LAT
                steps = 4 if both else 2
                for c_no, n in enumerate(CHUNKS):
                    with dve.Fori(0, n // 2) as i:
                        for q in range(2):
                            split_lo(4 * i + (2 * blk + 2 * q + 3), (2 * q + 3) % RING)
                            split_lo(4 * i + (2 * blk + 2 * q + 4), (2 * q + 4) % RING)
                            t_at = taps_at(layer) + steps * (f + q)
                            wt = [par[:, ds(2 * i + (FFN_DW_W + layer * P + FT * k + f + q), 1)] for k in (0, 2)]
                            t = tmp[:, q]
                            dve.wait_ge(g_first, 2 * i + (layer * FT + f + q + 1))
                            streams = [(bank(q, 1), 0, LAT)] + ([(bank(q, 2)[:, CTX:], LAT, CTX)] if both else [])
                            for b, t0, m in streams:
                                v.scalar_tensor_tensor(t[:, t0 + 1:t0 + m], b[:, 0:m - 1], wt[0], t[:, t0 + 1:t0 + m],
                                                       ALU.mult, ALU.add).then_inc(g_taps, 1)
                            for n_s, (b, t0, m) in enumerate(streams):
                                dve.wait_ge(g_taps, 2 * steps * i + (t_at + n_s + 1))
                                v.scalar_tensor_tensor(t[:, t0:t0 + m - 1], b[:, 1:m], wt[1], t[:, t0:t0 + m - 1],
                                                       ALU.mult, ALU.add).then_inc(g_taps, 1)
                            dve.wait_ge(g_silu, 2 * i + (layer * FT + f + q + 1))
                            o = v.tensor_tensor(m32[:, q, LATS], bank(q, 0), tmp[:, q, LATS], ALU.mult)
                            if both:
                                o = v.tensor_tensor(m32[:, q, CTXS], bank(q, 2)[:, 0:CTX], tmp[:, q, CTXS], ALU.mult)
                            o.then_inc(slot_read[q], 1)
                            dve.wait_ge(mid_hi_ready, 2 * i + (layer * FT + f + q + 1))
                            v.tensor_tensor(mid_lo[:, ds(2 * i + q, 1), 0:w], m32[:, q:q + 1, 0:w],
                                            mid_hi[:, ds(2 * i + q, 1), 0:w].bitcast(F32), ALU.subtract) \
                                .then_inc(mid_lo_ready, 1)
                    f += n
                    blk, s = blk + n, s + n
                    out_phase(blk, s, x_at, both, norm=3 + 2 * layer if c_no == len(CHUNKS) - 1 else None)
                    blk, s, x_at = blk + 4, s + KT, x_at + KT

            recip(2, True)
            normed(2 * KT, 2 * KT, True)
            ffn(FFN0, S_FFN0, 0, True, KT)
            recip(3, True)
            normed(3 * KT, 3 * KT, True)

            dve.wait_ge(lg_step, 1)
            v.tensor_scalar(lgam512[:], ngam[:], -float(LAT), None, ALU.mult)
            v.tensor_scalar(lgam[:], ngam[:], -1.0, None, ALU.mult).then_inc(lg_step, 1)

            def grid(ap, parts=slice(0, P)):
                return ap[parts].rearrange("p (r c) -> p r c", c=GRID_W)

            def rotate(p, dst, scale, n, frees=None):
                for f in range(2):
                    n_at = n + 4 * f
                    if f == 0:
                        cs = [rrow[:, a, :].unsqueeze(2).to_broadcast([P, ROWS, GRID_W]) for a in range(2)]
                    else:
                        cs = [rcol[:, a, :].unsqueeze(1).to_broadcast([P, ROWS, GRID_W]) for a in range(2)]
                    if n_at:
                        dve.wait_ge(rot_step, n_at)
                    src = bank(p, f)
                    v.scalar_tensor_tensor(grid(cosd), grid(src), scale, cs[0], ALU.mult, ALU.mult).then_inc(rot_step, 1)
                    for a in range(2):
                        to, frm = slice(64 * a, 64 * a + 64), slice(64 - 64 * a, 128 - 64 * a)
                        o = v.scalar_tensor_tensor(grid(rot, to), grid(src, frm), scale, cs[1][to], ALU.mult, ALU.mult)
                        if f == 1 and a == 1 and frees is not None:
                            o.then_inc(slot_read[p], 1)
                            dve.wait_ge(slot_read[p], frees)
                        else:
                            o.then_inc(rot_step, 1)
                            dve.wait_ge(rot_step, n_at + 2 + a)
                    v.tensor_tensor(dst[:, f, :], cosd, rot, ALU.add).then_inc(rot_step, 1)

            def y_parts(h):
                dve.wait_ge(y_hi_ready, 2 * h + 2)
                for f in range(2):
                    v.tensor_tensor(y_lo[:, 2 * h + f, :], ps[:, 6 + f, :], y_hi[:, 2 * h + f, :].bitcast(F32),
                                    ALU.subtract).then_inc(y_lo_ready, 1)

            for h in range(HEADS):
                blk, s = RET + 5 * h, S_RET + HEAD_USES * h
                u = 2 * blk
                split_lo(u + 3, (u + 3) % RING)
                if h == 0:
                    dve.wait_ge(ages_in, 16 * 3)
                if h:
                    dve.wait_ge(qdec_ready, 2 * h)
                v.tensor_scalar(decay[:, 0, :], iota[:], tcol[:, 0:1], 0.0, ALU.subtract, ALU.max).then_inc(age_ready, 1)
                v.tensor_scalar(decay[:, 1, :], iota[:], tcol[:, 1:2], 0.0, ALU.subtract, ALU.min).then_inc(age_ready, 1)
                split_lo(u + 4, (u + 4) % RING)
                dve.wait_ge(unit_done, 2 * blk + 2)
                if h:
                    dve.wait_ge(yT_done, h)
                rotate(0, qT, DH ** -0.5, 15 * h, s // 2 + 1)
                split_lo(u + 5, (u + 5) % RING)
                if h:
                    y_parts(h - 1)
                split_lo(u + 6, (u + 6) % RING)
                dve.wait_ge(decay_exp, 2 * h + 1)
                v.tensor_tensor(decay[:, 0, 0:P], decay[:, 0, 0:P], tup[:], ALU.mult)
                v.tensor_tensor(decay[:, 1, LAT - P:LAT], decay[:, 1, LAT - P:LAT], tlow[:], ALU.mult) \
                    .then_inc(decay_ready, 1)
                dve.wait_ge(unit_done, 2 * (blk + 1) + 2)
                if h == 0:
                    dve.wait_ge(zeta_ready, 2 * HEADS)
                rotate(1, kT, 1.0, 15 * h + 7)
                for t in range(CT):
                    for d in range(2):
                        o = v.tensor_scalar(kctx[:, d, t, :], bank(1, 2)[:, t * DH:(t + 1) * DH], zeta[:, h, d, t:t + 1],
                                            None, ALU.mult)
                o.then_inc(slot_read[1], 1)
                split_lo(u + 7, (u + 7) % RING)
                split_lo(u + 8, (u + 8) % RING)
                for j in range(LT):
                    dve.wait_ge(score_done, 7 * h + 2 + j)
                    if j == 0:
                        dve.wait_ge(decay_ready, h + 1)
                    at0 = sum(LT - a for a in range(j)) * P
                    at1 = sum(a + 1 for a in range(j)) * P
                    b = ps[:, 6 + j % 2, :]
                    v.tensor_tensor(scores[:, 0, at0:at0 + LAT - j * P], b[:, j * P:], decay[:, 0, 0:LAT - j * P], ALU.mult)
                    v.tensor_tensor(scores[:, 1, at1:at1 + (j + 1) * P], b[:, 0:(j + 1) * P],
                                    decay[:, 1, LAT - (j + 1) * P:], ALU.mult).then_inc(score_read, 1)
                dve.wait_ge(decay_exp, 2 * h + 2)
                dve.wait_ge(rot_step, 15 * h + 15)
                for d, dst in enumerate((q_dec, kT[:])):
                    v.tensor_tensor(dst, qT[:], decay[:, d, :].unsqueeze(1).to_broadcast([P, 2, LAT]), ALU.mult) \
                        .then_inc(qdec_ready, 1)
                for d in range(2):
                    n = 2 * h + d
                    if d == 0:
                        split_lo(u + 9, (u + 9) % RING)
                        split_lo(u + 10, (u + 10) % RING)
                    else:
                        split_lo(u + 11, (u + 11) % RING)
                        split_lo(u + 12, (u + 12) % RING)
                    dve.wait_ge(slot_read[0], (s + 4 + 2 * d) // 2 + 1)
                    dve.wait_ge(gn_in, 32 * (h + 1))
                    v.tensor_tensor(gate, gate, gn_row[:, d, :].unsqueeze(1).to_broadcast([P, LT, DH]), ALU.mult) \
                        .then_inc(gate_ready, 1)
                    dve.wait_ge(score_done, 7 * h + 6 + d)
                    if n:
                        dve.wait_ge(y_step, 3 * h + d)
                    for i in range(LT):
                        o_i = ps[:, 3 + i // 2, (i % 2) * DH:(i % 2 + 1) * DH]
                        o = v.bn_stats(gn_st[:, i, :], o_i)
                    o.then_inc(gn_stats, 1)
                    dve.wait_ge(gn_stats, 2 * n + 1)
                    for i in range(LT):
                        o = v.bn_aggr(gn_mv[:, i, :], gn_st[:, i, :])
                    o.then_inc(gn_stats, 1)
                    dve.wait_ge(gn_std, n + 1)
                    v.reciprocal(gn_mv[:, :, 1], gn_mv[:, :, 1]).then_inc(gn_rstd, 1)
                    dve.wait_ge(gn_rstd, n + 1)
                    dst = y_tok if d == 0 else q_dec.rearrange("p a b -> p (a b)").rearrange("p (t v) -> p t v", t=LT)
                    for i in range(LT):
                        o_i = ps[:, 3 + i // 2, (i % 2) * DH:(i % 2 + 1) * DH]
                        o = v.tensor_scalar(dst[:, i, :], o_i, gn_mv[:, i, 0:1], gn_mv[:, i, 1:2], ALU.subtract, ALU.mult)
                    o.then_inc(slot_read[1], 1)
                    dve.wait_ge(slot_read[1], (s + 5 + 2 * d) // 2 + 1)
                    dve.wait_ge(gate_ready, n + 1)
                    if d == 0:
                        v.tensor_tensor(y_tok, y_tok, gate, ALU.mult).then_inc(y_step, 1)
                    else:
                        v.tensor_tensor(dst, dst, gate, ALU.mult).then_inc(y_step, 1)
                        dve.wait_ge(y_step, 3 * h + 2)
                        v.tensor_tensor(y_tok, y_tok, dst, ALU.add).then_inc(y_step, 1)
            y_parts(HEADS - 1)
            out_phase(RET_OUT, S_RET_OUT, KT * 4, False, norm=4)
            recip(4, False)
            normed(4 * KT, 4 * KT, False)
            ffn(FFN1, S_FFN1, 1, False, KT * 5)
            recip(5, False)
            for j in range(KT):
                if j >= 2:
                    dve.wait_ge(xT_done, KT + j - 1)
                v.scalar_tensor_tensor(tmp[:, j % 2, LATS], X[:, j, LATS], par[:, FINAL_G + j:FINAL_G + j + 1],
                                       rstd[:, LATS], ALU.mult, ALU.mult).then_inc(fin_ready, 1)


_INS = ["x", "c", "ctx", "c_ctx", "ada_w", "ada_b", "norm1_g", "norm2_g", "conv_pw1_w", "conv_pw1_b", "conv_dw_w",
        "conv_dw_b", "conv_ln_g", "conv_ln_b", "conv_pw2_w", "conv_pw2_b", "ret_w_in", "ret_w_out", "ret_decay_f",
        "ret_decay_b", "ret_gn_f", "ret_gn_b", "ffn_w_in", "ffn_dw_w", "ffn_dw_b", "ffn_w_out", "final_g"]


def shape_constants():
    import numpy as np
    f = np.float32
    p = np.arange(P)
    half = DH // 4
    freqs = (10000.0 ** (-np.arange(half, dtype=f) / f(half))).astype(f)
    sign = np.where(p < half, -1.0, 1.0)[:, None]

    def table(pos):
        ang = (pos[None, :].astype(f) * freqs[p % half][:, None]).astype(f).astype(np.float64)
        return np.stack([np.cos(ang), sign * np.sin(ang)], axis=1).astype(f)

    col = np.stack([p, p + LAT - P, CTX - 1 - p, CTX - 1 - P - p, p, p + P], axis=1).astype(f)
    return {
        "eye": np.eye(P, dtype=f),
        "ages": np.broadcast_to(np.arange(LAT, dtype=f), (P, LAT)).copy(),
        "tri_low": (p[None, :] <= p[:, None]).astype(f),
        "tri_up": (p[None, :] >= p[:, None]).astype(f),
        "rope_row": table(np.arange(ROWS)),
        "rope_col": table(np.arange(GRID_W)),
        "token_cols": col,
    }


def kernel(**inputs):
    import numpy as _np
    import concourse.bacc as _bacc
    from concourse import mybir as _mybir
    from concourse.bass_utils import run_bass_kernel_spmd as _run

    nc = _bacc.Bacc("TRN2", target_bir_lowering=False, num_devices=1)
    arrays, args = {}, []
    for name, a in [(n, _np.ascontiguousarray(inputs[n])) for n in _INS] + list(shape_constants().items()):
        arrays[f"in_{name}"] = a
        args.append(nc.dram_tensor(f"in_{name}", a.shape, _mybir.dt.from_np(a.dtype), kind="ExternalInput").ap())
    args.append(nc.dram_tensor("out", (1, LAT, D), _mybir.dt.float32, kind="ExternalOutput").ap())
    backbone(nc, *args)
    r = _run(nc, [arrays], core_ids=[0])
    return r.results[0]["out"]
```

```python
from contextlib import ExitStack

import concourse.bass as bass
from concourse import mybir

F32 = mybir.dt.float32
F32R = mybir.dt.float32r
ALU = mybir.AluOpType
ACT = mybir.ActivationFunctionType
ds = bass.ds

P = 128
D = 1024
KT = D // P
LAT, CTX = 512, 256
TOK = LAT + CTX
LT, CT = LAT // P, CTX // P
PART = CTX
DEPTH = 2
F = ((8 * D // 3 + 127) // 128) * 128
FT = F // P
TAPS = 31
PAD = TAPS // 2
CTX_PAD = PAD + LAT + PAD
PADW = CTX_PAD + CTX + PAD
CTX_OUT = LAT + PAD
OUTW = CTX_OUT + CTX
HEADS, DH = 4, 256
GRID_W = 64
ROWS = LAT // GRID_W
NORM_EPS, GN_EPS = 1e-6, 1e-5
CHUNKS = [FT - 16, 8, 8]
RING = 4

PW1, PW2 = 0, KT
FFN0 = PW2 + KT // 2
FFN_BLOCKS = FT + 4 * len(CHUNKS)
RET = FFN0 + FFN_BLOCKS
RET_OUT = RET + 5 * HEADS
FFN1 = RET_OUT + KT // 2
BLOCKS = FFN1 + FFN_BLOCKS
UNITS = 2 * BLOCKS

NORM_PARTS = [3, 3, 3, 3, 2, 2]
PARTS_BEFORE = [sum(NORM_PARTS[:n]) for n in range(7)]
FULL = KT // 2


def tail_uses(parts):
    return FULL + (KT - FULL) * parts


S_XT = 0
S_PW1 = S_XT + 12
S_LN = S_PW1 + 2 * KT
S_PW2 = S_LN + 2
S_FFN0 = S_PW2 + 3 * KT
S_FFN = FT + KT * (len(CHUNKS) - 1)
S_RET = S_FFN0 + S_FFN + tail_uses(3)
HEAD_USES = 8
S_RET_OUT = S_RET + HEAD_USES * HEADS
S_FFN1 = S_RET_OUT + tail_uses(2)
S_OUT = S_FFN1 + S_FFN + tail_uses(2)

X_FFN0 = 3 * KT
X_RET_OUT = X_FFN0 + 2 * KT + tail_uses(3)
X_FFN1 = X_RET_OUT + tail_uses(2)
SQ_BEFORE = {2: 0, 3: 3 * KT, 4: 3 * KT + tail_uses(3), 5: 3 * KT + tail_uses(3) + tail_uses(2)}
ADDS_BEFORE = {2: 0, 3: 3 * (KT - 1), 4: 3 * (KT - 1) + tail_uses(3) - 1, 5: 3 * (KT - 1) + tail_uses(3) + tail_uses(2) - 2}
PARTS_DONE = {2: 0, 3: 2 * KT, 4: 2 * KT + 8, 5: 2 * KT + 12}
TAIL_TILES = [[], [0, 1, 2], [3, 4, 5], [6, 7]]
LN_TILES = [[0, 1], [2, 3], [4, 5], [6, 7]]


def sq_count(norm, u, t=None):
    if u < FULL and t is None:
        return SQ_BEFORE[norm] + u + 1
    at = 0 if norm == 2 and u < FULL else (3 * FULL if norm == 2 else FULL)
    return SQ_BEFORE[norm] + at + FULL * t + u % FULL + 1


def add_count(norm, u, t=None):
    if u < FULL and t is None:
        return ADDS_BEFORE[norm] + u
    if u < FULL:
        return ADDS_BEFORE[norm] + (FULL - 1) * t + u
    return ADDS_BEFORE[norm] + (3 if norm == 2 else 1) * (FULL - 1) + FULL * t + u % FULL + 1


ADA_B = 0
NORM1, NORM2 = 96, 112
PW1_B, DW_B, LN_G, LN_B, PW2_B, FFN_DW_B, FINAL_G, C_COL = 128, 144, 152, 160, 168, 176, 220, 228
DW_W = 256
FFN_DW_W = 512
GROUP = 4
PE_TAPS = 9
DVE_TAPS = TAPS - PE_TAPS


def backbone(nc, x, c, ctx_tok, c_ctx, ada_w, ada_b, norm1_g, norm2_g, pw1_w, pw1_b, dw_w, dw_b, ln_g, ln_b,
             pw2_w, pw2_b, ret_w_in, ret_w_out, decay_f, decay_b, gn_f, gn_b, ffn_w_in, ffn_dw_w, ffn_dw_b,
             ffn_w_out, final_g, eye, ages, tri_low, tri_up, rope_row, rope_col, token_cols, out):
    with ExitStack() as stack:
        def sb(name, shape, dt=F32, where=stack):
            return where.enter_context(nc.sbuf_tensor(name, shape, dt))

        def sem(name):
            return stack.enter_context(nc.semaphore(name))

        X = sb("X", [P, KT, TOK])
        H_hi = sb("H_hi", [P, KT, TOK], F32R)
        H_lo = sb("H_lo", [P, KT, TOK], F32R)
        w_raw = sb("w_raw", [P, RING, KT * P])
        w_hi = sb("w_hi", [P, RING, KT * P], F32R)
        w_lo = sb("w_lo", [P, RING, KT * P], F32R)
        rstd = sb("rstd", [P, TOK])
        sq = sb("sq", [P, 2, TOK])
        tmp = sb("tmp", [P, 2, TOK])
        par = sb("par", [P, 768])
        ident = sb("ident", [P, P])
        mean_of = sb("mean_of", [P, P])
        eps = sb("eps", [P, 2])
        silu_c = sb("silu_c", [P, KT, 32])
        mod = sb("mod", [P, DEPTH, 48, 2])
        gain = sb("gain", [P, DEPTH, 2, KT, 2])
        pw2_gb = sb("pw2_gb", [P, KT, 2])
        decay_log = sb("decay_log", [P, 2 * HEADS])
        lgam = sb("lgam", [P, 2 * HEADS])
        ngam = sb("ngam", [P, 2 * HEADS])
        lgam512 = sb("lgam512", [P, 2 * HEADS])
        rrow = sb("rrow", [P, 2, ROWS])
        rcol = sb("rcol", [P, 2, GRID_W])
        tcol = sb("tcol", [P, 6])
        zeta = sb("zeta", [P, HEADS, 2, CT])
        with ExitStack() as ph:
            conv = sb("conv", [P, KT, OUTW + 1], F32, ph)
            ada = sb("ada", [P, 2, KT // 2, GROUP * P], F32, ph)
            tap_hi = sb("tap_hi", [P, PE_TAPS * KT], F32R, ph)
            tap_lo = sb("tap_lo", [P, PE_TAPS * KT], F32, ph)
            with ExitStack() as start:
                ada_more = sb("ada_more", [P, 2, KT // 2, GROUP * P], F32, start)
                ada_row0 = sb("ada_row0", [P, GROUP * P], F32, start)
            diag_hi = sb("diag_hi", [P, 2, PE_TAPS, P], F32R, ph)
            diag_lo = sb("diag_lo", [P, 2, PE_TAPS, P], F32R, ph)
            u_hi = sb("u_hi", [P, PADW], F32R, ph)
            u_lo = sb("u_lo", [P, PADW], F32R, ph)
        with ExitStack() as ph:
            mid_hi = sb("mid_hi", [P, 8, TOK], F32R, ph)
            mid_lo = sb("mid_lo", [P, 8, TOK], F32R, ph)
            m32 = sb("m32", [P, 2, TOK], F32, ph)
        with ExitStack() as ph:
            y_hi = sb("y_hi", [P, KT, LAT], F32R, ph)
            y_lo = sb("y_lo", [P, KT, LAT], F32R, ph)
            qT = sb("qT", [P, 2, LAT], F32, ph)
            kT = sb("kT", [P, 2, LAT], F32, ph)
            V = sb("V", [P, LT, DH], F32, ph)
            scores = sb("scores", [P, 2, 10 * P], F32, ph)
            state = sb("state", [P, 2, 2, DH], F32, ph)
            decay = sb("decay", [P, 2, LAT], F32, ph)
            iota = sb("iota", [P, LAT], F32, ph)
            tlow = sb("tlow", [P, P], F32, ph)
            tup = sb("tup", [P, P], F32, ph)
            gn_st = sb("gn_st", [P, LT, 6], F32, ph)
            gn_mv = sb("gn_mv", [P, LT, 2], F32, ph)
        y_tok = qT[:].rearrange("p f t -> p (f t)").rearrange("p (t v) -> p t v", t=LT)
        flat_tmp, flat_sq = (a[:].rearrange("p a b -> p (a b)") for a in (tmp, sq))
        upad = [flat_tmp[:, 0:PADW], flat_sq[:, 0:PADW]]
        def ada_row(m):
            beside = not isinstance(m, int) or 4 <= m <= 20
            return flat_tmp[:, 2 * TOK - GROUP * P:] if beside else ada_row0[:]

        ada_first = [ada[:], w_raw[:].rearrange("p (h k) n -> p h (k n)", h=2).rearrange("p h (k n) -> p h k n", n=GROUP * P),
                     ada_more[:], ada[:]]
        norm_buf = [tmp[:, 0], tmp[:, 1], sq[:, 0], sq[:, 1]]
        q_dec = tmp[:, 0:2, :].rearrange("p a b -> p (a b)")[:, 0:2 * LAT].rearrange("p (a b) -> p a b", a=2)
        rot = tmp[:, 0:2, :].rearrange("p a b -> p (a b)")[:, 2 * LAT:3 * LAT]
        cosd = rstd[:, 0:LAT]
        gate = sq[:, 0:2, :].rearrange("p a b -> p (a b)")[:, 0:LT * DH].rearrange("p (a b) -> p a b", a=LT)
        gn_row = sq[:, 0:2, :].rearrange("p a b -> p (a b)")[:, LT * DH:LT * DH + 2 * DH].rearrange(
            "p (a b) -> p a b", a=2)
        kctx = scores[:, 0, 0:4 * DH].rearrange("p (d t v) -> p d t v", d=2, t=CT)
        vctx = scores[:, 1, 0:2 * DH].rearrange("p (t v) -> p t v", t=CT)
        xin = conv[:, :, :].rearrange("p a b -> p (a b)")[:, 0:6 * D].rearrange("p (t d) -> p t d", t=6)
        prow = tmp[:, :, :].rearrange("p a b -> p (a b)")[:, 0:768].rearrange("p (a b) -> p a b", b=P)
        otok = conv[:, :, :].rearrange("p a b -> p (a b)")[:, 0:LT * D].rearrange("p (t d) -> p t d", t=LT)

        ps = stack.enter_context(nc.psum_tensor("ps", [P, 8, 512], F32))

        raw_ready = [sem(f"raw_ready{r}") for r in range(RING)]
        hi_ready = sem("hi_ready")
        lo_ready = sem("lo_ready")
        unit_done = sem("unit_done")
        slot_read = [sem("slot_read0"), sem("slot_read1")]
        par_rows = sem("par_rows")
        consts_in = sem("consts_in")
        eye_in = sem("eye_in")
        ages_in = sem("ages_in")
        tokens_in = [sem("tokens_in0"), sem("tokens_in1"), sem("tokens_in2")]
        ada_first_in = [sem(f"ada_first_in{g}") for g in range(4)]
        part_done = sem("part_done")
        stat_sq = sem("stat_sq")
        stat_used = sem("stat_used")
        filled = sem("filled")
        par_T = sem("par_T")
        par_ready = sem("par_ready")
        silu_c_ready = sem("silu_c_ready")
        ada_in = [sem("ada_in0"), sem("ada_in1")]
        ada_done = sem("ada_done")
        ada_row_ready = sem("ada_row_ready")
        ada_T = sem("ada_T")
        mod_sum = sem("mod_sum")
        mod_ready = sem("mod_ready")
        xT_done = sem("xT_done")
        sq_ready = sem("sq_ready")
        ssq_ready = sem("ssq_ready")
        sq_summed = sem("sq_summed")
        modulated = sem("modulated")
        taps_split = sem("taps_split")
        padded = sem("padded")
        diag_ready = sem("diag_ready")
        u_hi_ready = sem("u_hi_ready")
        u_lo_ready = sem("u_lo_ready")
        conv_done = sem("conv_done")
        std_ready = sem("std_ready")
        rstd_ready = sem("rstd_ready")
        scaled = sem("scaled")
        h_hi_ready = sem("h_hi_ready")
        h_lo_ready = sem("h_lo_ready")
        sig_ready = sem("sig_ready")
        tap_done = sem("tap_done")
        mu_summed = sem("mu_summed")
        centered = sem("centered")
        ln_scaled = sem("ln_scaled")
        ln_silu = sem("ln_silu")
        x_updated = sem("x_updated")
        g_first = sem("g_first")
        g_taps = sem("g_taps")
        g_silu = sem("g_silu")
        mid_hi_ready = sem("mid_hi_ready")
        mid_lo_ready = sem("mid_lo_ready")
        lg_step = sem("lg_step")
        zeta_ready = sem("zeta_ready")
        gn_in = sem("gn_in")
        rot_step = sem("rot_step")
        age_ready = sem("age_ready")
        decay_exp = sem("decay_exp")
        decay_ready = sem("decay_ready")
        score_done = sem("score_done")
        score_read = sem("score_read")
        qdec_ready = sem("qdec_ready")
        gn_stats = sem("gn_stats")
        gn_var = sem("gn_var")
        gn_std = sem("gn_std")
        gn_rstd = sem("gn_rstd")
        gate_ready = sem("gate_ready")
        y_step = sem("y_step")
        yT_done = sem("yT_done")
        y_hi_ready = sem("y_hi_ready")
        y_lo_ready = sem("y_lo_ready")
        fin_ready = sem("fin_ready")
        stored = sem("stored")

        LATS, CTXS = slice(0, LAT), slice(LAT, TOK)

        def part(t):
            return slice(t * PART, (t + 1) * PART)

        def groups(both):
            return [(0, LATS), (1, CTXS)] if both else [(0, LATS)]

        def stat_bank(norm, t):
            bank = (1, 4, 5)[t] if norm < 2 else 6 + (PARTS_BEFORE[norm] + t) % 2
            return ps[:, bank, 0:PART]

        def modulation_of(norm, t):
            return (0 if norm < 3 else 1), (0 if norm in (0, 3) else 1), t // 2

        def shift(norm, t, j):
            layer, half, m = modulation_of(norm, t)
            return mod[:, layer, 24 * half + j, m:m + 1]

        def conv_part(j, t):
            return conv[:, j, t * PART:(t + 1) * PART] if t < 2 else conv[:, j, CTX_OUT:OUTW]

        def taps_at(layer):
            return 4 * FT * layer

        def first_squares(t, n):
            return (sq if n % 2 == 0 else tmp)[:, :, part(t)]

        block = stack.enter_context(nc.Block())

        @block.sync
        def _(sp):
            for n, (lo, rows, src) in enumerate([
                    (0, 96, ada_b.rearrange("l (t p) -> (l t) p", p=P)),
                    (NORM1, 16, norm1_g.rearrange("l (t p) -> (l t) p", p=P)),
                    (NORM2, 16, norm2_g.rearrange("l (t p) -> (l t) p", p=P)),
                    (PW1_B, 16, pw1_b.rearrange("l (t p) -> (l t) p", p=P)),
                    (DW_B, 8, dw_b.rearrange("l (t p) -> (l t) p", p=P)),
                    (LN_G, 8, ln_g.rearrange("l (t p) -> (l t) p", p=P)),
                    (LN_B, 8, ln_b.rearrange("l (t p) -> (l t) p", p=P)),
                    (PW2_B, 8, pw2_b.rearrange("l (t p) -> (l t) p", p=P)),
                    (FFN_DW_B, 44, ffn_dw_b.rearrange("l (t p) -> (l t) p", p=P)),
                    (FINAL_G, 8, final_g.rearrange("(t p) -> t p", p=P)),
                    (C_COL, 8, c.rearrange("b (t p) -> (b t) p", p=P)),
                    (C_COL + 8, 8, c_ctx.rearrange("(t p) -> t p", p=P)),
                    (DW_W, 128, dw_w[0].rearrange("k (t p) -> (k t) p", p=P)[0:128]),
                    (DW_W + 128, 120, dw_w[0].rearrange("k (t p) -> (k t) p", p=P)[128:248]),
                    (FFN_DW_W, 66, ffn_dw_w[0].rearrange("k (t p) -> (k t) p", p=P)),
                    (FFN_DW_W + 128, 66, ffn_dw_w[1].rearrange("k (t p) -> (k t) p", p=P))]):
                r0 = lo % P
                sp.dma_start(prow[r0:r0 + rows, lo // P, :], src).then_inc(par_rows, 16)
                if n == 0:
                    sp.dma_start(ident[:], eye).then_inc(eye_in, 16)
            for dst, src in ((rrow[:], rope_row), (rcol[:], rope_col), (tcol[:], token_cols),
                             (decay_log[:, 0:HEADS], decay_f.to_broadcast([P, HEADS])),
                             (decay_log[:, HEADS:], decay_b.to_broadcast([P, HEADS]))):
                sp.dma_start(dst, src).then_inc(consts_in, 16)

            def load(unit, r, src):
                if not (isinstance(unit, int) and unit < RING):
                    sp.wait_ge(lo_ready, unit - (RING - 1))
                k = src.shape[0] // P
                sp.dma_start(w_raw[:, r, 0:k * P].rearrange("p (k n) -> p k n", n=P),
                             src.rearrange("(k p) n -> p k n", p=P)).then_inc(raw_ready[r], 16)

            def load_pairs(first, w, half, n):
                def body(i):
                    for q in range(2):
                        for h in range(2):
                            load(2 * first + 4 * i + 2 * q + h, 2 * q + h,
                                 w[:, ds(i * (2 * P) + (q * P + h * half), P)])
                if first == PW1:
                    body(0)
                with sp.Fori(1 if first == PW1 else 0, n // 2) as i:
                    body(i)

            def load_cols(first, w, n):
                with sp.Fori(0, n // 2) as i:
                    for u in range(4):
                        load(2 * first + 4 * i + u, u, w[:, ds(i * (4 * P) + u * P, P)])

            def load_ffn(first, layer):
                w_in, w_out = ffn_w_in[layer], ffn_w_out[layer]
                f = 0
                for n in CHUNKS:
                    load_pairs(first, w_in[:, f * P:], F, n)
                    load_cols(first + n, w_out[f * P:(f + n) * P, :], 4)
                    first += n + 4
                    f += n

            sp.wait_ge(ada_done, 4)
            load_pairs(PW1, pw1_w[0], D, KT)
            load_cols(PW2, pw2_w[0], KT // 2)
            load_ffn(FFN0, 0)
            for h in range(HEADS):
                for part in range(5):
                    for u in range(2):
                        unit = 2 * (RET + 5 * h + part) + u
                        load(unit, unit % RING, ret_w_in[0][:, part * D + h * DH + u * P:part * D + h * DH + (u + 1) * P])
            load_cols(RET_OUT, ret_w_out[0], KT // 2)
            load_ffn(FFN1, 1)
            for t in range(2):
                for jj in range(KT // 2):
                    n = 4 * t + jj
                    sp.wait_ge(slot_read[n % 2], (S_OUT + n) // 2 + 1)
                    cols = slice(2 * jj * P, 2 * (jj + 1) * P)
                    sp.dma_start(out[0].rearrange("(t p) d -> p t d", p=P)[:, 2 * t:2 * t + 2, cols],
                                 otok[:, 2 * t:2 * t + 2, cols]).then_inc(stored, 16)
            sp.wait_ge(stored, 16 * KT)

        @block.gpsimd
        def _(pool):
            nc.gpsimd.memset(mean_of[:], 1.0 / D).then_inc(filled, 1)
            nc.gpsimd.memset(eps[:, 0:1], NORM_EPS).then_inc(filled, 1)
            nc.gpsimd.memset(eps[:, 1:2], GN_EPS).then_inc(filled, 1)
            nc.gpsimd.memset(silu_c[:], 0.0).then_inc(filled, 1)

            def load_group(layer, col, done):
                for half in range(2):
                    pool.wait_ge(ada_done, done + half)
                    rows = slice(half * D // 2, (half + 1) * D // 2)
                    pool.dma_start(ada[:, half], ada_w[layer][rows, ds(col, GROUP * P)]
                                   .rearrange("(k p) n -> p k n", p=P)).then_inc(ada_in[half], 16)
            for m in range(4):
                for half in range(2):
                    if m == 3:
                        pool.wait_ge(ada_done, half + 1)
                    if m == 0 and half:
                        pool.wait_ge(par_rows, 16 * 16)
                    rows = slice(half * D // 2, (half + 1) * D // 2)
                    pool.dma_start(ada_first[m][:, half], ada_w[0][rows, m * GROUP * P:(m + 1) * GROUP * P]
                                   .rearrange("(k p) n -> p k n", p=P)).then_inc(ada_first_in[m], 16)
            with pool.Fori(0, KT) as i:
                load_group(0, i * (GROUP * P) + 4 * GROUP * P, 4 * i + 7)
                load_group(1, i * (GROUP * P), 4 * i + 9)
            with pool.Fori(0, 4) as i:
                load_group(1, i * (GROUP * P) + KT * GROUP * P, 2 * i + 39)
            for h in range(HEADS):
                if h == 0:
                    pool.wait_ge(h_lo_ready, KT * PARTS_BEFORE[4])
                    for dst, src in ((iota, ages), (tlow, tri_low), (tup, tri_up)):
                        pool.dma_start(dst[:], src).then_inc(ages_in, 16)
                else:
                    pool.wait_ge(y_step, 3 * h)
                for n, g in enumerate((gn_f, gn_b)):
                    pool.dma_start(gn_row[:, n, :], g[:, h * DH:(h + 1) * DH].to_broadcast([P, DH])) \
                        .then_inc(gn_in, 16)

        @block.tensor
        def _(pe):
            def mm(o, a, b, first, last):
                return nc.tensor.matmul(o, a, b, start=first, stop=last, skip_group_check=True)

            def slot_free(s, half):
                p = s % 2
                if half is None:
                    half = s // 2
                if not (isinstance(half, int) and half < 1):
                    pe.wait_ge(slot_read[p], half)

            def unit_product(unit, r, kt, src, streams, ready=None, done=unit_done):
                s_hi, s_lo = src
                pe.wait_ge(lo_ready, unit + 1)
                for k in range(kt):
                    if ready is not None:
                        pe.wait_ge(ready[0], ready[1] + (k + 1))
                    a_hi, a_lo = w_hi[:, r, k * P:(k + 1) * P], w_lo[:, r, k * P:(k + 1) * P]
                    for a, b in ((a_hi, s_hi), (a_hi, s_lo), (a_lo, s_hi)):
                        for o, toks in streams:
                            m = mm(o, a, b[:, k, toks], k == 0 and a is a_hi and b is s_hi, k == kt - 1 and a is a_lo)
                if done is not None:
                    m.then_inc(done, 1)
                return m

            def slot(p, bank):
                return ps[:, 3 * p + bank, :]

            def pair_block(blk, q, s, half, src, both, ready):
                slot_free(s, half)
                for h in range(2):
                    streams = [(slot(s % 2, h), LATS)]
                    if both:
                        streams.append((slot(s % 2, 2)[:, h * CTX:(h + 1) * CTX], CTXS))
                    unit_product(2 * blk + h, 2 * q + h, KT, src, streams, ready)

            def sum_squares(norm, t):
                g = PARTS_BEFORE[norm] + t
                pe.wait_ge(ssq_ready, add_count(norm, KT - 1, t))
                pe.wait_ge(std_ready, g - 1)
                mm(stat_bank(norm, t), mean_of[:], rstd[:, part(t)], True, True).then_inc(sq_summed, 1)

            def sum_tiles(norm, t, n_at, steps, src):
                for n in range(steps):
                    pe.wait_ge(stat_sq, n_at + n + 1)
                    tiles = src(n)
                    for a, tile in enumerate(tiles):
                        last = n == steps - 1 and a == len(tiles) - 1
                        m = mm(stat_bank(norm, t), mean_of[:], tile, n == 0 and a == 0, last)
                    m.then_inc(sq_summed if n == steps - 1 else stat_used, 1)

            def out_phase(blk, s, kt, src, both, ready):
                with pe.Fori(0, 2) as i:
                    for u in range(4):
                        slot_free(s + u, s // 2 + 2 * i + u // 2)
                        streams = [(slot((s + u) % 2, 0), LATS)] + \
                            ([(slot((s + u) % 2, 2)[:, 0:CTX], CTXS)] if both else [])
                        unit_product(2 * blk + 4 * i + u, u, kt, src, streams, ready)

            def part_slot_free(s, n):
                if n < 2:
                    slot_free(s + n, None)
                elif n >= 6:
                    pe.wait_ge(slot_read[(s + n) % 2], (s + n) // 2 - 2)

            def by_parts(unit, s, kt, src, parts, norm):
                for t in range(parts):
                    for i in range(4):
                        n = 4 * t + i
                        part_slot_free(s, n)
                        unit_product(unit + i, i, kt, src, [(slot((s + n) % 2, n // 2 % 3)[:, 0:PART], part(t))],
                                     None, unit_done if t == parts - 1 else part_done)
                        if i == 0 and t:
                            sum_squares(norm, t - 1)

            def out_phase_norm(blk, s, kt, src, both, ready, norm):
                for u in range(FULL):
                    slot_free(s + u, None)
                    streams = [(slot((s + u) % 2, 0), LATS)] + \
                        ([(slot((s + u) % 2, 2)[:, 0:CTX], CTXS)] if both else [])
                    unit_product(2 * blk + u, u, kt, src, streams, ready)
                by_parts(2 * blk + FULL, s + FULL, kt, src, 3 if both else 2, norm)

            def ada_products(m):
                if not isinstance(m, int) or m:
                    pe.wait_ge(ada_row_ready, m)
                first = isinstance(m, int) and m < 4
                for half in range(2):
                    if first:
                        pe.wait_ge(ada_first_in[m], 32)
                    else:
                        pe.wait_ge(ada_in[half], 16 * m - 48)
                    w = ada_first[m][:, half] if first else ada[:, half]
                    for k in range(KT // 2):
                        o = mm(ps[32 * k:32 * k + 32, 6, :], silu_c[:, half * (KT // 2) + k, :], w[:, k, :],
                               half == 0, half == 1)
                    o.then_inc(ada_done, 1)

            def ada_transposes(m):
                pe.wait_ge(ada_row_ready, m + 1)
                if not isinstance(m, int) or m:
                    pe.wait_ge(mod_sum, m)
                for t in range(GROUP):
                    o = nc.tensor.transpose(ps[:, 7, t * P:(t + 1) * P], ada_row(m)[:, t * P:(t + 1) * P], ident[:])
                o.then_inc(ada_T, 1)

            def token_transposes(t):
                pe.wait_ge(tokens_in[t], 32)
                for jj in range(KT // 2):
                    s = S_XT + 4 * t + jj
                    slot_free(s, None)
                    for a in range(2):
                        for tt in range(2):
                            m = nc.tensor.transpose(slot(s % 2, 0)[:, a * PART + tt * P:a * PART + (tt + 1) * P],
                                                    xin[:, 2 * t + tt, (2 * jj + a) * P:(2 * jj + a + 1) * P], ident[:])
                    m.then_inc(xT_done, 1)

            def token_squares(t):
                sum_tiles(0, t, 4 * t, 4, lambda n: [first_squares(t, n)[:, a, :] for a in range(2)])

            pe.wait_ge(eye_in, 16)
            token_transposes(0)
            token_transposes(1)
            pe.wait_ge(par_rows, 16 * 16)
            for j, rows in enumerate((128, 116, 128, 120, 66, 66)):
                m = nc.tensor.transpose(ps[:, 6 + j // 4, (j % 4) * P:(j % 4) * P + rows], prow[0:rows, j, :],
                                        ident[0:rows, 0:rows])
            m.then_inc(par_T, 1)
            pe.wait_ge(filled, 4)
            token_squares(0)
            token_transposes(2)
            token_squares(1)
            pe.wait_ge(silu_c_ready, 2)
            ada_products(0)
            token_squares(2)
            for m in range(1, 4):
                ada_products(m)
                ada_transposes(m - 1)
            ada_transposes(3)

            def conv_taps(b, p):
                n = b + S_PW1 // 2
                pe.wait_ge(slot_read[1], n)
                pe.wait_ge(diag_ready, b + 1)
                pe.wait_ge(u_lo_ready, b + 1)
                for k in range(PE_TAPS):
                    for a, u in ((diag_hi, u_hi), (diag_hi, u_lo), (diag_lo, u_hi)):
                        first, last = k == 0 and a is diag_hi and u is u_hi, k == PE_TAPS - 1 and a is diag_lo
                        mm(slot(1, 0), a[:, p, k, :], u[:, k:k + LAT], first, last)
                        m = mm(slot(1, 2)[:, 0:CTX], a[:, p, k, :], u[:, CTX_OUT + k:OUTW + k], first, last)
                m.then_inc(conv_done, 1)

            def pw1_body(i):
                for q in range(2):
                    b = 2 * i + q
                    pe.wait_ge(slot_read[0], b + S_PW1 // 2)
                    if isinstance(i, int) and b == 0:
                        for t in range(3):
                            if t == 2:
                                ada_products(4)
                            for h in range(2):
                                o = slot(0, 2)[:, h * CTX:(h + 1) * CTX] if t == 2 else slot(0, h)[:, part(t)]
                                unit_product(h, h, KT, (H_hi, H_lo), [(o, part(t))], (h_lo_ready, KT * t),
                                             unit_done if t == 2 else None)
                    else:
                        for h in range(2):
                            unit_product(4 * i + (2 * q + h), 2 * q + h, KT, (H_hi, H_lo),
                                         [(slot(0, h), LATS), (slot(0, 2)[:, h * CTX:(h + 1) * CTX], CTXS)])
                            if h == 0:
                                ada_products(4 * i + (2 * q + 4))
                    ada_transposes(4 * i + (2 * q + 4))
                    ada_products(4 * i + (2 * q + 5))
                    if not (isinstance(i, int) and b == 0):
                        conv_taps(2 * i + (q - 1), 1 - q)
                    ada_transposes(4 * i + (2 * q + 5))
            pw1_body(0)
            with pe.Fori(1, KT // 2) as i:
                pw1_body(i)
            ada_products(20)
            conv_taps(KT - 1, 1)
            ada_transposes(20)
            slot_free(S_LN, None)
            for j in range(KT):
                if j == KT - 1:
                    ada_products(21)
                pe.wait_ge(slot_read[1], S_PW1 // 2 + j + 1)
                mm(slot(0, 0), mean_of[:], conv[:, j, 0:LAT], j == 0, j == KT - 1)
                m = mm(slot(0, 2)[:, 0:CTX], mean_of[:], conv[:, j, CTX_OUT:OUTW], j == 0, j == KT - 1)
            m.then_inc(mu_summed, 1)
            ada_transposes(21)

            def variance(t):
                sum_tiles(1, t, 12 + KT * t, KT, lambda n: [norm_buf[n % 4][:, part(t)]])

            for t in range(3):
                variance(t)
            src = (H_hi, H_lo)
            for t in range(3):
                for i in range(4):
                    n = 4 * t + i
                    part_slot_free(S_PW2, n)
                    unit_product(2 * PW2 + i, i, KT, src, [(slot(n % 2, n // 2 % 3)[:, 0:PART], part(t))],
                                 (h_lo_ready, KT * (PARTS_BEFORE[1] + t)), unit_done if t == 2 else part_done)
                    if n in (1, 5):
                        ada_products(22 + t)
                    if n in (2, 6):
                        ada_transposes(22 + t)
            by_parts(2 * PW2 + FULL, S_PW2 + 12, KT, src, 3, 2)

            def ffn(blk, s, layer, both):
                norm = 2 + 2 * layer
                last = 2 if both else 1
                H = (H_hi, H_lo)
                order = [(0, 0), (1, 0), (0, 1), (0, 2), (1, 1), (1, 2)] if both else [(0, 0), (1, 0), (0, 1), (1, 1)]
                for q, t in order:
                    if t == 0:
                        slot_free(s + q, None)
                    for h in range(2):
                        o = slot(q, 2)[:, h * CTX:(h + 1) * CTX] if t == 2 else slot(q, h)[:, part(t)]
                        unit_product(2 * blk + 2 * q + h, 2 * q + h, KT, H, [(o, part(t))],
                                     (h_lo_ready, KT * (PARTS_BEFORE[norm] + t)) if q == 0 else None,
                                     unit_done if t == last else None)
                        if q == 0 and t == 0 and h == 0:
                            sum_squares(norm, last)
                mid_at = layer * FT
                for c_no, n in enumerate(CHUNKS):
                    with pe.Fori(1 if c_no == 0 else 0, n // 2) as i:
                        for q in range(2):
                            pair_block(blk + 2 * i + q, q, s + q, s // 2 + i, H, both, None)
                    blk, s = blk + n, s + n
                    if c_no < len(CHUNKS) - 1:
                        out_phase(blk, s, n, (mid_hi, mid_lo), both, (mid_lo_ready, mid_at))
                    else:
                        out_phase_norm(blk, s, n, (mid_hi, mid_lo), both, (mid_lo_ready, mid_at), 3 + 2 * layer)
                    mid_at += n
                    blk, s = blk + 4, s + KT

            ffn(FFN0, S_FFN0, 0, True)

            H2 = (H_hi, H_lo)

            def token_major(blk, streams):
                u0 = 2 * blk % RING
                pe.wait_ge(lo_ready, 2 * blk + 2)
                for o, t0 in streams:
                    for k in range(KT):
                        b_hi, b_lo = (w[:, u0:u0 + 2, k * P:(k + 1) * P] for w in (w_hi, w_lo))
                        a_hi, a_lo = (a[:, k, t0:t0 + P] for a in H2)
                        mm(o, a_hi, b_hi, k == 0, False)
                        mm(o, a_hi, b_lo, False, False)
                        m = mm(o, a_lo, b_hi, False, k == KT - 1)
                return m

            def toks4(p):
                return [(ps[:, 3 * p + t // 2, (t % 2) * DH:(t % 2 + 1) * DH], t * P) for t in range(LT)]

            def toks2(p):
                return [(ps[:, 3 * p + 2, t * DH:(t + 1) * DH], LAT + t * P) for t in range(CT)]

            def transposes(h):
                pe.wait_ge(y_step, 3 * (h + 1))
                for f in range(2):
                    for t in range(LT):
                        m = nc.tensor.transpose(ps[:, 6 + f, t * P:(t + 1) * P], y_tok[:, t, f * P:(f + 1) * P], ident[:])
                m.then_inc(yT_done, 1)

            h_at = KT * PARTS_BEFORE[3]
            for h in range(HEADS):
                blk, s = RET + 5 * h, S_RET + HEAD_USES * h
                slot_free(s, None)
                for t in range(1 if h else 2):
                    for u in range(2):
                        toks = LATS if h else part(t)
                        unit_product(2 * blk + u, (2 * blk + u) % RING, KT, H2, [(slot(0, u)[:, toks], toks)],
                                     None if h else (h_lo_ready, h_at + KT * t), unit_done if h or t else None)
                        if h == 0 and t == 0 and u == 0:
                            sum_squares(3, 2)
                if h:
                    transposes(h - 1)
                blk += 1
                slot_free(s + 1, None)
                pe.wait_ge(lo_ready, 2 * blk + 2)
                if h:
                    token_major(blk, toks2(1))
                for u in range(2):
                    unit_product(2 * blk + u, (2 * blk + u) % RING, KT, H2, [(slot(1, u), LATS)], None,
                                 unit_done if h else None)
                if h == 0:
                    pe.wait_ge(h_lo_ready, h_at + 3 * KT)
                    token_major(blk, toks2(1)).then_inc(unit_done, 2)
                blk += 1
                slot_free(s + 2, None)
                token_major(blk, toks4(0) + toks2(0)).then_inc(unit_done, 2)
                slot_free(s + 3, None)
                pe.wait_ge(slot_read[0], (s + 2) // 2 + 1)
                for d in range(2):
                    for f in range(2):
                        for t in range(CT):
                            m = mm(ps[:, 3 + d, f * DH:(f + 1) * DH], kctx[:, d, t, f * P:(f + 1) * P], vctx[:, t, :],
                                   t == 0, t == CT - 1)
                m.then_inc(score_done, 1)
                pe.wait_ge(rot_step, 15 * h + 15)
                for j in range(LT):
                    n = h * LT + j
                    if n >= 2:
                        pe.wait_ge(score_read, n - 1)
                    if j < 2 and h >= 1:
                        pe.wait_ge(y_lo_ready, 2 * h)
                    for f in range(2):
                        m = mm(ps[:, 6 + j % 2, :], kT[:, f, j * P:(j + 1) * P], qT[:, f, :], f == 0, f == 1)
                    m.then_inc(score_done, 1)
                for d in range(2):
                    blk += 1
                    slot_free(s + 4 + 2 * d, None)
                    token_major(blk, toks4(0)).then_inc(unit_done, 2)
                    slot_free(s + 5 + 2 * d, None)
                    pe.wait_ge(score_read, (h + 1) * LT)
                    pe.wait_ge(qdec_ready, 2 * h + d + 1)
                    for i in range(LT):
                        o = ps[:, 3 + i // 2, (i % 2) * DH:(i % 2 + 1) * DH]
                        js = range(0, i + 1) if d == 0 else range(i, LT)
                        for n, j in enumerate(js):
                            at = sum((LT - a) if d == 0 else (a + 1) for a in range(j)) + (i - j if d == 0 else i)
                            mm(o, scores[:, d, at * P:(at + 1) * P], V[:, j, :], n == 0, False)
                        for f in range(2):
                            m = mm(o, (q_dec if d == 0 else kT)[:, f, i * P:(i + 1) * P], state[:, d, f, :], False, f == 1)
                    m.then_inc(score_done, 1)
            transposes(HEADS - 1)
            pe.wait_ge(y_lo_ready, 2 * HEADS)
            out_phase_norm(RET_OUT, S_RET_OUT, KT, (y_hi, y_lo), False, None, 4)
            ffn(FFN1, S_FFN1, 1, False)
            for n in range(8):
                t, jj = n // 4, n % 4
                s = S_OUT + n
                if n == 2:
                    sum_squares(5, 1)
                slot_free(s, None)
                pe.wait_ge(fin_ready, n + 1)
                for tt in range(2):
                    for a in range(2):
                        m = nc.tensor.transpose(slot(s % 2, 0)[:, tt * PART + a * P:tt * PART + (a + 1) * P],
                                                first_squares(t, jj)[:, a, tt * P:(tt + 1) * P], ident[:])
                m.then_inc(xT_done, 1)

        @block.scalar
        def _(act):
            A = nc.scalar.activation

            def split_hi(unit, r):
                if isinstance(unit, int):
                    if unit >= UNITS:
                        return
                    act.wait_ge(raw_ready[r], 16 * (unit // RING + 1))
                    if unit >= RING:
                        act.wait_ge(unit_done, unit - (RING - 1))
                A(w_hi[:, r, :], w_raw[:, r, :], ACT.Copy).then_inc(hi_ready, 1)

            def split_hi_at(base, i, off):
                unit = base + off
                if isinstance(i, int):
                    return split_hi(unit + 4 * i, unit % RING)
                act.wait_ge(raw_ready[unit % RING], 16 * i + 16 * (unit // RING + 1))
                act.wait_ge(unit_done, 4 * i + (unit - (RING - 1)))
                A(w_hi[:, unit % RING, :], w_raw[:, unit % RING, :], ACT.Copy).then_inc(hi_ready, 1)

            def bank(p, b):
                return ps[:, 3 * p + b, :]

            def square(norm, u, w, t=None):
                cols = slice(0, w) if t is None else part(t)
                n = sq_count(norm, u, t)
                if u >= FULL and t is not None and u - 2 < FULL and norm != 2:
                    act.wait_ge(ssq_ready, add_count(norm, u - 2))
                elif u >= 3:
                    act.wait_ge(ssq_ready, add_count(norm, u - 2, t))
                A((rstd if u == 0 else sq[:, u % 2])[:, cols], X[:, u, cols], ACT.Square).then_inc(sq_ready, 1)

            def root(norm, t):
                act.wait_ge(sq_summed, PARTS_BEFORE[norm] + t + 1)
                A(rstd[:, part(t)], stat_bank(norm, t), ACT.Sqrt, bias=eps[:, 0:1]).then_inc(std_ready, 1)

            def norm_hi(norm, t, tiles):
                n_at = KT * (PARTS_BEFORE[norm] + t)

                def hi(j):
                    b = norm_buf[j % 4][:, part(t)]
                    if norm == 1:
                        act.wait_ge(modulated, KT * t + j + 1)
                        A(H_hi[:, j, part(t)], b, ACT.Copy).then_inc(h_hi_ready, 1)
                    else:
                        A(H_hi[:, j, part(t)], b, ACT.Identity, bias=shift(norm, t, j)).then_inc(h_hi_ready, 1)
                for n, j in enumerate(tiles):
                    act.wait_ge(scaled, n_at + j + 1)
                    if norm != 1:
                        hi(j)
                        continue
                    b = norm_buf[j % 4][:, part(t)]
                    A(b, b, ACT.Silu, scale=par[:, LN_G + j:LN_G + j + 1], bias=par[:, LN_B + j:LN_B + j + 1]) \
                        .then_inc(modulated, 1)
                    if n:
                        hi(tiles[n - 1])
                if norm == 1 and tiles:
                    hi(tiles[-1])

            def ada_copy(m):
                act.wait_ge(ada_done, 2 * m + 2)
                if not isinstance(m, int) or m:
                    act.wait_ge(ada_T, m)
                A(ada_row(m), ps[:, 6, :], ACT.Copy).then_inc(ada_row_ready, 1)

            for t in range(LT):
                act.dma_start(xin[:, t, :], x[0, t * P:(t + 1) * P, :]).then_inc(tokens_in[t // 2], 16)
            for t in range(CT):
                act.dma_start(xin[:, LT + t, :], ctx_tok[0, t * P:(t + 1) * P, :]).then_inc(tokens_in[2], 16)
            act.wait_ge(filled, 4)
            act.wait_ge(par_ready, 1)
            for v in range(2):
                A(silu_c[:, :, v], par[:, C_COL + 8 * v:C_COL + 8 * v + 8], ACT.Silu).then_inc(silu_c_ready, 1)
            def token_squares(t):
                for jj in range(KT // 2):
                    s = S_XT + 4 * t + jj
                    act.wait_ge(slot_read[s % 2], s // 2 + 1)
                    if jj >= 2:
                        act.wait_ge(stat_used, 3 * t + jj - 1)
                    A(first_squares(t, jj), X[:, 2 * jj:2 * jj + 2, part(t)], ACT.Square).then_inc(stat_sq, 1)
            token_squares(0)
            token_squares(1)
            root(0, 0)
            token_squares(2)
            root(0, 1)
            ada_copy(0)
            root(0, 2)
            ada_copy(1)
            split_hi(0, 0)
            split_hi(1, 1)
            ada_copy(2)
            split_hi(2, 2)
            ada_copy(3)
            A(tap_hi[:], par[:, DW_W:DW_W + PE_TAPS * KT], ACT.Copy).then_inc(taps_split, 1)
            for t in range(3):
                norm_hi(0, t, range(KT))
            act.wait_ge(taps_split, 2)
            act.wait_ge(h_lo_ready, 3 * KT)

            def pw1_body(i):
                for q in range(2):
                    split_hi_at(2 * PW1, i, 2 * q + 3)
                    ada_copy(4 * i + (2 * q + 4))
                    split_hi_at(2 * PW1, i, 2 * q + 4)
                    act.wait_ge(unit_done, 4 * i + (2 * q + 2))
                    b = par[:, ds(2 * i + (PW1_B + KT + q), 1)]
                    A(rstd[:, LATS], bank(0, 1), ACT.Sigmoid, bias=b)
                    A(rstd[:, CTXS], bank(0, 2)[:, CTX:], ACT.Sigmoid, bias=b).then_inc(sig_ready, 1)
                    ada_copy(4 * i + (2 * q + 5))
                    for k in range(PE_TAPS):
                        A(diag_hi[:, q, k, :], ident[:], ACT.Copy, scale=tap_hi[:, ds(2 * i + (KT * k + q), 1)].bitcast(F32))
                        a = A(diag_lo[:, q, k, :], ident[:], ACT.Copy, scale=tap_lo[:, ds(2 * i + (KT * k + q), 1)])
                    a.then_inc(diag_ready, 1)
                    act.wait_ge(slot_read[0], 2 * i + (S_PW1 // 2 + q + 1))
                    if not (isinstance(i, int) and q == 0):
                        act.wait_ge(conv_done, 2 * i + q)
                    A(u_hi[:], upad[q], ACT.Copy).then_inc(u_hi_ready, 1)
            pw1_body(0)
            with act.Fori(1, KT // 2) as i:
                pw1_body(i)
            ada_copy(20)
            split_hi(2 * PW2 + 3, 3)
            ada_copy(21)
            def center_squares(t):
                for j in range(KT):
                    if t == 0 or j < KT - 1:
                        act.wait_ge(centered, (0, 8, 15)[t] + j + 1)
                    else:
                        act.wait_ge(slot_read[t - 1], S_LN // 2 + 1)
                    if j >= 4:
                        act.wait_ge(stat_used, 9 + 7 * t + j - 3)
                    A(norm_buf[j % 4][:, part(t)], conv_part(j, t), ACT.Square).then_inc(stat_sq, 1)

            center_squares(0)
            center_squares(1)
            root(1, 0)
            center_squares(2)
            root(1, 1)
            root(1, 2)
            norm_hi(1, 0, range(KT))

            def gated(p, both, gates, bias=None):
                for m, toks in groups(both):
                    a = A(tmp[:, p, toks], bank(p, 0) if m == 0 else bank(p, 2)[:, 0:CTX], ACT.Identity,
                          scale=gates[m], bias=0.0 if bias is None else bias[m])
                a.then_inc(slot_read[p], 1)

            def gated_part(p, b, t, gates, bias=None):
                A(tmp[:, p, part(t)], bank(p, b)[:, 0:PART], ACT.Identity, scale=gates[t // 2],
                  bias=0.0 if bias is None else bias[t // 2]).then_inc(slot_read[p], 1)

            def out_phase(blk, s, x_at, both, layer, gate_at):
                with act.Fori(0, 2) as i:
                    for u in range(4):
                        p = u % 2
                        split_hi_at(2 * blk, i, u + 3)
                        act.wait_ge(unit_done, 4 * i + (2 * blk + u + 1))
                        act.wait_ge(x_updated, 4 * i + (x_at + u - 1))
                        g = [mod[:, layer, ds(4 * i + (gate_at + u), 1), m] for m in range(2)]
                        gated(p, both, g)

            def by_parts(unit, first, s, x_at, e0, parts, layer, gate_at, norm, done_at, beside, bias=False):
                for t in range(parts):
                    for i in range(4):
                        u, n = first + i, 4 * t + i
                        e = e0 + n
                        p = (s + e) % 2
                        if t == parts - 1:
                            act.wait_ge(unit_done, unit + i + 1)
                        else:
                            act.wait_ge(part_done, done_at + n + 1)
                        if x_at + e - 1 > 0:
                            act.wait_ge(x_updated, x_at + e - 1)
                        g = [mod[:, layer, gate_at + u, m:m + 1] for m in range(2)]
                        gated_part(p, n // 2 % 3, t, g, [pw2_gb[:, u, m:m + 1] for m in range(2)] if bias else None)
                        last = t == parts - 1 and i == 3
                        if not last:
                            beside(t, i)
                        act.wait_ge(x_updated, x_at + e + 1)
                        square(norm, u, None, t)
                        if last:
                            beside(t, i)
                        if t == parts - 1 and (i < 3 or first == 0):
                            split_hi(unit + 4 + i, i)

            def tail_steps(norm):
                def beside(t, i):
                    if t and i == 0:
                        root(norm, t - 1)
                    elif t and norm < 5:
                        norm_hi(norm, t - 1, TAIL_TILES[i])
                return beside

            def norm_end(unit, norm, t):
                split_hi(unit + 11, 3)
                if norm < 5:
                    root(norm, t)
                    norm_hi(norm, t, range(KT))

            def out_phase_norm(blk, s, x_at, both, layer, gate_at, norm):
                for u in range(FULL):
                    p = u % 2
                    split_hi(2 * blk + u + 3, (u + 3) % RING)
                    act.wait_ge(unit_done, 2 * blk + u + 1)
                    act.wait_ge(x_updated, x_at + u - 1)
                    gated(p, both, [mod[:, layer, gate_at + u, m:m + 1] for m in range(2)])
                    act.wait_ge(x_updated, x_at + u + 1)
                    square(norm, u, TOK if both else LAT)
                split_hi(2 * blk + 7, 3)
                by_parts(2 * blk + FULL, FULL, s, x_at, FULL, 3 if both else 2, layer, gate_at, norm, PARTS_DONE[norm],
                         tail_steps(norm))
                norm_end(2 * blk, norm, 2 if both else 1)

            act.wait_ge(mod_ready, 5)

            def ln_steps(t, i):
                if t < 2:
                    norm_hi(1, t + 1, LN_TILES[i])
                if (t, i) in ((0, 1), (1, 1)):
                    ada_copy(22 + t)
            by_parts(2 * PW2, 0, S_PW2, 0, 0, 3, 0, 16, 2, 0, ln_steps, bias=True)
            by_parts(2 * PW2 + FULL, FULL, S_PW2, 0, 3 * FULL, 3, 0, 16, 2, 2 * FULL, tail_steps(2), bias=True)
            norm_end(2 * PW2, 2, 2)

            def ffn(blk, s, layer, both, x_at):
                f = 0
                for c_no, n in enumerate(CHUNKS):
                    act.wait_ge(x_updated, x_at)

                    def pairs(i):
                        for q in range(2):
                            g_at = layer * FT + f + q
                            if not (isinstance(i, int) and q == 0):
                                split_hi_at(2 * blk, i, 2 * q + 3)
                            split_hi_at(2 * blk, i, 2 * q + 4)
                            act.wait_ge(unit_done, 4 * i + (2 * blk + 2 * q + 2))
                            w1 = par[:, ds(2 * i + (FFN_DW_W + layer * P + FT + f + q), 1)]
                            b = par[:, ds(2 * i + (FFN_DW_B + g_at), 1)]
                            a = A(tmp[:, q, LATS], bank(q, 1), ACT.Identity, scale=w1, bias=b)
                            if both:
                                a = A(tmp[:, q, CTXS], bank(q, 2)[:, CTX:], ACT.Identity, scale=w1, bias=b)
                            a.then_inc(g_first, 1)
                            w = TOK if both else LAT
                            act.wait_ge(g_taps, (8 if both else 4) * i + (taps_at(layer) + (4 if both else 2) * (f + q + 1)))
                            A(tmp[:, q, 0:w], tmp[:, q, 0:w], ACT.Silu).then_inc(g_silu, 1)
                            act.wait_ge(slot_read[q], i + (s // 2 + 1))
                            A(mid_hi[:, ds(2 * i + q, 1), 0:w], m32[:, q:q + 1, 0:w], ACT.Copy).then_inc(mid_hi_ready, 1)
                    if c_no == 0:
                        pairs(0)
                    with act.Fori(1 if c_no == 0 else 0, n // 2) as i:
                        pairs(i)
                    f += n
                    blk, s = blk + n, s + n
                    if c_no < len(CHUNKS) - 1:
                        out_phase(blk, s, x_at, both, layer, 40)
                    else:
                        out_phase_norm(blk, s, x_at, both, layer, 40, 3 + 2 * layer)
                    blk, s, x_at = blk + 4, s + KT, x_at + KT

            ffn(FFN0, S_FFN0, 0, True, X_FFN0)

            act.wait_ge(consts_in, 16 * 5)
            A(ngam[:], decay_log[:], ACT.Exp).then_inc(lg_step, 1)
            act.wait_ge(lg_step, 2)
            for h in range(HEADS):
                for d in range(2):
                    A(zeta[:, h, d, :], tcol[:, 2 + 2 * d:4 + 2 * d], ACT.Exp,
                      scale=lgam[:, HEADS * d + h:HEADS * d + h + 1]).then_inc(zeta_ready, 1)
            def y_parts(h):
                act.wait_ge(yT_done, h + 1)
                for f in range(2):
                    A(y_hi[:, 2 * h + f, :], ps[:, 6 + f, :], ACT.Copy).then_inc(y_hi_ready, 1)

            for h in range(HEADS):
                blk, s = RET + 5 * h, S_RET + HEAD_USES * h
                ab = slice(h, h + 1), slice(HEADS + h, HEADS + h + 1)
                u = 2 * blk
                if h:
                    split_hi(u + 3, (u + 3) % RING)
                act.wait_ge(age_ready, 2 * h + 2)
                A(decay[:, 0, :], decay[:, 0, :], ACT.Exp, scale=lgam[:, ab[0]])
                A(decay[:, 1, :], decay[:, 1, :], ACT.Exp, scale=ngam[:, ab[1]]).then_inc(decay_exp, 1)
                split_hi(u + 4, (u + 4) % RING)
                split_hi(u + 5, (u + 5) % RING)
                if h:
                    y_parts(h - 1)
                split_hi(u + 6, (u + 6) % RING)
                act.wait_ge(unit_done, 2 * (blk + 2) + 2)
                A(V[:].rearrange("p a b -> p (a b)"), ps[:, 0:2, :].rearrange("p a b -> p (a b)"), ACT.Copy)
                A(vctx.rearrange("p a b -> p (a b)"), ps[:, 2, :], ACT.Copy).then_inc(slot_read[0], 1)
                split_hi(u + 7, (u + 7) % RING)
                split_hi(u + 8, (u + 8) % RING)
                act.wait_ge(score_done, 7 * h + 1)
                A(state[:].rearrange("p d f v -> p (d f v)"), ps[:, 3:5, :].rearrange("p a b -> p (a b)"),
                  ACT.Copy).then_inc(slot_read[1], 1)
                act.wait_ge(score_read, LT * (h + 1))
                A(decay[:, 0, :], iota[:], ACT.Exp, scale=lgam[:, ab[0]], bias=lgam[:, ab[0]])
                A(decay[:, 1, :], iota[:], ACT.Exp, scale=ngam[:, ab[1]], bias=lgam512[:, ab[1]]).then_inc(decay_exp, 1)
                for d in range(2):
                    act.wait_ge(unit_done, 2 * (blk + 3 + d) + 2)
                    if 2 * h + d >= 1:
                        act.wait_ge(y_step, 3 * h + d)
                    A(gate.rearrange("p a b -> p (a b)"), ps[:, 0:2, :].rearrange("p a b -> p (a b)"), ACT.Silu) \
                        .then_inc(slot_read[0], 1)
                    if d == 0:
                        split_hi(u + 9, (u + 9) % RING)
                        split_hi(u + 10, (u + 10) % RING)
                    else:
                        split_hi(u + 11, (u + 11) % RING)
                        split_hi(u + 12, (u + 12) % RING)
                    act.wait_ge(gn_stats, 2 * (2 * h + d) + 2)
                    A(gn_mv[:, :, 1], gn_mv[:, :, 1], ACT.Sqrt, bias=eps[:, 1:2]).then_inc(gn_std, 1)
            y_parts(HEADS - 1)
            out_phase_norm(RET_OUT, S_RET_OUT, X_RET_OUT, False, 1, 16, 4)
            ffn(FFN1, S_FFN1, 1, False, X_FFN1)
            for n in range(8):
                t, jj = n // 4, n % 4
                p = n % 2
                if n == 2:
                    root(5, 1)
                act.wait_ge(xT_done, 12 + n + 1)
                A(otok[:, 2 * t:2 * t + 2, 2 * jj * P:2 * (jj + 1) * P],
                  bank(p, 0).rearrange("p (t n) -> p t n", t=2), ACT.Copy).then_inc(slot_read[p], 1)

        @block.vector
        def _(dve):
            v = nc.vector

            def bank(p, b):
                return ps[:, 3 * p + b, :]

            def split_lo(unit, r):
                if isinstance(unit, int) and unit >= UNITS:
                    return
                dve.wait_ge(hi_ready, unit + 1)
                v.tensor_tensor(w_lo[:, r, :], w_raw[:, r, :], w_hi[:, r, :].bitcast(F32), ALU.subtract) \
                    .then_inc(lo_ready, 1)

            def recip(norm, t):
                g = PARTS_BEFORE[norm] + t
                dve.wait_ge(std_ready, g + 1)
                v.reciprocal(rstd[:, part(t)], rstd[:, part(t)]).then_inc(rstd_ready, 1)
                dve.wait_ge(rstd_ready, g + 1)

            def add_squares(norm, u, w, t=None):
                cols = slice(0, w) if t is None else part(t)
                dve.wait_ge(sq_ready, sq_count(norm, u, t))
                n = add_count(norm, u, t)
                if n > 1:
                    dve.wait_ge(ssq_ready, n - 1)
                v.tensor_tensor(rstd[:, cols], rstd[:, cols], sq[:, u % 2, cols], ALU.add).then_inc(ssq_ready, 1)

            def norm_scale(norm, t, tiles):
                for j in tiles:
                    b = norm_buf[j % 4][:, part(t)]
                    if j >= 4:
                        dve.wait_ge(h_lo_ready, KT * (PARTS_BEFORE[norm] + t) + j - 3)
                    if norm == 1:
                        o = v.tensor_tensor(b, conv_part(j, t), rstd[:, part(t)], ALU.mult)
                    else:
                        layer, half, m = modulation_of(norm, t)
                        o = v.scalar_tensor_tensor(b, X[:, j, part(t)], gain[:, layer, half, j, m:m + 1], rstd[:, part(t)],
                                                   ALU.mult, ALU.mult)
                    o.then_inc(scaled, 1)

            def norm_lo(norm, t, tiles):
                for j in tiles:
                    dve.wait_ge(h_hi_ready, KT * (PARTS_BEFORE[norm] + t) + j + 1)
                    dst, b, hi = H_lo[:, j, part(t)], norm_buf[j % 4][:, part(t)], H_hi[:, j, part(t)].bitcast(F32)
                    if norm == 1:
                        o = v.tensor_tensor(dst, b, hi, ALU.subtract)
                    else:
                        o = v.scalar_tensor_tensor(dst, b, shift(norm, t, j), hi, ALU.add, ALU.subtract)
                    o.then_inc(h_lo_ready, 1)

            def normed(norm, t):
                norm_scale(norm, t, range(3))
                for j in range(KT):
                    if j + 3 < KT:
                        norm_scale(norm, t, [j + 3])
                    norm_lo(norm, t, [j])

            def two(ap):
                return ap.unsqueeze(2).to_broadcast([P, ap.shape[1], 2])

            def ada_sum(m, layer, g):
                dve.wait_ge(ada_T, m + 1)
                v.tensor_reduce(mod[:, layer, GROUP * g:GROUP * (g + 1), :],
                                ps[:, 7, :].rearrange("p (t j c) -> p t c j", j=4, c=32)[:, :, 0:2, :],
                                mybir.AxisListType.X, ALU.add).then_inc(mod_sum, 1)

            def modulation(m, layer, t0, t1, at):
                dve.wait_ge(mod_sum, m + 1)
                v.tensor_tensor(mod[:, layer, t0:t1, :], mod[:, layer, t0:t1, :],
                                two(par[:, ADA_B + 48 * layer + t0:ADA_B + 48 * layer + t1]), ALU.add) \
                    .then_inc(mod_ready, 1)
                at += 1
                dve.wait_ge(mod_ready, at)
                for sub, (col, g) in enumerate(((8, NORM1), (32, NORM2))):
                    if t0 <= col < t1:
                        v.scalar_tensor_tensor(gain[:, layer, sub], mod[:, layer, col:col + KT, :], 1.0,
                                               two(par[:, g + KT * layer:g + KT * (layer + 1)]), ALU.add, ALU.mult) \
                            .then_inc(mod_ready, 1)

            for t in range(3):
                if t == 2:
                    dve.wait_ge(par_T, 1)
                    v.tensor_copy(par[:, 0:244], ps[:, 6, 0:244])
                    v.tensor_copy(par[:, 256:504], ps[:, 6, 256:504])
                    for layer in range(DEPTH):
                        o = v.tensor_copy(par[:, FFN_DW_W + P * layer:FFN_DW_W + P * layer + 66],
                                          ps[:, 7, P * layer:P * layer + 66])
                    o.then_inc(par_ready, 1)
                for jj in range(KT // 2):
                    s = S_XT + 4 * t + jj
                    dve.wait_ge(xT_done, s + 1)
                    v.tensor_copy(X[:, 2 * jj:2 * jj + 2, part(t)], bank(s % 2, 0).rearrange("p (a n) -> p a n", a=2)) \
                        .then_inc(slot_read[s % 2], 1)
            for p in range(2):
                dve.wait_ge(slot_read[p], S_PW1 // 2)
            dve.wait_ge(par_ready, 1)
            recip(0, 0)
            recip(0, 1)
            ada_sum(0, 0, 0)
            recip(0, 2)
            ada_sum(1, 0, 1)
            split_lo(0, 0)
            split_lo(1, 1)
            ada_sum(2, 0, 2)
            split_lo(2, 2)
            ada_sum(3, 0, 3)
            modulation(3, 0, 0, 16, 0)
            dve.wait_ge(taps_split, 1)
            v.tensor_tensor(tap_lo[:], par[:, DW_W:DW_W + PE_TAPS * KT], tap_hi[:].bitcast(F32), ALU.subtract) \
                .then_inc(taps_split, 1)
            dve.wait_ge(mod_ready, 2)
            for t in range(3):
                normed(0, t)
            dve.wait_ge(h_lo_ready, 3 * KT)
            for b in upad:
                for lo, hi in ((0, PAD), (PAD + LAT, CTX_PAD), (CTX_PAD + CTX, PADW)):
                    o = v.memset(b[:, lo:hi], 0.0)
            o.then_inc(padded, 1)

            def taps(b, ks):
                row = conv[:, b, 0:OUTW]
                for k in ks:
                    n = b * DVE_TAPS + k - PE_TAPS
                    w = par[:, DW_W + KT * k + b:DW_W + KT * k + b + 1]
                    if k == PE_TAPS:
                        o = v.tensor_scalar(row, upad[b % 2][:, k:k + OUTW], w, None, ALU.mult)
                    else:
                        dve.wait_ge(tap_done, n)
                        o = v.scalar_tensor_tensor(row, upad[b % 2][:, k:k + OUTW], w, row, ALU.mult, ALU.add)
                    o.then_inc(tap_done, 1)

            def merge(b):
                dve.wait_ge(conv_done, b + 1)
                dve.wait_ge(tap_done, DVE_TAPS * (b + 1))
                bias = par[:, DW_B + b:DW_B + b + 1]
                v.scalar_tensor_tensor(conv[:, b, 0:LAT], bank(1, 0), bias, conv[:, b, 0:LAT], ALU.add, ALU.add)
                v.scalar_tensor_tensor(conv[:, b, CTX_OUT:OUTW], bank(1, 2)[:, 0:CTX], bias, conv[:, b, CTX_OUT:OUTW],
                                       ALU.add, ALU.add).then_inc(slot_read[1], 1)

            for b in range(KT):
                split_lo(2 * b + 3, (2 * b + 3) % RING)
                split_lo(2 * b + 4, (2 * b + 4) % RING)
                dve.wait_ge(sig_ready, b + 1)
                if b == 0:
                    dve.wait_ge(padded, 1)
                if b >= 2:
                    dve.wait_ge(u_lo_ready, b - 1)
                bias = par[:, PW1_B + b:PW1_B + b + 1]
                v.scalar_tensor_tensor(upad[b % 2][:, PAD:PAD + LAT], bank(0, 0), bias, rstd[:, LATS], ALU.add, ALU.mult)
                v.scalar_tensor_tensor(upad[b % 2][:, CTX_PAD:CTX_PAD + CTX], bank(0, 2)[:, 0:CTX], bias, rstd[:, CTXS],
                                       ALU.add, ALU.mult).then_inc(slot_read[0], 1)
                dve.wait_ge(slot_read[0], S_PW1 // 2 + b + 1)
                ada_sum(4 + 2 * b, 0, 4 + b)
                taps(b, range(PE_TAPS, PE_TAPS + 11))
                if b:
                    merge(b - 1)
                dve.wait_ge(u_hi_ready, b + 1)
                v.tensor_tensor(u_lo[:], upad[b % 2], u_hi[:].bitcast(F32), ALU.subtract).then_inc(u_lo_ready, 1)
                ada_sum(5 + 2 * b, 1, b)
                taps(b, range(PE_TAPS + 11, TAPS))
            merge(KT - 1)
            ada_sum(20, 1, 8)
            split_lo(2 * PW2 + 3, 3)
            modulation(18, 0, 16, 48, 2)
            v.tensor_tensor(pw2_gb[:], mod[:, 0, 16:24, :], two(par[:, PW2_B:PW2_B + KT]), ALU.mult) \
                .then_inc(mod_ready, 1)

            def center(t):
                for j in range(KT):
                    last = j == KT - 1
                    mean = bank(0, 0)[:, part(t)] if t < 2 else bank(0, 2)[:, 0:PART]
                    v.tensor_tensor(conv_part(j, t), conv_part(j, t), mean, ALU.subtract) \
                        .then_inc(slot_read[t - 1] if last and t else centered, 1)
            dve.wait_ge(mu_summed, 1)
            for t in range(3):
                center(t)
            ada_sum(21, 1, 9)
            dve.wait_ge(centered, 8)
            dve.wait_ge(slot_read[0], S_LN // 2 + 1)
            dve.wait_ge(slot_read[1], S_LN // 2 + 1)
            recip(1, 0)
            normed(1, 0)
            recip(1, 1)
            recip(1, 2)

            def residual(s, x_at, i, u, both, col):
                w = TOK if both else LAT
                p = (s + u) % 2
                if isinstance(i, int) and i == 0:
                    dve.wait_ge(slot_read[p], (s + u) // 2 + 1)
                else:
                    dve.wait_ge(slot_read[p], 2 * i + ((s + u) // 2 + 1))
                row = X[:, col, 0:w]
                if not isinstance(col, int):
                    row = row.rearrange("p a b -> p (a b)")
                v.tensor_tensor(row, row, tmp[:, p, 0:w], ALU.add).then_inc(x_updated, 1)

            def residual_part(s, x_at, e, u, t):
                p = (s + e) % 2
                dve.wait_ge(slot_read[p], (s + e) // 2 + 1)
                v.tensor_tensor(X[:, u, part(t)], X[:, u, part(t)], tmp[:, p, part(t)], ALU.add).then_inc(x_updated, 1)

            def out_phase(blk, s, x_at, both):
                with dve.Fori(0, 2) as i:
                    for u in range(4):
                        split_lo(4 * i + (2 * blk + u + 3), (u + 3) % RING)
                        dve.wait_ge(x_updated, x_at - KT + 4 * i + (u + 1))
                        residual(s, x_at, i, u, both, ds(4 * i + u, 1))

            def by_parts(unit, first, s, x_at, e0, parts, norm, before, after):
                for t in range(parts):
                    for i in range(4):
                        u, e = first + i, e0 + 4 * t + i
                        before(t, i)
                        if x_at and t == 0:
                            dve.wait_ge(x_updated, x_at - KT + u + 1)
                        residual_part(s, x_at, e, u, t)
                        last = t == parts - 1 and i == 3
                        if not last:
                            after(t, i)
                        if u:
                            add_squares(norm, u, None, t)
                        if last:
                            after(t, i)
                        if t == parts - 1 and (i < 3 or first == 0):
                            split_lo(unit + 4 + i, i)

            def tail_before(norm):
                def step(t, i):
                    if t and i:
                        norm_scale(norm, t - 1, TAIL_TILES[i])
                return step

            def tail_after(norm):
                def step(t, i):
                    if t:
                        if i == 0:
                            recip(norm, t - 1)
                        else:
                            norm_lo(norm, t - 1, TAIL_TILES[i])
                return step

            def final_step(t, i):
                if t and i == 0:
                    recip(5, 0)
                elif t and i < 3:
                    final_pair(i - 1)

            def final_pair(n):
                t, jj = n // 4, n % 4
                if n >= 2:
                    dve.wait_ge(xT_done, 12 + n - 1)
                for a in range(2):
                    j = 2 * jj + a
                    o = v.scalar_tensor_tensor(first_squares(t, n)[:, a, :], X[:, j, part(t)],
                                               par[:, FINAL_G + j:FINAL_G + j + 1], rstd[:, part(t)], ALU.mult, ALU.mult)
                o.then_inc(fin_ready, 1)

            def out_phase_norm(blk, s, x_at, both, norm):
                for u in range(FULL):
                    split_lo(2 * blk + u + 3, (u + 3) % RING)
                    dve.wait_ge(x_updated, x_at - KT + u + 1)
                    residual(s, x_at, 0, u, both, u)
                    if u:
                        add_squares(norm, u, TOK if both else LAT)
                split_lo(2 * blk + 7, 3)
                final = norm == 5
                by_parts(2 * blk + FULL, FULL, s, x_at, FULL, 3 if both else 2, norm,
                         (lambda t, i: None) if final else tail_before(norm), final_step if final else tail_after(norm))
                split_lo(2 * blk + 11, 3)
                if not final:
                    recip(norm, 2 if both else 1)
                    normed(norm, 2 if both else 1)

            def ln_before(t, i):
                if t < 2:
                    norm_scale(1, t + 1, LN_TILES[i])

            def ln_after(t, i):
                if t < 2:
                    norm_lo(1, t + 1, LN_TILES[i])
                if (t, i) in ((0, 2), (1, 2)):
                    ada_sum(22 + t, 1, 10 + t)
                if (t, i) == (1, 3):
                    modulation(23, 1, 0, 48, 5)

            by_parts(2 * PW2, 0, S_PW2, 0, 0, 3, 2, ln_before, ln_after)
            dve.wait_ge(mod_ready, 8)
            by_parts(2 * PW2 + FULL, FULL, S_PW2, 0, 3 * FULL, 3, 2, tail_before(2), tail_after(2))
            split_lo(2 * PW2 + 11, 3)
            recip(2, 2)
            normed(2, 2)

            def ffn(blk, s, layer, both, x_at):
                f = 0
                w = TOK if both else LAT
                steps = 4 if both else 2
                for c_no, n in enumerate(CHUNKS):
                    def pairs(i):
                        for q in range(2):
                            if not (isinstance(i, int) and q == 0):
                                split_lo(4 * i + (2 * blk + 2 * q + 3), (2 * q + 3) % RING)
                            split_lo(4 * i + (2 * blk + 2 * q + 4), (2 * q + 4) % RING)
                            t_at = taps_at(layer) + steps * (f + q)
                            wt = [par[:, ds(2 * i + (FFN_DW_W + layer * P + FT * k + f + q), 1)] for k in (0, 2)]
                            t = tmp[:, q]
                            dve.wait_ge(g_first, 2 * i + (layer * FT + f + q + 1))
                            streams = [(bank(q, 1), 0, LAT)] + ([(bank(q, 2)[:, CTX:], LAT, CTX)] if both else [])
                            for b, t0, m in streams:
                                v.scalar_tensor_tensor(t[:, t0 + 1:t0 + m], b[:, 0:m - 1], wt[0], t[:, t0 + 1:t0 + m],
                                                       ALU.mult, ALU.add).then_inc(g_taps, 1)
                            for n_s, (b, t0, m) in enumerate(streams):
                                dve.wait_ge(g_taps, 2 * steps * i + (t_at + n_s + 1))
                                v.scalar_tensor_tensor(t[:, t0:t0 + m - 1], b[:, 1:m], wt[1], t[:, t0:t0 + m - 1],
                                                       ALU.mult, ALU.add).then_inc(g_taps, 1)
                            dve.wait_ge(g_silu, 2 * i + (layer * FT + f + q + 1))
                            o = v.tensor_tensor(m32[:, q, LATS], bank(q, 0), tmp[:, q, LATS], ALU.mult)
                            if both:
                                o = v.tensor_tensor(m32[:, q, CTXS], bank(q, 2)[:, 0:CTX], tmp[:, q, CTXS], ALU.mult)
                            o.then_inc(slot_read[q], 1)
                            dve.wait_ge(mid_hi_ready, 2 * i + (layer * FT + f + q + 1))
                            v.tensor_tensor(mid_lo[:, ds(2 * i + q, 1), 0:w], m32[:, q:q + 1, 0:w],
                                            mid_hi[:, ds(2 * i + q, 1), 0:w].bitcast(F32), ALU.subtract) \
                                .then_inc(mid_lo_ready, 1)
                    if c_no == 0:
                        pairs(0)
                    with dve.Fori(1 if c_no == 0 else 0, n // 2) as i:
                        pairs(i)
                    f += n
                    blk, s = blk + n, s + n
                    if c_no < len(CHUNKS) - 1:
                        out_phase(blk, s, x_at, both)
                    else:
                        out_phase_norm(blk, s, x_at, both, 3 + 2 * layer)
                    blk, s, x_at = blk + 4, s + KT, x_at + KT

            ffn(FFN0, S_FFN0, 0, True, X_FFN0)

            dve.wait_ge(lg_step, 1)
            v.tensor_scalar(lgam512[:], ngam[:], -float(LAT), None, ALU.mult)
            v.tensor_scalar(lgam[:], ngam[:], -1.0, None, ALU.mult).then_inc(lg_step, 1)

            def grid(ap, parts=slice(0, P)):
                return ap[parts].rearrange("p (r c) -> p r c", c=GRID_W)

            def rotate(p, dst, scale, n, frees=None):
                for f in range(2):
                    n_at = n + 4 * f
                    if f == 0:
                        cs = [rrow[:, a, :].unsqueeze(2).to_broadcast([P, ROWS, GRID_W]) for a in range(2)]
                    else:
                        cs = [rcol[:, a, :].unsqueeze(1).to_broadcast([P, ROWS, GRID_W]) for a in range(2)]
                    if n_at:
                        dve.wait_ge(rot_step, n_at)
                    src = bank(p, f)
                    v.scalar_tensor_tensor(grid(cosd), grid(src), scale, cs[0], ALU.mult, ALU.mult).then_inc(rot_step, 1)
                    for a in range(2):
                        to, frm = slice(64 * a, 64 * a + 64), slice(64 - 64 * a, 128 - 64 * a)
                        o = v.scalar_tensor_tensor(grid(rot, to), grid(src, frm), scale, cs[1][to], ALU.mult, ALU.mult)
                        if f == 1 and a == 1 and frees is not None:
                            o.then_inc(slot_read[p], 1)
                            dve.wait_ge(slot_read[p], frees)
                        else:
                            o.then_inc(rot_step, 1)
                            dve.wait_ge(rot_step, n_at + 2 + a)
                    v.tensor_tensor(dst[:, f, :], cosd, rot, ALU.add).then_inc(rot_step, 1)

            def y_parts(h):
                dve.wait_ge(y_hi_ready, 2 * h + 2)
                for f in range(2):
                    v.tensor_tensor(y_lo[:, 2 * h + f, :], ps[:, 6 + f, :], y_hi[:, 2 * h + f, :].bitcast(F32),
                                    ALU.subtract).then_inc(y_lo_ready, 1)

            for h in range(HEADS):
                blk, s = RET + 5 * h, S_RET + HEAD_USES * h
                u = 2 * blk
                if h:
                    split_lo(u + 3, (u + 3) % RING)
                if h == 0:
                    dve.wait_ge(ages_in, 16 * 3)
                if h:
                    dve.wait_ge(qdec_ready, 2 * h)
                v.tensor_scalar(decay[:, 0, :], iota[:], tcol[:, 0:1], 0.0, ALU.subtract, ALU.max).then_inc(age_ready, 1)
                v.tensor_scalar(decay[:, 1, :], iota[:], tcol[:, 1:2], 0.0, ALU.subtract, ALU.min).then_inc(age_ready, 1)
                split_lo(u + 4, (u + 4) % RING)
                dve.wait_ge(unit_done, 2 * blk + 2)
                if h:
                    dve.wait_ge(yT_done, h)
                rotate(0, qT, DH ** -0.5, 15 * h, s // 2 + 1)
                split_lo(u + 5, (u + 5) % RING)
                if h:
                    y_parts(h - 1)
                split_lo(u + 6, (u + 6) % RING)
                dve.wait_ge(decay_exp, 2 * h + 1)
                v.tensor_tensor(decay[:, 0, 0:P], decay[:, 0, 0:P], tup[:], ALU.mult)
                v.tensor_tensor(decay[:, 1, LAT - P:LAT], decay[:, 1, LAT - P:LAT], tlow[:], ALU.mult) \
                    .then_inc(decay_ready, 1)
                dve.wait_ge(unit_done, 2 * (blk + 1) + 2)
                if h == 0:
                    dve.wait_ge(zeta_ready, 2 * HEADS)
                rotate(1, kT, 1.0, 15 * h + 7)
                for t in range(CT):
                    for d in range(2):
                        o = v.tensor_scalar(kctx[:, d, t, :], bank(1, 2)[:, t * DH:(t + 1) * DH], zeta[:, h, d, t:t + 1],
                                            None, ALU.mult)
                o.then_inc(slot_read[1], 1)
                split_lo(u + 7, (u + 7) % RING)
                split_lo(u + 8, (u + 8) % RING)
                for j in range(LT):
                    dve.wait_ge(score_done, 7 * h + 2 + j)
                    if j == 0:
                        dve.wait_ge(decay_ready, h + 1)
                    at0 = sum(LT - a for a in range(j)) * P
                    at1 = sum(a + 1 for a in range(j)) * P
                    b = ps[:, 6 + j % 2, :]
                    v.tensor_tensor(scores[:, 0, at0:at0 + LAT - j * P], b[:, j * P:], decay[:, 0, 0:LAT - j * P], ALU.mult)
                    v.tensor_tensor(scores[:, 1, at1:at1 + (j + 1) * P], b[:, 0:(j + 1) * P],
                                    decay[:, 1, LAT - (j + 1) * P:], ALU.mult).then_inc(score_read, 1)
                dve.wait_ge(decay_exp, 2 * h + 2)
                dve.wait_ge(rot_step, 15 * h + 15)
                for d, dst in enumerate((q_dec, kT[:])):
                    v.tensor_tensor(dst, qT[:], decay[:, d, :].unsqueeze(1).to_broadcast([P, 2, LAT]), ALU.mult) \
                        .then_inc(qdec_ready, 1)
                for d in range(2):
                    n = 2 * h + d
                    if d == 0:
                        split_lo(u + 9, (u + 9) % RING)
                        split_lo(u + 10, (u + 10) % RING)
                    else:
                        split_lo(u + 11, (u + 11) % RING)
                        split_lo(u + 12, (u + 12) % RING)
                    dve.wait_ge(slot_read[0], (s + 4 + 2 * d) // 2 + 1)
                    dve.wait_ge(gn_in, 32 * (h + 1))
                    v.tensor_tensor(gate, gate, gn_row[:, d, :].unsqueeze(1).to_broadcast([P, LT, DH]), ALU.mult) \
                        .then_inc(gate_ready, 1)
                    dve.wait_ge(score_done, 7 * h + 6 + d)
                    if n:
                        dve.wait_ge(y_step, 3 * h + d)
                    for i in range(LT):
                        o_i = ps[:, 3 + i // 2, (i % 2) * DH:(i % 2 + 1) * DH]
                        o = v.bn_stats(gn_st[:, i, :], o_i)
                    o.then_inc(gn_stats, 1)
                    dve.wait_ge(gn_stats, 2 * n + 1)
                    for i in range(LT):
                        o = v.bn_aggr(gn_mv[:, i, :], gn_st[:, i, :])
                    o.then_inc(gn_stats, 1)
                    dve.wait_ge(gn_std, n + 1)
                    v.reciprocal(gn_mv[:, :, 1], gn_mv[:, :, 1]).then_inc(gn_rstd, 1)
                    dve.wait_ge(gn_rstd, n + 1)
                    dst = y_tok if d == 0 else q_dec.rearrange("p a b -> p (a b)").rearrange("p (t v) -> p t v", t=LT)
                    for i in range(LT):
                        o_i = ps[:, 3 + i // 2, (i % 2) * DH:(i % 2 + 1) * DH]
                        o = v.tensor_scalar(dst[:, i, :], o_i, gn_mv[:, i, 0:1], gn_mv[:, i, 1:2], ALU.subtract, ALU.mult)
                    o.then_inc(slot_read[1], 1)
                    dve.wait_ge(slot_read[1], (s + 5 + 2 * d) // 2 + 1)
                    dve.wait_ge(gate_ready, n + 1)
                    if d == 0:
                        v.tensor_tensor(y_tok, y_tok, gate, ALU.mult).then_inc(y_step, 1)
                    else:
                        v.tensor_tensor(dst, dst, gate, ALU.mult).then_inc(y_step, 1)
                        dve.wait_ge(y_step, 3 * h + 2)
                        v.tensor_tensor(y_tok, y_tok, dst, ALU.add).then_inc(y_step, 1)
            y_parts(HEADS - 1)
            out_phase_norm(RET_OUT, S_RET_OUT, X_RET_OUT, False, 4)
            ffn(FFN1, S_FFN1, 1, False, X_FFN1)
            for n in range(2, 8):
                if n == 4:
                    recip(5, 1)
                final_pair(n)


_INS = ["x", "c", "ctx", "c_ctx", "ada_w", "ada_b", "norm1_g", "norm2_g", "conv_pw1_w", "conv_pw1_b", "conv_dw_w",
        "conv_dw_b", "conv_ln_g", "conv_ln_b", "conv_pw2_w", "conv_pw2_b", "ret_w_in", "ret_w_out", "ret_decay_f",
        "ret_decay_b", "ret_gn_f", "ret_gn_b", "ffn_w_in", "ffn_dw_w", "ffn_dw_b", "ffn_w_out", "final_g"]


def shape_constants():
    import numpy as np
    f = np.float32
    p = np.arange(P)
    half = DH // 4
    freqs = (10000.0 ** (-np.arange(half, dtype=f) / f(half))).astype(f)
    sign = np.where(p < half, -1.0, 1.0)[:, None]

    def table(pos):
        ang = (pos[None, :].astype(f) * freqs[p % half][:, None]).astype(f).astype(np.float64)
        return np.stack([np.cos(ang), sign * np.sin(ang)], axis=1).astype(f)

    col = np.stack([p, p + LAT - P, CTX - 1 - p, CTX - 1 - P - p, p, p + P], axis=1).astype(f)
    return {
        "eye": np.eye(P, dtype=f),
        "ages": np.broadcast_to(np.arange(LAT, dtype=f), (P, LAT)).copy(),
        "tri_low": (p[None, :] <= p[:, None]).astype(f),
        "tri_up": (p[None, :] >= p[:, None]).astype(f),
        "rope_row": table(np.arange(ROWS)),
        "rope_col": table(np.arange(GRID_W)),
        "token_cols": col,
    }


def kernel(**inputs):
    import numpy as _np
    import concourse.bacc as _bacc
    from concourse import mybir as _mybir
    from concourse.bass_utils import run_bass_kernel_spmd as _run

    nc = _bacc.Bacc("TRN2", target_bir_lowering=False, num_devices=1)
    arrays, args = {}, []
    for name, a in [(n, _np.ascontiguousarray(inputs[n])) for n in _INS] + list(shape_constants().items()):
        arrays[f"in_{name}"] = a
        args.append(nc.dram_tensor(f"in_{name}", a.shape, _mybir.dt.from_np(a.dtype), kind="ExternalInput").ap())
    args.append(nc.dram_tensor("out", (1, LAT, D), _mybir.dt.float32, kind="ExternalOutput").ap())
    backbone(nc, *args)
    r = _run(nc, [arrays], core_ids=[0])
    return r.results[0]["out"]
```
